# Optimizing a Trainium2 kernel written in Bass

```python
import math
import jax, jax.numpy as jnp
from jax import lax
import numpy as np

D_MODEL = 1024
BATCH = 1
SEQ = 256
DEPTH = 2
DEC_BATCH = 8
DEC_SEQ = 4
PAST_LEN = 2048
PAGE_SIZE = 128

CONV_A_WIDTH = D_MODEL // 2
CONV_A_K = 3
ATT_HEADS = 8
ATT_HEAD_DIM = 64
ATT_WIDTH = ATT_HEADS * ATT_HEAD_DIM
MOBA_BLOCK = 256
MOBA_TOPK = 3
MOBA_QCHUNK = 16
IN0_WIDTH = 3 * CONV_A_WIDTH + 3 * ATT_WIDTH
MIX0_WIDTH = CONV_A_WIDTH + ATT_WIDTH

SSM_D_INNER = 2 * D_MODEL
SSM_HEAD_DIM = 64
SSM_HEADS = SSM_D_INNER // SSM_HEAD_DIM
SSM_GROUPS = 4
SSM_STATE = 128
SSM_CONV_K = 4
SSM_CHUNK = 128
SSM_CONV_DIM = SSM_D_INNER + 2 * SSM_GROUPS * SSM_STATE
SSM_IN_WIDTH = SSM_D_INNER + SSM_CONV_DIM + SSM_HEADS

FFN_HIDDEN = -(-8 * D_MODEL // (3 * 256)) * 256
NORM_EPS = 1e-6

kernel_name = 'hybrid_conv_moba_ssd_decoder_step'

def rmsnorm(x, w):
    xf = x.astype(jnp.float32)
    y = xf * lax.rsqrt(jnp.mean(xf * xf, axis=-1, keepdims=True) + NORM_EPS)
    return (y * w.astype(jnp.float32)).astype(x.dtype)

def ffn_sublayer(x, pre_w, w_gate, w_up, w_down, post_w):
    h = rmsnorm(x, pre_w)
    y = (jax.nn.silu(h @ w_gate) * (h @ w_up)) @ w_down
    return x + rmsnorm(y, post_w)

def causal_dwconv(u, hist, w):
    k_width = w.shape[0]
    t_len = u.shape[1]
    full = jnp.concatenate([hist.astype(u.dtype), u], axis=1)
    y = sum(w[j] * full[:, j:j + t_len] for j in range(k_width))
    return y, full[:, t_len:]

def moba_prompt(q, k, v):
    bn, s_len, n_h, dh = q.shape
    scale = dh ** -0.5
    nb = -(-s_len // MOBA_BLOCK)
    pad = nb * MOBA_BLOCK - s_len
    qh = q.transpose(0, 2, 1, 3)
    kh = jnp.pad(k.transpose(0, 2, 1, 3), ((0, 0), (0, 0), (0, pad), (0, 0)))
    vh = jnp.pad(v.transpose(0, 2, 1, 3), ((0, 0), (0, 0), (0, pad), (0, 0)))
    kb = kh.reshape(bn, n_h, nb, MOBA_BLOCK, dh)
    vb = vh.reshape(bn, n_h, nb, MOBA_BLOCK, dh)
    k_mean = jnp.mean(kb.astype(jnp.float32), axis=3)
    n_sel = min(MOBA_TOPK, nb - 1)
    bi = jnp.arange(bn)[:, None, None, None]
    hi = jnp.arange(n_h)[None, :, None, None]
    blk_ids = jnp.arange(nb)
    offs_q = jnp.arange(MOBA_QCHUNK)
    offs_k = jnp.arange(MOBA_BLOCK)

    def one_chunk(c):
        q0 = c * MOBA_QCHUNK
        own0 = (q0 // MOBA_BLOCK) * MOBA_BLOCK
        qc = lax.dynamic_slice_in_dim(qh, q0, MOBA_QCHUNK, axis=2)
        k_own = lax.dynamic_slice_in_dim(kh, own0, MOBA_BLOCK, axis=2)
        v_own = lax.dynamic_slice_in_dim(vh, own0, MOBA_BLOCK, axis=2)
        q_pos = q0 + offs_q
        k_pos = own0 + offs_k
        s_own = jnp.einsum('bhqd,bhkd->bhqk', qc, k_own, preferred_element_type=jnp.float32) * scale
        s_own = jnp.where(k_pos[None, :] <= q_pos[:, None], s_own, -jnp.inf)
        if n_sel == 0:
            p = jax.nn.softmax(s_own, axis=-1).astype(v.dtype)
            return jnp.einsum('bhqk,bhkd->bhqd', p, v_own)
        gate = jnp.einsum('bhqd,bhnd->bhqn', qc.astype(jnp.float32), k_mean)
        gate = jnp.where(blk_ids < q0 // MOBA_BLOCK, gate, -jnp.inf)
        g_top, sel = lax.top_k(gate, n_sel)
        k_sel = kb[bi, hi, sel].reshape(bn, n_h, MOBA_QCHUNK, n_sel * MOBA_BLOCK, dh)
        v_sel = vb[bi, hi, sel].reshape(bn, n_h, MOBA_QCHUNK, n_sel * MOBA_BLOCK, dh)
        s_sel = jnp.einsum('bhqd,bhqkd->bhqk', qc, k_sel, preferred_element_type=jnp.float32) * scale
        valid = jnp.repeat(jnp.isfinite(g_top), MOBA_BLOCK, axis=-1)
        s_sel = jnp.where(valid, s_sel, -jnp.inf)
        p = jax.nn.softmax(jnp.concatenate([s_own, s_sel], axis=-1), axis=-1).astype(v.dtype)
        return (jnp.einsum('bhqk,bhkd->bhqd', p[..., :MOBA_BLOCK], v_own)
                + jnp.einsum('bhqk,bhqkd->bhqd', p[..., MOBA_BLOCK:], v_sel))

    out = lax.map(one_chunk, jnp.arange(s_len // MOBA_QCHUNK))
    return out.transpose(1, 0, 3, 2, 4).reshape(bn, s_len, n_h * dh)

def moba_sample(q, k, v, cache_k, cache_v, page_table):
    bd, t_len, n_h, dh = q.shape
    scale = dh ** -0.5
    ppb = MOBA_BLOCK // PAGE_SIZE
    own0 = (PAST_LEN // MOBA_BLOCK) * MOBA_BLOCK
    n_cand = own0 // MOBA_BLOCK
    n_own_pages = (PAST_LEN - own0) // PAGE_SIZE
    qh = q.transpose(0, 2, 1, 3)
    kh = k.transpose(0, 2, 1, 3)
    vh = v.transpose(0, 2, 1, 3)
    own_pages = page_table[:, own0 // PAGE_SIZE: PAST_LEN // PAGE_SIZE]

    def own_rows(cache, new):
        rows = cache[own_pages].transpose(0, 2, 1, 3, 4).reshape(bd, n_h, n_own_pages * PAGE_SIZE, dh)
        return jnp.concatenate([rows.astype(new.dtype), new], axis=2)

    k_own = own_rows(cache_k, kh)
    v_own = own_rows(cache_v, vh)
    q_pos = PAST_LEN + jnp.arange(t_len)
    k_pos = own0 + jnp.arange(k_own.shape[2])
    s_own = jnp.einsum('bhqd,bhkd->bhqk', qh, k_own, preferred_element_type=jnp.float32) * scale
    s_own = jnp.where(k_pos[None, :] <= q_pos[:, None], s_own, -jnp.inf)
    if n_cand == 0:
        p = jax.nn.softmax(s_own, axis=-1).astype(v.dtype)
        out = jnp.einsum('bhqk,bhkd->bhqd', p, v_own)
        return out.transpose(0, 2, 1, 3).reshape(bd, t_len, n_h * dh)
    cand = cache_k[page_table[:, :n_cand * ppb]]
    k_mean = jnp.mean(cand.astype(jnp.float32).reshape(bd, n_cand, ppb, n_h, PAGE_SIZE, dh), axis=(2, 4))
    gate = jnp.einsum('bhqd,bnhd->bhqn', qh.astype(jnp.float32), k_mean)
    n_sel = min(MOBA_TOPK, n_cand)
    _, sel = lax.top_k(gate, n_sel)
    logical = sel[..., None] * ppb + jnp.arange(ppb)
    phys = page_table[jnp.arange(bd)[:, None, None, None, None], logical]
    hi = jnp.arange(n_h)[None, :, None, None, None]
    k_sel = cache_k[phys, hi].reshape(bd, n_h, t_len, n_sel * MOBA_BLOCK, dh).astype(kh.dtype)
    v_sel = cache_v[phys, hi].reshape(bd, n_h, t_len, n_sel * MOBA_BLOCK, dh).astype(vh.dtype)
    s_sel = jnp.einsum('bhqd,bhqkd->bhqk', qh, k_sel, preferred_element_type=jnp.float32) * scale
    n_own = k_own.shape[2]
    p = jax.nn.softmax(jnp.concatenate([s_own, s_sel], axis=-1), axis=-1).astype(v.dtype)
    out = (jnp.einsum('bhqk,bhkd->bhqd', p[..., :n_own], v_own)
           + jnp.einsum('bhqk,bhqkd->bhqd', p[..., n_own:], v_sel))
    return out.transpose(0, 2, 1, 3).reshape(bd, t_len, n_h * dh)

def even_mixer(h, conv_hist, w_in, conv_w, w_out, attend):
    bn, t_len, _ = h.shape
    split_at = [CONV_A_WIDTH, 2 * CONV_A_WIDTH, 3 * CONV_A_WIDTH,
                3 * CONV_A_WIDTH + ATT_WIDTH, 3 * CONV_A_WIDTH + 2 * ATT_WIDTH]
    gate_b, gate_c, u, q, k, v = jnp.split(h @ w_in, split_at, axis=-1)
    conv_out, new_hist = causal_dwconv(gate_c * u, conv_hist, conv_w)
    y_a = gate_b * conv_out
    heads = lambda t: t.reshape(bn, t_len, ATT_HEADS, ATT_HEAD_DIM)
    q, k, v = heads(q), heads(k), heads(v)
    y_b = attend(q, k, v)
    y = jnp.concatenate([y_a, y_b], axis=-1) @ w_out
    return y, new_hist, k, v

def ssd_scan(x, dt, a, b_in, c_in, init_state):
    bn, t_len, n_h, p_dim = x.shape
    n_g, n_s = b_in.shape[2], b_in.shape[3]
    r = n_h // n_g
    cl = SSM_CHUNK if t_len % SSM_CHUNK == 0 else t_len
    nc = t_len // cl
    f32 = jnp.float32
    xdt = (x.astype(f32) * dt[..., None]).reshape(bn, nc, cl, n_g, r, p_dim)
    a_cum = jnp.cumsum((dt * a).reshape(bn, nc, cl, n_g, r), axis=2)
    bc = b_in.astype(f32).reshape(bn, nc, cl, n_g, n_s)
    cc = c_in.astype(f32).reshape(bn, nc, cl, n_g, n_s)
    causal = jnp.tril(jnp.ones((cl, cl), bool))[None, None, :, :, None, None]
    seg = a_cum[:, :, :, None] - a_cum[:, :, None, :]
    decay = jnp.exp(jnp.where(causal, seg, -jnp.inf))
    cb = jnp.einsum('bclgn,bcsgn->bclsg', cc, bc)
    y_diag = jnp.einsum('bclsg,bclsgr,bcsgrp->bclgrp', cb, decay, xdt)
    decay_to_end = jnp.exp(a_cum[:, :, -1:] - a_cum)
    chunk_states = jnp.einsum('bclgn,bclgr,bclgrp->bcgrpn', bc, decay_to_end, xdt)
    chunk_decay = jnp.exp(a_cum[:, :, -1])

    def carry_step(s, inp):
        st, dec = inp
        return s * dec[..., None, None] + st, s

    s0 = init_state.astype(f32).reshape(bn, n_g, r, p_dim, n_s)
    s_final, s_enter = lax.scan(carry_step, s0,
                                (jnp.moveaxis(chunk_states, 1, 0), jnp.moveaxis(chunk_decay, 1, 0)))
    s_enter = jnp.moveaxis(s_enter, 0, 1)
    y_off = jnp.einsum('bclgn,bcgrpn,bclgr->bclgrp', cc, s_enter, jnp.exp(a_cum))
    y = (y_diag + y_off).reshape(bn, t_len, n_h, p_dim)
    return y, s_final.reshape(bn, n_h, p_dim, n_s).astype(init_state.dtype)

def mamba2_mixer(h, conv_hist, ssm_state, w_in, conv_w, conv_b, dt_bias, a_log, d_skip, norm_w, w_out):
    bn, t_len, _ = h.shape
    z, xbc, dt = jnp.split(h @ w_in, [SSM_D_INNER, SSM_D_INNER + SSM_CONV_DIM], axis=-1)
    xbc, new_conv_hist = causal_dwconv(xbc, conv_hist, conv_w)
    xbc = jax.nn.silu(xbc + conv_b)
    xs, b_in, c_in = jnp.split(xbc, [SSM_D_INNER, SSM_D_INNER + SSM_GROUPS * SSM_STATE], axis=-1)
    xs = xs.reshape(bn, t_len, SSM_HEADS, SSM_HEAD_DIM)
    b_in = b_in.reshape(bn, t_len, SSM_GROUPS, SSM_STATE)
    c_in = c_in.reshape(bn, t_len, SSM_GROUPS, SSM_STATE)
    dt = jax.nn.softplus(dt.astype(jnp.float32) + dt_bias.astype(jnp.float32))
    a = -jnp.exp(a_log.astype(jnp.float32))
    y, new_state = ssd_scan(xs, dt, a, b_in, c_in, ssm_state)
    y = y + d_skip.astype(jnp.float32)[:, None] * xs.astype(jnp.float32)
    y = y.astype(h.dtype).reshape(bn, t_len, SSM_D_INNER)
    y = rmsnorm(y * jax.nn.silu(z), norm_w)
    return y @ w_out, new_conv_hist, new_state

def setup_inputs(seed: int = 0) -> dict:
    key = jax.random.key(seed)
    keys = jax.random.split(key, 64)
    counter = [0]

    def nk():
        counter[0] += 1
        return keys[counter[0] - 1]

    f32 = jnp.float32
    dense = lambda fi, fo: jax.random.normal(nk(), (fi, fo), f32) * fi ** -0.5
    gain = lambda n: 1.0 + 0.05 * jax.random.normal(nk(), (n,), f32)
    n_pages = PAST_LEN // PAGE_SIZE
    n_pool = (5 * DEC_BATCH * n_pages + 3) // 4
    inp = {}
    inp['x_prompt'] = jax.random.normal(nk(), (BATCH, SEQ, D_MODEL), f32)
    inp['x_sample'] = jax.random.normal(nk(), (DEC_BATCH, DEC_SEQ, D_MODEL), f32)
    inp['cache_k'] = jax.random.normal(nk(), (n_pool, ATT_HEADS, PAGE_SIZE, ATT_HEAD_DIM), f32)
    inp['cache_v'] = jax.random.normal(nk(), (n_pool, ATT_HEADS, PAGE_SIZE, ATT_HEAD_DIM), f32)
    inp['page_table'] = jax.random.permutation(nk(), n_pool)[:DEC_BATCH * n_pages].reshape(DEC_BATCH, n_pages).astype(jnp.int32)
    inp['state_conv_a'] = jax.random.normal(nk(), (DEC_BATCH, CONV_A_K - 1, CONV_A_WIDTH), f32)
    inp['state_conv_ssm'] = jax.random.normal(nk(), (DEC_BATCH, SSM_CONV_K - 1, SSM_CONV_DIM), f32)
    inp['state_ssm'] = 0.1 * jax.random.normal(nk(), (DEC_BATCH, SSM_HEADS, SSM_HEAD_DIM, SSM_STATE), f32)
    inp['l0_norm_mix_pre'] = gain(D_MODEL)
    inp['l0_w_in'] = dense(D_MODEL, IN0_WIDTH)
    inp['l0_conv_w'] = jax.random.normal(nk(), (CONV_A_K, CONV_A_WIDTH), f32) * CONV_A_K ** -0.5
    inp['l0_w_out'] = dense(MIX0_WIDTH, D_MODEL)
    inp['l0_norm_mix_post'] = gain(D_MODEL)
    inp['l0_norm_ffn_pre'] = gain(D_MODEL)
    inp['l0_ffn_gate'] = dense(D_MODEL, FFN_HIDDEN)
    inp['l0_ffn_up'] = dense(D_MODEL, FFN_HIDDEN)
    inp['l0_ffn_down'] = dense(FFN_HIDDEN, D_MODEL)
    inp['l0_norm_ffn_post'] = gain(D_MODEL)
    inp['l1_norm_mix_pre'] = gain(D_MODEL)
    inp['l1_w_in'] = dense(D_MODEL, SSM_IN_WIDTH)
    inp['l1_conv_w'] = jax.random.normal(nk(), (SSM_CONV_K, SSM_CONV_DIM), f32) * SSM_CONV_K ** -0.5
    inp['l1_conv_b'] = 0.01 * jax.random.normal(nk(), (SSM_CONV_DIM,), f32)
    dt0 = jnp.exp(jax.random.uniform(nk(), (SSM_HEADS,), f32) * (math.log(0.1) - math.log(0.001)) + math.log(0.001))
    inp['l1_dt_bias'] = dt0 + jnp.log(-jnp.expm1(-dt0))
    inp['l1_a_log'] = jnp.log(jax.random.uniform(nk(), (SSM_HEADS,), f32, minval=1.0, maxval=16.0))
    inp['l1_d_skip'] = 1.0 + 0.1 * jax.random.normal(nk(), (SSM_HEADS,), f32)
    inp['l1_norm_gate'] = gain(SSM_D_INNER)
    inp['l1_w_out'] = dense(SSM_D_INNER, D_MODEL)
    inp['l1_norm_mix_post'] = gain(D_MODEL)
    inp['l1_norm_ffn_pre'] = gain(D_MODEL)
    inp['l1_ffn_gate'] = dense(D_MODEL, FFN_HIDDEN)
    inp['l1_ffn_up'] = dense(D_MODEL, FFN_HIDDEN)
    inp['l1_ffn_down'] = dense(FFN_HIDDEN, D_MODEL)
    inp['l1_norm_ffn_post'] = gain(D_MODEL)
    return inp

def reference(x_prompt, x_sample, cache_k, cache_v, page_table, state_conv_a, state_conv_ssm, state_ssm,
              l0_norm_mix_pre, l0_w_in, l0_conv_w, l0_w_out, l0_norm_mix_post,
              l0_norm_ffn_pre, l0_ffn_gate, l0_ffn_up, l0_ffn_down, l0_norm_ffn_post,
              l1_norm_mix_pre, l1_w_in, l1_conv_w, l1_conv_b, l1_dt_bias, l1_a_log, l1_d_skip,
              l1_norm_gate, l1_w_out, l1_norm_mix_post,
              l1_norm_ffn_pre, l1_ffn_gate, l1_ffn_up, l1_ffn_down, l1_norm_ffn_post):
    xp, xs = x_prompt, x_sample
    bp, s_len, _ = xp.shape
    attend_sample = lambda q, k, v: moba_sample(q, k, v, cache_k, cache_v, page_table)
    for layer in range(DEPTH):
        if layer % 2 == 0:
            hist0 = jnp.zeros((bp, CONV_A_K - 1, CONV_A_WIDTH), xp.dtype)
            yp, conv_a_prompt, kp, vp = even_mixer(rmsnorm(xp, l0_norm_mix_pre), hist0,
                                                   l0_w_in, l0_conv_w, l0_w_out, moba_prompt)
            ys, conv_a_sample, ks, vs = even_mixer(rmsnorm(xs, l0_norm_mix_pre), state_conv_a,
                                                   l0_w_in, l0_conv_w, l0_w_out, attend_sample)
            xp = xp + rmsnorm(yp, l0_norm_mix_post)
            xs = xs + rmsnorm(ys, l0_norm_mix_post)
            xp = ffn_sublayer(xp, l0_norm_ffn_pre, l0_ffn_gate, l0_ffn_up, l0_ffn_down, l0_norm_ffn_post)
            xs = ffn_sublayer(xs, l0_norm_ffn_pre, l0_ffn_gate, l0_ffn_up, l0_ffn_down, l0_norm_ffn_post)
            to_pages = lambda t: t.reshape(bp, s_len // PAGE_SIZE, PAGE_SIZE, ATT_HEADS, ATT_HEAD_DIM).transpose(0, 1, 3, 2, 4)
            k_prompt, v_prompt = to_pages(kp), to_pages(vp)
            k_sample, v_sample = ks.transpose(0, 2, 1, 3), vs.transpose(0, 2, 1, 3)
        else:
            conv0 = jnp.zeros((bp, SSM_CONV_K - 1, SSM_CONV_DIM), xp.dtype)
            ssm0 = jnp.zeros((bp, SSM_HEADS, SSM_HEAD_DIM, SSM_STATE), xp.dtype)
            yp, conv_ssm_prompt, ssm_prompt = mamba2_mixer(
                rmsnorm(xp, l1_norm_mix_pre), conv0, ssm0, l1_w_in, l1_conv_w, l1_conv_b,
                l1_dt_bias, l1_a_log, l1_d_skip, l1_norm_gate, l1_w_out)
            ys, conv_ssm_sample, ssm_sample = mamba2_mixer(
                rmsnorm(xs, l1_norm_mix_pre), state_conv_ssm, state_ssm, l1_w_in, l1_conv_w, l1_conv_b,
                l1_dt_bias, l1_a_log, l1_d_skip, l1_norm_gate, l1_w_out)
            xp = xp + rmsnorm(yp, l1_norm_mix_post)
            xs = xs + rmsnorm(ys, l1_norm_mix_post)
            xp = ffn_sublayer(xp, l1_norm_ffn_pre, l1_ffn_gate, l1_ffn_up, l1_ffn_down, l1_norm_ffn_post)
            xs = ffn_sublayer(xs, l1_norm_ffn_pre, l1_ffn_gate, l1_ffn_up, l1_ffn_down, l1_norm_ffn_post)
    return (xp, xs, k_prompt, v_prompt, k_sample, v_sample, conv_a_prompt, conv_a_sample,
            conv_ssm_prompt, conv_ssm_sample, ssm_prompt, ssm_sample)


_drawn_inputs = setup_inputs


def setup_inputs(seed=0):
    import zlib

    import numpy as np

    out = dict(_drawn_inputs(seed))
    spreads = {}
    factors = {'l1_conv_b': 3.292}
    for name, (base, spread) in spreads.items():
        noise = np.random.default_rng([zlib.crc32(name.encode()), seed]).standard_normal(out[name].shape)
        drawn = base * np.exp(spread * noise) if base else spread * noise
        out[name] = __import__('jax').numpy.asarray(drawn.astype(out[name].dtype))
    for name, factor in factors.items():
        out[name] = (out[name] * factor).astype(out[name].dtype)
    return out
```

```python
from contextlib import ExitStack

import concourse.bass as bass
from concourse import mybir

F32 = mybir.dt.float32
I32 = mybir.dt.int32
ACT = mybir.ActivationFunctionType
ALU = mybir.AluOpType
AX = mybir.AxisListType
ds = bass.ds

P = 128
NEG = -1.0e30


def hybrid_decoder_kernel(
    nc, x_prompt, x_sample, cache_k, cache_v, page_table, state_conv_a, state_conv_ssm, state_ssm,
    l0_norm_mix_pre, l0_w_in, l0_conv_w, l0_w_out, l0_norm_mix_post,
    l0_norm_ffn_pre, l0_ffn_gate, l0_ffn_up, l0_ffn_down, l0_norm_ffn_post,
    l1_norm_mix_pre, l1_w_in, l1_conv_w, l1_conv_b, l1_dt_bias, l1_a_log, l1_d_skip,
    l1_norm_gate, l1_w_out, l1_norm_mix_post,
    l1_norm_ffn_pre, l1_ffn_gate, l1_ffn_up, l1_ffn_down, l1_norm_ffn_post,
    y_prompt, y_sample, k_prompt, v_prompt, k_sample, v_sample,
    conv_a_prompt, conv_a_sample, conv_ssm_prompt, conv_ssm_sample, ssm_prompt, ssm_sample,
):
    _, NP, D = x_prompt.shape
    NB, T, _ = x_sample.shape
    NS = NB * T
    NT = NP + NS
    KD = D // P
    NPOOL, H, PAGE, DH = cache_k.shape
    NPAGES = page_table.shape[1]
    BLOCK = 2 * PAGE
    NBLK = NPAGES * PAGE // BLOCK
    TOPK = 3
    SCALE = float(DH) ** -0.5
    CA = state_conv_a.shape[2] // P
    M_IN0 = l0_w_in.shape[1] // P
    MQ, MK, MV = 3 * CA, 3 * CA + H * DH // P, 3 * CA + 2 * H * DH // P
    FM = l0_ffn_gate.shape[1] // P
    SH = l1_a_log.shape[0]
    DI = l1_w_out.shape[0]
    CX = DI // P
    NST = state_ssm.shape[3]
    CC = state_conv_ssm.shape[2] // P
    G = (CC - CX) // 2
    HG = SH // G
    PG = HG // 2
    HB = NB // 2
    HC = HB * H * T
    QT = H * T
    assert HC == P and PAGE == P and 2 * DH == P and NST == P and BLOCK == 2 * P

    UC = 2 * P
    R = 5

    def column_units(w, first, count):
        v = w.rearrange("(k p) n -> p k n", p=P)
        return [(v[:, k:min(k + KD, v.shape[1]), c:c + UC], min(KD, v.shape[1] - k))
                for c in range(first, first + count * UC, UC) for k in range(0, v.shape[1], KD)]

    in0_units = column_units(l0_w_in, MQ * P, (M_IN0 - MQ) // 2) + column_units(l0_w_in, 0, MQ // 2)

    def gate_up(g, u):
        return [x for pair in zip(column_units(g, 0, FM // 2), column_units(u, 0, FM // 2)) for x in pair]

    units_a = in0_units
    units_b = (column_units(l0_w_out, 0, KD // 2) + gate_up(l0_ffn_gate, l0_ffn_up)
               + column_units(l0_ffn_down, 0, KD // 2)
               + column_units(l1_w_in, DI, CC // 2) + column_units(l1_w_in, 0, CX // 2))
    state_units = [(state_ssm[b].rearrange("(k q) p n -> (q p) k n", q=2), CX) for b in range(NB)]
    units_c = (column_units(l1_w_out, 0, KD // 2) + gate_up(l1_ffn_gate, l1_ffn_up)
               + column_units(l1_ffn_down, 0, KD // 2))
    units = units_a + units_b + state_units + units_c
    FIRST_STATE = len(units_a) + len(units_b)

    KVS = 8

    with ExitStack() as ctx:
        def sb(name, shape, dt=F32):
            return ctx.enter_context(nc.sbuf_tensor(name, shape, dt))

        def sem(name):
            return ctx.enter_context(nc.semaphore(name))

        class Area:

            def __init__(self, tensor, at=0):
                self.tensor, self.at = tensor, at

            def take(self, *dims):
                n = 1
                for d in dims:
                    n *= d
                v = self.tensor[:, self.at:self.at + n]
                self.at += n
                assert self.at <= self.tensor.shape[1], self.at
                if len(dims) > 1:
                    names = "abcd"[:len(dims)]
                    v = v.rearrange(f"p ({' '.join(names)}) -> p {' '.join(names)}",
                                    **{m: d for m, d in zip(names[1:], dims[1:])})
                return v

        X = sb("X", [P, KD, NT])
        HX = sb("HX", [P, KD, NT])
        Y = sb("Y", [P, KD, NT])
        BIG = sb("BIG", [P, CC, NT])
        ring = sb("ring", [P, R, KD * UC])
        SQ = sb("SQ", [P, 4, NT])
        arena = sb("arena", [P, 19656])
        MIX = HX

        def flat(t):
            return t[:, :, :].rearrange("p k n -> p (k n)")

        a = Area(arena)
        kv = a.take(KVS, H, 2, DH)
        S = a.take(2, 2 * NBLK, HC)
        QB = a.take(H, NB, 2 * T)
        KOUT = a.take(3, H * DH)
        VTOK = a.take(3, H * DH)
        PT = a.take(2, 3 * P)
        KTB = a.take(2, 4 * P)
        POWN = a.take(2 * HC)
        CUP = a.take(CA, NP + 2)
        CUS = a.take(CA, NB, T + 2)
        coT_a = a.take(CA * P)
        SP = Area(flat(SQ)).take(2, 3 * P)
        DIAG = Area(flat(Y)).take(NBLK, P)
        OSB = Area(flat(Y), NBLK * P).take(2, H * DH)
        XIN = Area(arena).take(3, D)
        PARIN = Area(arena, 3 * D).take(2, P)
        HISTA_IN = Area(arena, 3 * D + 2 * P).take(CA * P)
        HISTS_IN = Area(arena, 3 * D + 2 * P + CA * P).take(CC * P)
        HID = Area(arena).take(FM, NT)
        GS = Area(arena, FM * NT).take(2, NT)
        US = Area(arena, (FM + 2) * NT).take(2, NT)
        YT = Area(arena).take(3, D)
        a = Area(arena)
        ZS = a.take(CX, NT)
        SEG = a.take(HG, NT)
        XW0 = a.take(HG * DH)
        SENT = a.take(HG * DH)
        STP = a.take(PG, NST)
        BT = a.take(3, G * NST)
        CBM = a.take(G, NT)
        S0T = a.take(2, 4 * P)
        XDT = Area(flat(HX)).take(2, 2, HG * DH)
        XW1 = Area(flat(Y)).take(2, 2, HG * DH)
        Q1 = slice(NS, 2 * NS)
        q = Area(arena, a.at)
        XDS = q.take(DI)
        E2 = q.take(CX, P)
        hwa = q.take(6, NT)
        hw = hwa[0:SH, :, :]
        q = Area(arena, a.at)
        XWS = q.take(DI)
        BMASK = q.take(G, NB, NST)
        CO1T = Area(arena, a.at).take(CC * P)
        CQ = 2 * NS

        ident = sb("ident", [P, P])
        ones = sb("ones", [P, P])
        tri3 = sb("tri3", [P, 3, P])
        trilT = sb("trilT", [P, P])
        bd01 = sb("bd01", [NS, NS])
        own_bias = sb("own_bias", [NS, 2 * HC])
        bmask01 = sb("bmask01", [NS, NB])
        tie = sb("tie", [P, NBLK, NBLK])
        sel = sb("sel", [P, QT])
        eps = sb("eps", [P, 1])
        par = sb("par", [P, 2, P])
        hists = sb("hists", [P, CC, NB * 3])
        RT = sb("RT", [P, NT])
        RR = sb("RR", [P, NT])
        pages = sb("pages", [1, NB * NPAGES], I32)
        small = sb("small", [P, 384])
        RD = sb("RD", [P, 2, HC])
        RM = sb("RM", [P, 2, HC])
        co_a = sb("co_a", [P, CA, 2 + 2 * NB])
        ext = sb("ext", [P, 2, NP + 3])
        exts = sb("exts", [P, 2, NB, T + 3])
        co_s = sb("co_s", [P, CC, 3 + 3 * NB])
        wdt = sb("wdt", [P, KD, SH])
        hp3 = sb("hp3", [SH, 3])
        hs = sb("hs", [P, NT])
        tc = sb("tc", [P, 3, P])
        dec = sb("dec", [P, CX, NB + 1])
        decin = sb("decin", [SH, NB + 1])
        YOS = sb("YOS", [P, CX, NB, T])
        EBT = sb("EBT", [P, 2, NT - P])
        YTMP = sb("YTMP", [P, 2, NT])
        XCH = sb("XCH", [P, 2, NT - P])

        acc = [ctx.enter_context(nc.psum_tensor(f"acc{i}", [P, 512], F32)) for i in range(4)]
        trb = [ctx.enter_context(nc.psum_tensor(f"trb{i}", [P, 512], F32)) for i in range(2)]
        scb = [ctx.enter_context(nc.psum_tensor(f"scb{i}", [P, 512], F32)) for i in range(2)]
        stat = scb[0]

        PN = {n: i * KD for i, n in enumerate(
            ["mix_pre0", "mix_post0", "ffn_pre0", "ffn_post0", "mix_pre1", "mix_post1", "ffn_pre1", "ffn_post1"])}
        PGATE, PCA, PCB = 8 * KD, 8 * KD + CX, 8 * KD + CX + 3 * CA
        N_PAR0 = PCB + CC

        consts = sem("consts")
        zeroed = sem("zeroed")
        ld_x, ld_par, ld_hist, ld_head, ld_pages = (sem(n) for n in ("ld_x", "ld_par", "ld_hist", "ld_head", "ld_pages"))
        w_in = [sem(f"w_in{i}") for i in range(R)]
        w_used = sem("w_used")
        kv_in = [sem(f"kv_in{i}") for i in range(KVS)]
        kv_credit = sem("kv_credit")
        tr_full = sem("tr_full")
        tr_act = sem("tr_act")
        tr_dve = sem("tr_dve")
        acc_full = sem("acc_full")
        acc_free = sem("acc_free")
        sq_made = sem("sq_made")
        sq_used = sem("sq_used")
        rt_made = sem("rt_made")
        r_made = sem("r_made")
        hx_made = sem("hx_made")
        x_made = sem("x_made")
        qb_made = sem("qb_made")
        kt_used = sem("kt_used")
        s0_used = sem("s0_used")
        s_free = sem("s_free")
        d_step = [sem(f"d_step{i}") for i in range(2)]
        p_made = sem("p_made")
        o_full = sem("o_full")
        o_copied = sem("o_copied")
        o_used = sem("o_used")
        pp_ready = sem("pp_ready")
        pp_exp = sem("pp_exp")
        pp_made = sem("pp_made")
        pt_used = sem("pt_used")
        mix_made = sem("mix_made")
        hid_silu = sem("hid_silu")
        hid_made = sem("hid_made")
        zs_made = sem("zs_made")
        cv_made = sem("cv_made")
        xc_made = sem("xc_made")
        co_made = sem("co_made")
        dt_step = sem("dt_step")
        dt_act = sem("dt_act")
        hs_made = sem("hs_made")
        bt_made = sem("bt_made")
        g_made = sem("g_made")
        sent_made = sem("sent_made")
        stp_made = sem("stp_made")
        stp_out = sem("stp_out")
        seg_in = sem("seg_in")
        seg_exp = sem("seg_exp")
        seg_made = sem("seg_made")
        gy_made = sem("gy_made")
        st_made = sem("st_made")
        st_out = [sem(f"st_out{i}") for i in range(R)]
        vch = sem("vch")
        ach = sem("ach")
        stored = sem("stored")

        block = ctx.enter_context(nc.Block())

        TR_X = 0
        TR_PAR = TR_X + KD
        TR_HIST = TR_PAR + 2
        TR_KV = TR_HIST + 4
        TR_K = TR_KV + 6
        N_K = NB * NBLK * 2
        TR_PA = TR_K + N_K
        TR_COA = TR_PA + H
        TR_ST = TR_COA + 2
        TR_CO = TR_ST + NB * 4
        TR_Y = TR_CO + CC // 4

        ACC_MIX = M_IN0
        ACC_OUT0 = ACC_MIX + 2 + 2 * (1 + 2 + 1 + 1 + 1) + 2 * H + NB
        ACC_GU0 = ACC_OUT0 + KD
        ACC_DOWN0 = ACC_GU0 + 2 * FM
        ACC_IN1 = ACC_DOWN0 + KD
        ACC_DT = ACC_IN1 + CC
        ACC_Z = ACC_DT + 1
        ACC_SSD = ACC_Z + CX
        ACC_OUT1 = ACC_SSD + 1 + 3 + G + 1 + G + NB * (1 + G) + G * (2 + 1 + 1 + HG + 3 * PG)
        ACC_GU1 = ACC_OUT1 + KD
        ACC_DOWN1 = ACC_GU1 + 2 * FM
        freed, used = [], 0
        for first, tiles, kparts in ((0, M_IN0, 1), (ACC_OUT0, KD, 1), (ACC_GU0, 2 * FM, 1), (ACC_DOWN0, KD, -(-FM // KD)),
                                     (ACC_IN1, CC, 1), (ACC_Z, CX, 1), (None, NB, 1),
                                     (ACC_OUT1, KD, CX // KD), (ACC_GU1, 2 * FM, 1), (ACC_DOWN1, KD, -(-FM // KD))):
            if first is None:
                freed += [(st_out[(FIRST_STATE + b) % R], 16 * (b // R + 1)) for b in range(NB)]
                continue
            for pair in range(tiles // 2):
                for part in range(kparts - 1):
                    used += 1
                    freed.append((w_used, used))
                freed.append((acc_full, first + 2 * pair + 2))
        assert len(freed) == len(units)
        marks = {}

        @block.sync
        def _(sp):
            def load_units(lo, hi):
                for u in range(lo, hi):
                    src, kb = units[u]
                    if u >= R:
                        sp.wait_ge(*freed[u - R])
                    dst = ring[:, u % R, :].rearrange("p (k n) -> p k n", n=src.shape[2])[:, 0:kb, :]
                    sp.dma_start(dst, src).then_inc(w_in[u % R], 16)

            def load_blocks(cache):
                with sp.Fori(0, NB) as i:
                    for s in range(KVS):
                        sp.wait_ge(kv_credit, i * KVS + (s + 1) + (0 if cache is cache_k else NB * NBLK))
                        for half in range(2):
                            page = sp.value_load(pages[0:1, ds(i * NPAGES + 2 * s + half, 1)], min_val=0, max_val=NPOOL - 1)
                            sp.dma_start(
                                kv[half * DH:(half + 1) * DH, s, :, :, :],
                                cache[ds(page, 1), :, :, :].rearrange("o h (q j) d -> q (o h) j d", j=2),
                            ).then_inc(kv_in[s], 16)

            sp.dma_start(pages[:, :], page_table.rearrange("b n -> (b n)").unsqueeze(0)).then_inc(ld_pages, 16)
            load_units(0, R)
            sp.wait_ge(ld_pages, 16)
            load_units(R, len(units_a))
            load_blocks(cache_k)
            load_blocks(cache_v)
            load_units(len(units_a), len(units))

        @block.gpsimd
        def _(pool):
            n = [0]

            def step(ins):
                n[0] += 1
                ins.then_inc(consts, 1)
                pool.wait_ge(consts, n[0])

            step(pool.memset(ident[:, :], 0.0))
            step(pool.affine_select(out=ident[:, :], in_=ident[:, :], compare_op=ALU.not_equal, fill=1.0,
                                    base=0, pattern=[[-1, P]], channel_multiplier=1))
            step(pool.memset(ones[:, :], 1.0))
            step(pool.memset(eps[:, :], 1e-6))
            step(pool.memset(tri3[:, :, :], 0.0))
            for i in (0, 2):
                step(pool.affine_select(out=tri3[:, i, :], in_=tri3[:, i, :], compare_op=ALU.is_ge, fill=NEG,
                                        base=0, pattern=[[-1, P]], channel_multiplier=1))
            step(pool.memset(trilT[:, :], 1.0))
            step(pool.affine_select(out=trilT[:, :], in_=trilT[:, :], compare_op=ALU.is_ge, fill=0.0,
                                    base=0, pattern=[[1, P]], channel_multiplier=-1))

            def own_columns(t, fill, mid):
                step(pool.affine_select(out=t, in_=t, compare_op=ALU.is_ge, fill=fill,
                                        base=0, pattern=[[-T, NB]] + mid + [[0, T]], channel_multiplier=1))
                step(pool.affine_select(out=t, in_=t, compare_op=ALU.is_ge, fill=fill,
                                        base=0, pattern=[[T, NB]] + mid + [[1, T]], channel_multiplier=-1))

            step(pool.memset(bd01[:, :], 1.0))
            own_columns(bd01[:, :].rearrange("p (b t) -> p b t", t=T), 0.0, [])
            step(pool.memset(own_bias[:, :], 0.0))
            own_columns(own_bias[:, :].rearrange("p (b h t) -> p b h t", h=H, t=T), NEG, [[0, H]])
            step(pool.memset(bmask01[:, :], 1.0))
            step(pool.affine_select(out=bmask01[:, :], in_=bmask01[:, :], compare_op=ALU.is_ge, fill=0.0,
                                    base=0, pattern=[[-T, NB]], channel_multiplier=1))
            step(pool.affine_select(out=bmask01[:, :], in_=bmask01[:, :], compare_op=ALU.is_ge, fill=0.0,
                                    base=T - 1, pattern=[[T, NB]], channel_multiplier=-1))
            step(pool.memset(tie[:, :, :], 1.0))
            step(pool.affine_select(out=tie[:, :, :], in_=tie[:, :, :], compare_op=ALU.is_gt, fill=0.0,
                                    base=0, pattern=[[1, NBLK], [-1, NBLK]], channel_multiplier=0))
            step(pool.memset(sel[:, :], 0.0))
            for g in range(4):
                step(pool.affine_select(out=sel[:, :], in_=sel[:, :], compare_op=ALU.not_equal, fill=1.0,
                                        base=-QT * g, pattern=[[-1, QT]], channel_multiplier=1))
            pool.memset(QB[:, :, :, :], 0.0)
            pool.memset(VTOK[:, :, :], 0.0)
            pool.memset(POWN[:, :], 0.0)
            pool.memset(CUP[:, :, 0:2], 0.0)
            pool.memset(ext[:, :, 0:3], 0.0).then_inc(zeroed, 1)

            stores = [0]

            def store(dst, src, s=stored):
                pool.dma_start(dst, src).then_inc(s, 16)
                if s is stored:
                    stores[0] += 1

            pool.wait_ge(tr_act, TR_K // 2)
            pool.wait_ge(tr_dve, TR_K // 2)
            for buf, prompt, sample in ((KOUT, k_prompt, k_sample), (VTOK, v_prompt, v_sample)):
                for t in range(NP // PAGE):
                    store(prompt[0, t].rearrange("h q d -> q h d"),
                          buf[:, t, :].rearrange("p (h d) -> p h d", d=DH))
                for b in range(NB):
                    store(sample[b].rearrange("h t d -> t h d"),
                          buf[b * T:(b + 1) * T, 2, :].rearrange("p (h d) -> p h d", d=DH))
            pool.wait_ge(tr_act, (TR_COA + 2) // 2)
            pool.wait_ge(tr_dve, (TR_COA + 2) // 2)
            store(conv_a_prompt[0], coT_a[0:2, :])
            store(conv_a_sample.rearrange("b j c -> (b j) c"), coT_a[2:2 + 2 * NB, :])

            pool.wait_ge(mix_made, 2)
            pool.wait_ge(acc_full, ACC_IN1)
            pool.wait_ge(stored, 16 * stores[0])
            step(pool.memset(E2[0:SH, :, :], 0.0))
            step(pool.affine_select(out=E2[0:SH, :, :].rearrange("p k (q r) -> p k q r", q=2),
                                    in_=E2[0:SH, :, :].rearrange("p k (q r) -> p k q r", q=2),
                                    compare_op=ALU.not_equal, fill=1.0, base=0,
                                    pattern=[[-2, CX], [-1, 2], [0, DH]], channel_multiplier=1))
            marks["e2"] = n[0]
            step(pool.memset(CBM[:, :, :], 0.0))
            step(pool.memset(SEG[:, :, :], 0.0))
            marks["seg"] = n[0]
            for b in range(NB):
                pool.wait_ge(st_made, b + 1)
                u = FIRST_STATE + b
                store(ssm_sample[b].rearrange("(k q) p n -> (q p) k n", q=2),
                      ring[:, u % R, :].rearrange("p (k n) -> p k n", n=NST), st_out[u % R])
            pool.wait_ge(tr_act, (TR_Y) // 2)
            pool.wait_ge(tr_dve, (TR_Y) // 2)
            store(conv_ssm_prompt[0], CO1T[CQ:CQ + 3, :])
            store(conv_ssm_sample.rearrange("b j c -> (b j) c"), CO1T[CQ + 3:CQ + 3 + 3 * NB, :])
            for g in range(G):
                pool.wait_ge(stp_made, g + 1)
                store(ssm_prompt[0, g * HG:(g + 1) * HG].rearrange("(k q) p n -> (q p) k n", q=2), STP, stp_out)
            pool.wait_ge(tr_act, (TR_Y + 6) // 2)
            pool.wait_ge(tr_dve, (TR_Y + 6) // 2)
            for t in range(2):
                store(y_prompt[0, t * P:(t + 1) * P, :], YT[:, t, :])
            store(y_sample.rearrange("b t d -> (b t) d"), YT[0:NS, 2, :])
            pool.wait_ge(stored, 16 * stores[0])
            for b in range(NB):
                pool.wait_ge(st_out[(FIRST_STATE + b) % R], 16 * (b // R + 1))
            pool.wait_ge(stp_out, 16 * G)

        @block.tensor
        def _(pe):
            n_acc = [0]
            n_sq = [0]
            n_norm = [0]
            n_used = [0]

            def acc_open():
                n = n_acc[0]
                n_acc[0] += 1
                if n >= 4:
                    pe.wait_ge(acc_free, n - 3)
                return acc[n % 4]

            def tr_open(n):
                if n >= 2:
                    pe.wait_ge(tr_act if n % 2 == 0 else tr_dve, n // 2)
                return trb[n % 2]

            def weights(u):
                pe.wait_ge(w_in[u % R], 16 * (u // R + 1))
                return ring[:, u % R, :]

            def sum_square(last_of):
                count, total = last_of
                if count == 0 and n_norm[0] >= 1:
                    pe.wait_ge(rt_made, n_norm[0])
                pe.wait_ge(sq_made, n_sq[0] + 1)
                pe.matmul(stat[:, 0:NT], ones[:, :], SQ[:, n_sq[0] % 4, :],
                          start=(count == 0), stop=(count == total - 1)).then_inc(sq_used, 1)
                n_sq[0] += 1
                if count == total - 1:
                    n_norm[0] += 1

            def project(u, tiles, kdim, rhs, ready, first_pair_only=True, after=None):
                kparts = -(-kdim // KD)
                for pair in range(tiles // 2):
                    banks = [acc_open(), acc_open()]
                    for part in range(kparts):
                        w = weights(u)
                        ks = range(part * KD, min(part * KD + KD, kdim))
                        for i in range(2):
                            for k in ks:
                                if pair == 0 and i == 0:
                                    ready(k)
                                at = (k - part * KD) * UC + i * P
                                last = pe.matmul(banks[i][:, 0:NT], w[:, at:at + P], rhs[:, k, :],
                                                 start=(k == 0), stop=(k == kdim - 1))
                            if part == kparts - 1:
                                last.then_inc(acc_full, 1)
                        if part < kparts - 1:
                            last.then_inc(w_used, 1)
                        u += 1
                    if after:
                        after(pair)
                return u

            def hx_ready(base):
                return lambda k: pe.wait_ge(hx_made, base + k + 1)

            def out_project(u, kdim, rhs, ready):
                done = [0]

                def squares(pair):
                    for _ in range(0 if pair == 0 else 2):
                        sum_square((done[0], KD))
                        done[0] += 1

                u = project(u, KD, kdim, rhs, ready, after=squares)
                while done[0] < KD:
                    squares(1)
                return u

            pe.sem_inc(kt_used, 2)
            pe.wait_ge(consts, 2)
            pe.wait_ge(ld_x, 32)
            for k in range(KD):
                bank = tr_open(TR_X + k)
                for t in range(3):
                    rows = P if t < 2 else NS
                    last = pe.transpose(bank[:, t * P:t * P + rows], XIN[0:rows, t, k * P:(k + 1) * P], ident[0:rows, 0:rows])
                last.then_inc(tr_full, 1)
            pe.wait_ge(ld_par, 16 * 12)
            for i, rows in enumerate((N_PAR0, 4 * CC)):
                pe.transpose(tr_open(TR_PAR + i)[:, 0:rows], PARIN[0:rows, i, :], ident[0:rows, 0:rows]).then_inc(tr_full, 1)
            pe.wait_ge(ld_hist, 32)
            bank = tr_open(TR_HIST)
            for c in range(CA):
                last = pe.transpose(bank[:, c * 2 * NB:(c + 1) * 2 * NB], HISTA_IN[0:2 * NB, c * P:(c + 1) * P], ident[0:2 * NB, 0:2 * NB])
            last.then_inc(tr_full, 1)
            for i in range(3):
                bank = tr_open(TR_HIST + 1 + i)
                for c in range(CC // 3):
                    cc = i * (CC // 3) + c
                    last = pe.transpose(bank[:, c * 3 * NB:(c + 1) * 3 * NB], HISTS_IN[0:3 * NB, cc * P:(cc + 1) * P], ident[0:3 * NB, 0:3 * NB])
                last.then_inc(tr_full, 1)

            pe.wait_ge(consts, 3)
            for k in range(KD):
                sum_square((k, KD))
            u = project(0, M_IN0, KD, HX, hx_ready(0))
            pe.wait_ge(tr_full, TR_KV)
            pe.sem_inc(kv_credit, KVS)

            pe.wait_ge(acc_free, M_IN0)
            for h in list(range(0, H, 2)) + list(range(1, H, 2)):
                if h < 2:
                    bank = acc_open()
                rows = slice((h % 2) * DH, (h % 2 + 1) * DH)
                last = pe.matmul(bank[0:NS, 0:2 * HC].rearrange("p (b h t) -> p b h t", h=H, t=T)[:, :, h, :],
                                 BIG[rows, MK + h // 2, NP:NT],
                                 BIG[rows, MQ + h // 2, NP:NT].rearrange("p (b t) -> p b t", t=T), start=True, stop=True)
                if h >= H - 2:
                    last.then_inc(acc_full, 1)

            for i, m in enumerate((MK, MV)):
                for t in range(3):
                    rows = P if t < 2 else NS
                    bank = tr_open(TR_KV + 3 * i + t)
                    for c in range(H * DH // P):
                        last = pe.transpose(bank[0:rows, c * P:(c + 1) * P], BIG[:, m + c, t * P:t * P + rows], ident[:, :])
                    last.then_inc(tr_full, 1)

            def k_phase(half):
                with pe.Fori(0, HB // 2) as i:
                    prev = None
                    base = TR_K + half * HB * NBLK * 2

                    def scores(s, q):
                        e, blk = s // NBLK, s % NBLK
                        if blk == 0 and q == 0:
                            pe.wait_ge(s_free, i * 2 + (half * HB + e + 1))
                        pe.wait_ge(tr_dve if q else tr_act, i * 2 * KVS + (base // 2 + s + 1))
                        for hh in range(4):
                            h = 4 * q + hh
                            last = pe.matmul(scb[e][:, (blk * H + h) * 2 * T:(blk * H + h + 1) * 2 * T],
                                             KTB[:, q, hh * P:(hh + 1) * P],
                                             QB[:, h, ds(i * 2 + (half * HB + e), 1), :].rearrange("p o c -> p (o c)"),
                                             start=True, stop=True)
                            if q == 1 and hh == 0:
                                last.then_inc(kv_credit, 1)
                        last.then_inc(kt_used, 1)

                    for s in range(2 * KVS):
                        pe.wait_ge(kv_in[s % KVS], i * 64 + 32 * (half * HB + s // KVS + 1))
                        for q in range(2):
                            pe.wait_ge(tr_dve if q else tr_act, i * 2 * KVS + (base // 2 + s))
                            for hh in range(4):
                                last = pe.transpose(trb[q][:, hh * P:(hh + 1) * P],
                                                    kv[:, s % KVS, 4 * q + hh, :, :].rearrange("p j d -> p (j d)"), ident[:, :])
                            last.then_inc(tr_full, 1)
                            if prev:
                                scores(*prev)
                            prev = (s, q)
                    scores(*prev)

            def gate(half):
                pe.wait_ge(s_free, 2 + (half + 1) * HB)
                bank = acc_open()
                for blk in range(NBLK):
                    for j in range(2):
                        last = pe.matmul(bank[:, blk:blk + 1], S[:, half, 2 * blk + j, :], ones[:, 0:1],
                                         start=(j == 0), stop=(j == 1))
                last.then_inc(acc_full, 1)

            def on_all(src, wait):
                wait()
                bank = acc_open()
                width = src.free_size()
                pe.matmul(bank[:, 0:width], ones[:, :], src, start=True, stop=True).then_inc(acc_full, 1)

            def block_bias(half):
                for i in range(2):
                    on_all(DIAG[:, 4 * i:4 * i + 4, :], lambda: pe.wait_ge(d_step[half], 1))

            def turn_max(half):
                pe.wait_ge(d_step[half], 2)
                pe.transpose(acc_open()[:, 0:P], RM[:, half, :], ident[:, :]).then_inc(acc_full, 1)

            def spread_max(half):
                on_all(DIAG[:, 0, :], lambda: pe.wait_ge(d_step[half], 3))
                marks["spread", half] = n_acc[0]

            def prompt_scores(h):
                rows = slice((h % 2) * DH, (h % 2 + 1) * DH)
                q, k = BIG[rows, MQ + h // 2, :], BIG[rows, MK + h // 2, :]
                bank = acc_open()
                pe.matmul(bank[:, 0:P], q[:, 0:P], k[:, 0:P], start=True, stop=True)
                pe.matmul(bank[:, P:3 * P], q[:, P:2 * P], k[:, 0:2 * P], start=True, stop=True).then_inc(acc_full, 1)

            def prompt_turn(h):
                pe.wait_ge(pp_made, h + 1)
                bank = tr_open(TR_PA + h)
                for i in range(3):
                    last = pe.transpose(bank[:, i * P:(i + 1) * P], SP[:, h % 2, i * P:(i + 1) * P], ident[:, :])
                last.then_inc(tr_full, 1)

            def prompt_values(h):
                n = TR_PA + h
                pe.wait_ge(tr_act if n % 2 == 0 else tr_dve, n // 2 + 1)
                rows = slice((h % 2) * DH, (h % 2 + 1) * DH)
                cols = slice(h * DH, (h + 1) * DH)
                bank = acc_open()
                marks["pv", h] = n_acc[0]
                pe.matmul(bank[rows, 0:P], VTOK[:, 0, cols], PT[:, h % 2, 0:P], start=True, stop=True)
                pe.matmul(bank[rows, P:2 * P], VTOK[:, 0, cols], PT[:, h % 2, P:2 * P], start=True, stop=False)
                pe.matmul(bank[rows, P:2 * P], VTOK[:, 1, cols], PT[:, h % 2, 2 * P:3 * P], start=False,
                          stop=True).then_inc(acc_full, 1)

            def prompt_step(i):
                if i < H:
                    prompt_scores(i)
                if 1 <= i <= H:
                    prompt_turn(i - 1)
                if 2 <= i:
                    prompt_values(i - 2)

            pe.wait_ge(rt_made, 1)
            pe.wait_ge(qb_made, 1)
            k_phase(0)
            gate(0)
            k_phase(1)
            gate(1)
            block_bias(0)
            prompt_step(0)
            prompt_step(1)
            turn_max(0)
            prompt_step(2)
            prompt_step(3)
            spread_max(0)
            prompt_step(4)
            prompt_step(5)
            block_bias(1)
            prompt_step(6)
            prompt_step(7)
            turn_max(1)
            prompt_step(8)
            prompt_step(9)
            spread_max(1)

            def values(b):
                half, bb = b // HB, b % HB
                cols = slice(bb * QT, (bb + 1) * QT)
                bank = scb[b % 2]
                if b >= 2:
                    pe.wait_ge(o_copied, b - 1)
                for i in range(2 * NBLK):
                    blk, j = i // 2, i % 2
                    s = blk
                    if j == 0:
                        pe.wait_ge(kv_in[s], 32 * (NB + b + 1))
                    g = i % 4
                    last = pe.matmul(bank[g * QT:(g + 1) * QT, :], S[:, half, i, cols], kv[:, s, :, j, :],
                                     start=(i < 4), stop=(i >= 2 * NBLK - 4 and g != 0))
                    if j == 1:
                        last.then_inc(kv_credit, 1)
                pe.matmul(bank[0:QT, :], POWN[:, b * QT:(b + 1) * QT], VTOK[:, 2, :],
                          start=False, stop=True).then_inc(o_full, 1)

            def turn_values(b):
                pe.wait_ge(o_copied, b + 1)
                bank = acc_open()
                marks["o", b] = n_acc[0]
                for h in range(H):
                    last = pe.matmul(bank[(h % 2) * DH:(h % 2 + 1) * DH, (h // 2) * T:(h // 2 + 1) * T],
                                     OSB[:, b % 2, h * DH:(h + 1) * DH], sel[:, h * T:(h + 1) * T], start=True, stop=True)
                last.then_inc(acc_full, 1)

            for half in range(2):
                pe.wait_ge(p_made, 2 * half + 2)
                for b in range(half * HB, (half + 1) * HB):
                    values(b)
                    if b == half * HB:
                        pe.wait_ge(d_step[half], 4)
                        pe.matmul(acc_open()[:, 0:HC], ones[:, :], RM[:, half, :], start=True, stop=True).then_inc(acc_full, 1)
                    else:
                        turn_values(b - 1)
                turn_values((half + 1) * HB - 1)

            pe.wait_ge(mix_made, 1)
            for i in range(2):
                bank = tr_open(TR_COA + i)
                for c in range(CA // 2):
                    last = pe.transpose(bank[0:2 + 2 * NB, c * P:(c + 1) * P], co_a[:, i * (CA // 2) + c, :], ident[:, :])
                last.then_inc(tr_full, 1)

            assert n_acc[0] == ACC_OUT0
            u = out_project(u, KD, MIX, lambda k: pe.wait_ge(mix_made, 2) if k == 0 else None)

            def ffn(u, base, hid_base):
                u = project(u, 2 * FM, KD, HX, hx_ready(base), after=ffn_square)
                return out_project(u, FM, HID, lambda k: pe.wait_ge(hid_made, hid_base + k + 1))

            def ffn_square(pair):
                if pair == 0:
                    for k in range(KD):
                        sum_square((k, KD))

            u = ffn(u, KD, 0)

            u = project(u, CC, KD, HX, hx_ready(2 * KD), after=ffn_square)
            bank = acc_open()
            pe.wait_ge(ld_head, 64)
            for k in range(KD):
                last = pe.matmul(bank[0:SH, 0:NT], wdt[:, k, :], HX[:, k, :], start=(k == 0), stop=(k == KD - 1))
            last.then_inc(acc_full, 1)
            u = project(u, CX, KD, HX, lambda k: None)
            assert n_acc[0] == ACC_SSD

            pe.wait_ge(hs_made, 1)
            bank = acc_open()
            for t in range(3):
                rows = P if t < 2 else NS
                last = pe.transpose(bank[0:rows, t * P:(t + 1) * P], hs[:, t * P:t * P + rows], ident[:, :])
            last.then_inc(acc_full, 1)
            pe.wait_ge(xc_made, CC)
            for t in range(3):
                rows = P if t < 2 else NS
                bank = acc_open()
                for g in range(G):
                    last = pe.transpose(bank[0:rows, g * NST:(g + 1) * NST], BIG[:, CX + g, t * P:t * P + rows], ident[:, :])
                last.then_inc(acc_full, 1)
            for g in range(G):
                bank = acc_open()
                for t in range(3):
                    rows = P if t < 2 else NS
                    cols = slice(t * P, t * P + rows)
                    last = pe.matmul(bank[0:rows, cols], BIG[:, CX + g, cols], BIG[:, CX + G + g, cols], start=True, stop=True)
                last.then_inc(acc_full, 1)
            bank = acc_open()
            pe.wait_ge(consts, marks["e2"])
            for k in range(CX):
                last = pe.matmul(bank[:, k * (NB + 1):(k + 1) * (NB + 1)], E2[0:SH, k, :], decin[:, :], start=True, stop=True)
            last.then_inc(acc_full, 1)
            for g in range(G):
                bank = acc_open()
                for c in range(PG):
                    last = pe.transpose(bank[0:NS, c * P:(c + 1) * P], BIG[:, g * PG + c, NP:NT], ident[:, :])
                last.then_inc(acc_full, 1)

            pe.wait_ge(bt_made, 1)
            for b in range(NB):
                st = weights(u)
                u += 1
                yb = acc_open()
                for q in range(G):
                    n = TR_ST + b * G + q
                    bank = tr_open(n)
                    for hh in range(PG):
                        last = pe.transpose(bank[:, hh * P:(hh + 1) * P], st[:, (q * PG + hh) * NST:(q * PG + hh + 1) * NST], ident[:, :])
                    last.then_inc(tr_full, 1)
                    pe.wait_ge(tr_act if n % 2 == 0 else tr_dve, n // 2 + 1)
                    for hh in range(PG):
                        k = q * PG + hh
                        last = pe.matmul(yb[:, k * T:(k + 1) * T], S0T[:, q % 2, hh * P:(hh + 1) * P],
                                         BIG[:, CX + G + q, NP + b * T:NP + (b + 1) * T], start=True, stop=True)
                    last.then_inc(s0_used, 1)
                for q in range(G):
                    bank = acc_open()
                    for hh in range(PG):
                        k = q * PG + hh
                        last = pe.matmul(bank[:, hh * NST:(hh + 1) * NST], XWS[Q1, k * P:(k + 1) * P],
                                         BMASK[Q1, q, b, :], start=True, stop=True)
                        if q == 0 and hh == 0:
                            last.then_inc(acc_full, 1)
                    last.then_inc(acc_full, 1)

            pe.wait_ge(co_made, 1)
            for i in range(CC // 4):
                bank = tr_open(TR_CO + i)
                for c in range(4):
                    last = pe.transpose(bank[0:3 + 3 * NB, c * P:(c + 1) * P], co_s[:, 4 * i + c, :], ident[:, :])
                last.then_inc(tr_full, 1)

            for g in range(G):
                for t in range(2):
                    bank = acc_open()
                    for c in range(PG):
                        last = pe.transpose(bank[:, c * P:(c + 1) * P], BIG[:, g * PG + c, t * P:(t + 1) * P], ident[:, :])
                    last.then_inc(acc_full, 1)
                pe.wait_ge(g_made, g + 1)
                gp = g % 2
                bank = acc_open()
                pe.matmul(bank[:, :], BT[:, 0, g * NST:(g + 1) * NST], XW1[:, gp, 0, :], start=True, stop=True).then_inc(acc_full, 1)
                bank = acc_open()
                for c in range(PG):
                    cols = slice(c * P, (c + 1) * P)
                    pe.matmul(bank[:, cols], XW0[:, cols], BT[:, 0, g * NST:(g + 1) * NST], start=True, stop=False)
                    last = pe.matmul(bank[:, cols], XW1[:, gp, 1, cols], BT[:, 1, g * NST:(g + 1) * NST], start=False, stop=True)
                last.then_inc(acc_full, 1)
                for hh in range(HG):
                    h = g * HG + hh
                    pe.matmul(acc_open()[:, 0:NT], ident[0:SH, h:h + 1].to_broadcast([SH, P]), hw[:, 0, :],
                              start=True, stop=True).then_inc(acc_full, 1)
                pe.wait_ge(seg_made, g + 1)
                pe.wait_ge(sent_made, g + 1)
                for c in range(PG):
                    k = g * PG + c
                    bank = acc_open()
                    for r in range(2):
                        hh = 2 * c + r
                        rows = slice(r * DH, (r + 1) * DH)
                        cols = slice(hh * DH, (hh + 1) * DH)
                        for t in range(2):
                            pe.matmul(bank[rows, t * P:(t + 1) * P], XDT[:, gp, t, cols], SEG[:, hh, t * P:(t + 1) * P], start=True, stop=True)
                        last = pe.matmul(bank[rows, NP:NT], XDS[0:NS, g * HG * DH + hh * DH:g * HG * DH + (hh + 1) * DH],
                                         SEG[0:NS, hh, NP:NT], start=True, stop=True)
                    last.then_inc(acc_full, 1)
                    bank = acc_open()
                    pe.matmul(bank[:, 0:P], SENT[:, c * P:(c + 1) * P], BIG[:, CX + G + g, P:2 * P],
                              start=True, stop=True).then_inc(acc_full, 1)
                    bank = acc_open()
                    last = pe.matmul(bank[:, 0:NT - P], E2[0:SH, k, :], hw[:, 1, P:NT], start=True, stop=True)
                    last.then_inc(acc_full, 1)

                if g > 0:
                    for c in range(PG):
                        sum_square(((g - 1) * PG + c, CX))

            for c in range(PG):
                sum_square(((G - 1) * PG + c, CX))
            assert n_acc[0] == ACC_OUT1, (n_acc[0], ACC_OUT1)
            u = out_project(u, CX, BIG, lambda k: pe.wait_ge(hx_made, 3 * KD + k + 1))
            u = ffn(u, 3 * KD + CX, FM)

            for t in range(3):
                rows = P if t < 2 else NS
                for i in range(2):
                    bank = tr_open(TR_Y + 2 * t + i)
                    for c in range(4):
                        k = 4 * i + c
                        pe.wait_ge(x_made, 3 * KD + k + 1)
                        last = pe.transpose(bank[0:rows, c * P:(c + 1) * P], X[:, k, t * P:t * P + rows], ident[:, :])
                    last.then_inc(tr_full, 1)

        @block.scalar
        def _(act):
            n_sq, n_rt, n_hx, chain = [0], [0], [0], [0]

            def link(ins):
                chain[0] += 1
                ins.then_inc(ach, 1)
                act.wait_ge(ach, chain[0])

            def square(src):
                n = n_sq[0]
                n_sq[0] += 1
                if n >= 4:
                    act.wait_ge(sq_used, n - 3)
                act.activation(SQ[:, n % 4, :], src, ACT.Square).then_inc(sq_made, 1)

            def root(total):
                act.wait_ge(sq_used, n_sq[0])
                if n_rt[0] >= 1:
                    act.wait_ge(r_made, n_rt[0])
                n_rt[0] += 1
                act.activation(RT[:, :], stat[:, 0:NT], ACT.Sqrt, bias=eps[:, :], scale=1.0 / total).then_inc(rt_made, 1)

            def scaled(dst, src, col):
                act.activation(dst, src, ACT.Copy, scale=par[:, 0, col:col + 1]).then_inc(hx_made, 1)

            def copy_transposed(n, dst, src):
                act.wait_ge(tr_full, n + 1)
                act.activation(dst, src, ACT.Copy).then_inc(tr_act, 1)

            loads = [(x_prompt[0].rearrange("(t p) d -> p t d", p=P), XIN[:, 0:2, :], ld_x),
                     (x_sample.rearrange("b t d -> (b t) d"), XIN[0:NS, 2, :], ld_x)]
            row = 0
            for w in (l0_norm_mix_pre, l0_norm_mix_post, l0_norm_ffn_pre, l0_norm_ffn_post,
                      l1_norm_mix_pre, l1_norm_mix_post, l1_norm_ffn_pre, l1_norm_ffn_post, l1_norm_gate):
                k = w.shape[0] // P
                loads.append((w.rearrange("(k p) -> k p", p=P), PARIN[row:row + k, 0, :], ld_par))
                row += k
            loads.append((l0_conv_w.rearrange("j (k p) -> (j k) p", p=P), PARIN[row:row + 3 * CA, 0, :], ld_par))
            loads.append((l1_conv_b.rearrange("(k p) -> k p", p=P), PARIN[row + 3 * CA:row + 3 * CA + CC, 0, :], ld_par))
            loads.append((l1_conv_w.rearrange("j (k p) -> (j k) p", p=P), PARIN[0:4 * CC, 1, :], ld_par))
            loads.append((state_conv_a.rearrange("b j c -> (b j) c"), HISTA_IN[0:2 * NB, :], ld_hist))
            loads.append((state_conv_ssm.rearrange("b j c -> (b j) c"), HISTS_IN[0:3 * NB, :], ld_hist))
            loads.append((l1_w_in[:, DI + CC * P:].rearrange("(k p) n -> p k n", p=P), wdt[:, :, :], ld_head))
            for i, v in enumerate((l1_dt_bias, l1_a_log, l1_d_skip)):
                loads.append((v.unsqueeze(1), hp3[:, i:i + 1], ld_head))
            for src, dst, s in loads:
                act.dma_start(dst, src).then_inc(s, 16)

            for k in range(0, KD, 2):
                copy_transposed(TR_X + k, X[:, k, :], trb[0][:, 0:NT])
            copy_transposed(TR_PAR, par[:, 0, 0:N_PAR0], trb[0][:, 0:N_PAR0])
            copy_transposed(TR_HIST, CUS[:, :, :, 0:2], trb[0][:, 0:CA * 2 * NB].rearrange("p (c b j) -> p c b j", b=NB, j=2))
            n = 3 * NB * CC // 3
            copy_transposed(TR_HIST + 2, hists[:, CC // 3:2 * CC // 3, :], trb[0][:, 0:n].rearrange("p (c j) -> p c j", j=3 * NB))
            act.wait_ge(tr_act, (TR_HIST + 4) // 2)
            act.wait_ge(tr_dve, KD // 2)
            act.wait_ge(consts, 4)
            for k in range(KD):
                scaled(HX[:, k, :], X[:, k, :], PN["mix_pre0"] + k)
            for k in range(KD):
                square(X[:, k, :])
            root(D)

            for i, (dst, t) in enumerate(((KOUT, 0), (KOUT, 1), (KOUT, 2), (VTOK, 0), (VTOK, 1), (VTOK, 2))):
                if i % 2 == 0:
                    rows = P if t < 2 else NS
                    if i == 0:
                        act.wait_ge(zeroed, 1)
                    copy_transposed(TR_KV + i, dst[0:rows, t, :], trb[0][0:rows, :])

            def k_copies(half):
                with act.Fori(0, HB // 2) as i:
                    for s in range(2 * KVS):
                        n = half * HB * NBLK * 2 + 2 * s
                        act.wait_ge(kt_used, i * 4 * KVS + (n + 1))
                        act.wait_ge(tr_full, i * 4 * KVS + (TR_K + n + 1))
                        act.activation(KTB[:, 0, :], trb[0][:, :], ACT.Copy).then_inc(tr_act, 1)

            k_copies(0)
            k_copies(1)

            def prompt_exp(h):
                col = h * 12
                act.wait_ge(pp_ready, h + 1)
                act.activation(SP[:, h % 2, 0:P], SP[:, h % 2, 0:P], ACT.Exp, bias=small[:, col + 4:col + 5],
                               scale=SCALE, accum_out=small[:, col + 6:col + 7])
                act.activation(SP[:, h % 2, P:3 * P], SP[:, h % 2, P:3 * P], ACT.Exp, bias=small[:, col + 5:col + 6],
                               scale=SCALE, accum_out=small[:, col + 7:col + 8]).then_inc(pp_exp, 1)

            def prompt_step(i):
                if i < H:
                    prompt_exp(i)
                n = TR_PA + i - 1
                if 1 <= i <= H and n % 2 == 0:
                    if i >= 3:
                        act.wait_ge(acc_full, marks["pv", i - 3])
                    copy_transposed(n, PT[:, (i - 1) % 2, :], trb[0][:, 0:3 * P])

            def sample_exp(half):
                act.wait_ge(acc_free, marks["spread", half])
                act.activation(S[:, half, :, :], S[:, half, :, :], ACT.Exp, scale=SCALE).then_inc(p_made, 1)
                own = POWN[0:NS, half * HC:(half + 1) * HC]
                act.activation(own, own, ACT.Exp, scale=SCALE).then_inc(p_made, 1)

            for i in range(4):
                prompt_step(i)
            sample_exp(0)
            for i in range(4, 10):
                prompt_step(i)
            sample_exp(1)
            for b in range(NB):
                act.wait_ge(o_full, b + 1)
                if b >= 2:
                    act.wait_ge(acc_full, marks["o", b - 2])
                act.activation(OSB[:, b % 2, :], scb[b % 2][:, :], ACT.Copy).then_inc(o_copied, 1)
            copy_transposed(TR_COA, coT_a[0:2 + 2 * NB, 0:2 * P], trb[0][0:2 + 2 * NB, 0:2 * P])

            def post_norm(first_acc):
                for k in range(KD):
                    act.wait_ge(acc_free, first_acc + k + 1)
                    square(Y[:, k, :])
                root(D)

            def pre_norm(col, x_base):
                for k in range(KD):
                    act.wait_ge(x_made, x_base + k + 1)
                    scaled(HX[:, k, :], X[:, k, :], col + k)
                for k in range(KD):
                    square(X[:, k, :])
                root(D)

            def silus(first_acc):
                for m in range(FM):
                    act.wait_ge(acc_free, first_acc + 4 * (m // 2) + m % 2 + 1)
                    act.activation(GS[:, m % 2, :], GS[:, m % 2, :], ACT.Silu).then_inc(hid_silu, 1)

            post_norm(ACC_OUT0)
            pre_norm(PN["ffn_pre0"], 0)
            silus(ACC_GU0)
            post_norm(ACC_DOWN0)
            pre_norm(PN["mix_pre1"], KD)
            for c in range(CC):
                act.wait_ge(cv_made, c + 1)
                act.activation(BIG[:, c, :], BIG[:, c, :], ACT.Silu, bias=par[:, 0, PCB + c:PCB + c + 1]).then_inc(xc_made, 1)

            def dt_function(step, dst, src, func, scale=1.0):
                act.wait_ge(dt_step, step)
                act.activation(dst, src, func, scale=scale).then_inc(dt_act, 1)

            act.wait_ge(ld_head, 64)
            dt_function(1, hw[:, 5, :], hw[:, 4, :], ACT.Exp, -1.0)
            dt_function(1, hp3[:, 1:2], hp3[:, 1:2], ACT.Exp)
            dt_function(2, hw[:, 0, :], hw[:, 4, :], ACT.Ln)
            dt_function(3, hw[:, 1, :], hw[:, 0, :], ACT.Exp)
            dt_function(3, hw[:, 5, :], hw[:, 4, :], ACT.Exp)
            for m in range(CX):
                act.wait_ge(acc_free, ACC_Z + m + 1)
                act.activation(ZS[:, m, :], ZS[:, m, :], ACT.Silu).then_inc(zs_made, 1)

            for m in range(NB * G):
                if m % 2 == 0:
                    if m >= 2:
                        act.wait_ge(s0_used, m - 1)
                    copy_transposed(TR_ST + m, S0T[:, 0, :], trb[0][:, :])
            for i in range(0, CC // 4, 2):
                copy_transposed(TR_CO + i, CO1T[CQ:CQ + 3 + 3 * NB, i * 4 * P:(i + 1) * 4 * P], trb[0][0:3 + 3 * NB, :])
            for g in range(G):
                act.wait_ge(seg_in, g + 1)
                act.activation(SEG[:, :, :], SEG[:, :, :], ACT.Exp).then_inc(seg_exp, 1)
                for c in range(PG):
                    k = g * PG + c
                    act.wait_ge(gy_made, k + 1)
                    square(BIG[:, k, :])
                    scaled(BIG[:, k, :], BIG[:, k, :], PGATE + k)
            root(DI)
            post_norm(ACC_OUT1)
            pre_norm(PN["ffn_pre1"], 2 * KD)
            silus(ACC_GU1)
            post_norm(ACC_DOWN1)
            for t in range(3):
                rows = P if t < 2 else NS
                copy_transposed(TR_Y + 2 * t, YT[0:rows, t, 0:4 * P], trb[0][0:rows, :])

        @block.vector
        def _(dve):
            n_acc, chain, n_r = [0], [0], [0]

            def take():
                n = n_acc[0]
                n_acc[0] += 1
                dve.wait_ge(acc_full, n + 1)
                return acc[n % 4]

            def free(ins):
                ins.then_inc(acc_free, 1)

            def mark(ins):
                chain[0] += 1
                ins.then_inc(vch, 1)
                return chain[0]

            def link(ins):
                dve.wait_ge(vch, mark(ins))

            def copy_transposed(n, dst, src):
                dve.wait_ge(tr_full, n + 1)
                dve.tensor_copy(dst, src).then_inc(tr_dve, 1)

            def reciprocal_root():
                n_r[0] += 1
                dve.wait_ge(rt_made, n_r[0])
                dve.reciprocal(RR[:, :], RT[:, :]).then_inc(r_made, 1)
                dve.wait_ge(r_made, n_r[0])

            dve.sem_inc(s_free, 2)
            for k in range(1, KD, 2):
                copy_transposed(TR_X + k, X[:, k, :], trb[1][:, 0:NT])
            copy_transposed(TR_PAR + 1, par[:, 1, 0:4 * CC], trb[1][:, 0:4 * CC])
            third = CC // 3
            for i, n in ((0, TR_HIST + 1), (2, TR_HIST + 3)):
                copy_transposed(n, hists[:, i * third:(i + 1) * third, :],
                                trb[1][:, 0:third * 3 * NB].rearrange("p (c j) -> p c j", j=3 * NB))
            reciprocal_root()
            for m in list(range(MQ, M_IN0)) + list(range(MQ)):
                bank = take()
                free(dve.tensor_tensor(BIG[:, m, :], bank[:, 0:NT], RR[:, :], ALU.mult))

            dve.wait_ge(zeroed, 1)
            dve.wait_ge(acc_free, M_IN0)
            for h in range(H):
                for j in range(2):
                    last = dve.tensor_copy(
                        QB[j * DH:(j + 1) * DH, h, :, j * T:(j + 1) * T],
                        BIG[(h % 2) * DH:(h % 2 + 1) * DH, MQ + h // 2, NP:NT].rearrange("p (b t) -> p b t", t=T))
            last.then_inc(qb_made, 1)
            for r in range(2):
                own, add, got = (v.rearrange("p (b h r t) -> p b h r t", r=2, h=H // 2, t=T)[:, :, :, r, :]
                                 for v in (POWN[0:NS, :], own_bias[:, :], take()[0:NS, 0:2 * HC]))
                free(dve.tensor_tensor(own, got, add, ALU.add))
            for i, (dst, t) in enumerate(((KOUT, 0), (KOUT, 1), (KOUT, 2), (VTOK, 0), (VTOK, 1), (VTOK, 2))):
                if i % 2 == 1:
                    rows = P if t < 2 else NS
                    copy_transposed(TR_KV + i, dst[0:rows, t, :], trb[1][0:rows, :])

            def k_copies(half):
                with dve.Fori(0, HB // 2) as i:
                    for s in range(2 * KVS):
                        e, blk = s // NBLK, s % NBLK
                        n = half * HB * NBLK * 2 + 2 * s + 1
                        dve.wait_ge(kt_used, i * 4 * KVS + (n + 1))
                        dve.wait_ge(tr_full, i * 4 * KVS + (TR_K + n + 1))
                        dve.tensor_copy(KTB[:, 1, :], trb[1][:, :]).then_inc(tr_dve, 1)
                        if blk == NBLK - 1:
                            dve.wait_ge(kt_used, i * 4 * KVS + (n + 1 + 2))
                            for j in range(2):
                                last = dve.tensor_copy(
                                    S[:, half, :, :].rearrange("p (n j) c -> p n j c", j=2)[:, :, j, ds(i * 2 * QT + e * QT, QT)]
                                    .rearrange("p n (h t) -> p n h t", t=T),
                                    scb[e][:, :].rearrange("p (n h j t) -> p n h j t", n=NBLK, h=H, j=2)[:, :, :, j, :])
                            last.then_inc(s_free, 1)

            bias = [small[:, 100 + NBLK * i:100 + NBLK * (i + 1)] for i in range(2)]
            gates = small[:, 116:116 + NBLK]
            beats = small[:, 124:124 + NBLK * NBLK].rearrange("p (j i) -> p j i", i=NBLK)
            ties = small[:, 188:188 + NBLK * NBLK].rearrange("p (j i) -> p j i", i=NBLK)
            rank = small[:, 252:252 + NBLK]

            def choose(half):
                bank = take()
                ins = dve.tensor_copy(gates, bank[:, 0:NBLK])
                free(ins)
                dve.wait_ge(acc_free, n_acc[0])
                of_i = gates.unsqueeze(1).to_broadcast([P, NBLK, NBLK])
                of_j = gates.unsqueeze(2).to_broadcast([P, NBLK, NBLK])
                dve.tensor_tensor(beats, of_i, of_j, ALU.is_gt)
                link(dve.tensor_tensor(ties, of_i, of_j, ALU.is_equal))
                link(dve.tensor_tensor(ties, ties, tie[:, :, :], ALU.mult))
                link(dve.tensor_tensor(beats, beats, ties, ALU.add))
                link(dve.tensor_reduce(rank, beats, AX.X, ALU.add))
                link(dve.tensor_scalar(bias[half], rank, TOPK - 0.5, NEG, ALU.is_gt, ALU.mult))

            def bias_diagonals(half):
                dve.tensor_tensor(DIAG, ident[:, :].unsqueeze(1).to_broadcast([P, NBLK, P]),
                                  bias[half].unsqueeze(2).to_broadcast([P, NBLK, P]), ALU.mult).then_inc(d_step[half], 1)

            def mask_and_max(half):
                for i in range(2):
                    bank = take()
                    part = S[:, half, 8 * i:8 * i + 8, :].rearrange("p (n j) c -> p n j c", j=2)
                    free(dve.tensor_tensor(part, part, bank[:, :].rearrange("p (n c) -> p n c", c=HC).unsqueeze(2)
                                           .to_broadcast([P, 4, 2, HC]), ALU.add))
                dve.wait_ge(acc_free, n_acc[0])
                link(dve.tensor_reduce(RM[:, half, :], S[:, half, :, :].rearrange("p n c -> p c n"), AX.X, ALU.max))
                dve.tensor_tensor(RM[0:NS, half, :], RM[0:NS, half, :], POWN[0:NS, half * HC:(half + 1) * HC],
                                  ALU.max).then_inc(d_step[half], 1)

            def diagonal_max(half):
                bank = take()
                ins = dve.tensor_reduce(small[:, 260:261], bank[:, 0:P], AX.X, ALU.max)
                free(ins)
                dve.wait_ge(acc_free, n_acc[0])
                dve.tensor_scalar(DIAG[:, 0, :], ident[:, :], small[:, 260:261], None, ALU.mult).then_inc(d_step[half], 1)

            def less_max(half):
                bank = take()
                dve.tensor_tensor(S[:, half, :, :], S[:, half, :, :],
                                  bank[:, 0:HC].unsqueeze(1).to_broadcast([P, 2 * NBLK, HC]), ALU.subtract)
                own = POWN[0:NS, half * HC:(half + 1) * HC]
                free(dve.tensor_tensor(own, own, bank[0:NS, 0:HC], ALU.subtract))
                dve.wait_ge(acc_free, n_acc[0])

            def prompt_scores(h):
                col = h * 12
                bank = take()
                if h >= 2:
                    dve.wait_ge(tr_full, TR_PA + h - 1)
                sp = SP[:, h % 2, :]
                free(dve.tensor_tensor(sp, bank[:, 0:3 * P], tri3[:, :, :].rearrange("p a b -> p (a b)"), ALU.add))
                dve.wait_ge(acc_free, n_acc[0])
                link(dve.tensor_reduce(small[:, col:col + 3], sp.rearrange("p (a b) -> p a b", a=3), AX.X, ALU.max))
                link(dve.tensor_tensor(small[:, col + 1:col + 2], small[:, col + 1:col + 2], small[:, col + 2:col + 3], ALU.max))
                dve.tensor_scalar(small[:, col + 4:col + 6], small[:, col:col + 2], -SCALE, None, ALU.mult).then_inc(pp_ready, 1)

            def prompt_normalise(h):
                col = h * 12
                dve.wait_ge(pp_exp, h + 1)
                link(dve.reciprocal(small[:, col + 8:col + 10], small[:, col + 6:col + 8]))
                sp = SP[:, h % 2, :]
                dve.tensor_scalar(sp[:, 0:P], sp[:, 0:P], small[:, col + 8:col + 9], None, ALU.mult)
                dve.tensor_scalar(sp[:, P:3 * P], sp[:, P:3 * P], small[:, col + 9:col + 10], None, ALU.mult).then_inc(pp_made, 1)

            def prompt_step(i):
                if i < H:
                    prompt_scores(i)
                    prompt_normalise(i)
                n = TR_PA + i - 1
                if 1 <= i <= H and n % 2 == 1:
                    copy_transposed(n, PT[:, (i - 1) % 2, :], trb[1][:, 0:3 * P])
                if i >= 2:
                    h = i - 2
                    bank = take()
                    rows = slice((h % 2) * DH, (h % 2 + 1) * DH)
                    free(dve.tensor_copy(MIX[rows, CA + h // 2, 0:NP], bank[rows, 0:NP]))

            k_copies(0)
            dve.wait_ge(s_free, 2 + HB)
            choose(0)
            bias_diagonals(0)
            k_copies(1)
            choose(1)
            dve.wait_ge(s_free, 2 + NB)
            mask_and_max(0)
            prompt_step(0)
            prompt_step(1)
            diagonal_max(0)
            prompt_step(2)
            prompt_step(3)
            less_max(0)
            bias_diagonals(1)
            prompt_step(4)
            prompt_step(5)
            mask_and_max(1)
            prompt_step(6)
            prompt_step(7)
            diagonal_max(1)
            prompt_step(8)
            prompt_step(9)
            less_max(1)

            def conv_a():
                dve.wait_ge(tr_act, TR_HIST // 2 + 1)
                dve.tensor_tensor(CUP[:, :, 2:], BIG[:, CA:2 * CA, 0:NP], BIG[:, 2 * CA:3 * CA, 0:NP], ALU.mult)
                link(dve.tensor_tensor(CUS[:, :, :, 2:], BIG[:, CA:2 * CA, NP:NT].rearrange("p c (b t) -> p c b t", t=T),
                                       BIG[:, 2 * CA:3 * CA, NP:NT].rearrange("p c (b t) -> p c b t", t=T), ALU.mult))
                for j in range(3):
                    for c in range(CA):
                        w = par[:, 0, PCA + j * CA + c:PCA + j * CA + c + 1]
                        for dst, src in ((MIX[:, c, 0:NP], CUP[:, c, j:j + NP]),
                                         (MIX[:, c, NP:NT].rearrange("p (b t) -> p b t", t=T), CUS[:, c, :, j:j + T])):
                            if j == 0:
                                last = dve.tensor_scalar(dst, src, w, None, ALU.mult)
                            else:
                                last = dve.scalar_tensor_tensor(dst, src, w, dst, ALU.mult, ALU.add)
                    link(last)
                dve.tensor_tensor(MIX[:, 0:CA, :], MIX[:, 0:CA, :], BIG[:, 0:CA, :], ALU.mult)
                dve.tensor_copy(co_a[:, :, 0:2], CUP[:, :, NP:NP + 2])
                dve.tensor_copy(co_a[:, :, 2:].rearrange("p c (b j) -> p c b j", j=2), CUS[:, :, :, T:T + 2]).then_inc(mix_made, 1)

            def sum_probabilities(half):
                dve.wait_ge(p_made, 2 * half + 2)
                link(dve.tensor_reduce(RM[:, half, :], S[:, half, :, :].rearrange("p n c -> p c n"), AX.X, ALU.add))
                dve.tensor_tensor(RM[:, half, :], RM[:, half, :], POWN[:, half * HC:(half + 1) * HC],
                                  ALU.add).then_inc(d_step[half], 1)
                free(dve.reciprocal(RD[:, half, :], take()[:, 0:HC]))
                dve.wait_ge(acc_free, n_acc[0])

            def sample_output(b):
                bank = take()
                half, bb = b // HB, b % HB
                for r in range(2):
                    rows = slice(r * DH, (r + 1) * DH)
                    last = dve.tensor_tensor(
                        MIX[rows, CA:, NP + b * T:NP + (b + 1) * T],
                        bank[rows, 0:H // 2 * T].rearrange("p (h t) -> p h t", t=T),
                        RD[rows, half, bb * QT:(bb + 1) * QT].rearrange("p (h r t) -> p h r t", r=2, t=T)[:, :, r, :], ALU.mult)
                free(last)

            sum_probabilities(0)
            conv_a()
            for b in range(HB):
                sample_output(b)
            sum_probabilities(1)
            for b in range(HB, NB):
                sample_output(b)
            dve.wait_ge(acc_free, n_acc[0])
            dve.sem_inc(mix_made, 1)
            copy_transposed(TR_COA + 1, coT_a[0:2 + 2 * NB, 2 * P:4 * P], trb[1][0:2 + 2 * NB, 0:2 * P])

            def post_norm(col, input_norm=False):
                for k in range(KD):
                    if input_norm:
                        free(dve.tensor_tensor(Y[:, k, :], take()[:, 0:NT], RR[:, :], ALU.mult))
                    else:
                        free(dve.tensor_copy(Y[:, k, :], take()[:, 0:NT]))
                reciprocal_root()
                dve.wait_ge(acc_free, n_acc[0])
                marked = []
                for k in range(KD):
                    marked.append(mark(dve.scalar_tensor_tensor(Y[:, k, :], Y[:, k, :], par[:, 0, col + k:col + k + 1],
                                                                RR[:, :], ALU.mult, ALU.mult)))
                    if k:
                        dve.wait_ge(vch, marked[k - 1])
                        dve.tensor_tensor(X[:, k - 1, :], X[:, k - 1, :], Y[:, k - 1, :], ALU.add).then_inc(x_made, 1)
                dve.wait_ge(vch, marked[-1])
                dve.tensor_tensor(X[:, KD - 1, :], X[:, KD - 1, :], Y[:, KD - 1, :], ALU.add).then_inc(x_made, 1)

            def ffn(base):
                reciprocal_root()
                for pair in range(FM // 2):
                    for i in range(2):
                        bank = take()
                        if pair:
                            dve.wait_ge(hid_made, base + 2 * pair - 1 + i)
                        free(dve.tensor_tensor(GS[:, i, :], bank[:, 0:NT], RR[:, :], ALU.mult))
                    for i in range(2):
                        bank = take()
                        free(dve.tensor_tensor(US[:, i, :], bank[:, 0:NT], RR[:, :], ALU.mult))
                        dve.wait_ge(acc_free, n_acc[0])
                        dve.wait_ge(hid_silu, base + 2 * pair + i + 1)
                        dve.tensor_tensor(HID[:, 2 * pair + i, :], GS[:, i, :], US[:, i, :], ALU.mult).then_inc(hid_made, 1)

            post_norm(PN["mix_post0"])
            ffn(0)
            post_norm(PN["ffn_post0"])

            reciprocal_root()
            for c in range(CC):
                e = c % 2
                bank = take()
                new = exts[:, e, :, 3:]
                dve.tensor_tensor(ext[:, e, 3:], bank[:, 0:NP], RR[:, 0:NP], ALU.mult)
                dve.tensor_copy(exts[:, e, :, 0:3], hists[:, c, :].rearrange("p (b j) -> p b j", j=3))
                free(dve.tensor_tensor(new, bank[:, NP:NT].rearrange("p (b t) -> p b t", t=T),
                                       RR[:, NP:NT].rearrange("p (b t) -> p b t", t=T), ALU.mult))
                dve.wait_ge(acc_free, n_acc[0])
                dve.tensor_copy(co_s[:, c, 0:3], ext[:, e, NP:NP + 3])
                dve.tensor_copy(co_s[:, c, 3:].rearrange("p (b j) -> p b j", j=3), exts[:, e, :, T:T + 3])
                dst_p, dst_s = BIG[:, c, 0:NP], BIG[:, c, NP:NT].rearrange("p (b t) -> p b t", t=T)
                for j in range(4):
                    w = par[:, 1, j * CC + c:j * CC + c + 1]
                    for dst, src in ((dst_p, ext[:, e, j:j + NP]), (dst_s, exts[:, e, :, j:j + T])):
                        if j == 0:
                            last = dve.tensor_scalar(dst, src, w, None, ALU.mult)
                        else:
                            last = dve.scalar_tensor_tensor(dst, src, w, dst, ALU.mult, ALU.add)
                    if j < 3:
                        link(last)
                    else:
                        last.then_inc(cv_made, 1)
            dve.sem_inc(co_made, 1)

            dve.wait_ge(consts, marks["seg"])
            bank = take()
            w = [hw[:, i, :] for i in range(6)]
            ins = dve.tensor_tensor(w[3], bank[0:SH, 0:NT], RR[0:SH, :], ALU.mult)
            free(ins)
            dve.wait_ge(acc_free, n_acc[0])
            dve.wait_ge(ld_head, 64)
            link(dve.tensor_scalar(w[3], w[3], hp3[:, 0:1], None, ALU.add))
            link(dve.tensor_scalar(w[4], w[3], -1.0, None, ALU.mult))
            dve.tensor_tensor(w[4], w[4], w[3], ALU.max).then_inc(dt_step, 1)
            dve.wait_ge(dt_act, 2)
            dve.tensor_scalar(w[4], w[5], 1.0, None, ALU.add).then_inc(dt_step, 1)
            dve.wait_ge(dt_step, 2)
            link(dve.tensor_scalar(w[1], w[4], -1.0, None, ALU.add))
            link(dve.tensor_scalar(w[2], w[1], 0.0, None, ALU.is_equal))
            link(dve.tensor_tensor(w[1], w[1], w[2], ALU.add))
            dve.wait_ge(dt_act, 3)
            dve.tensor_tensor(w[0], w[0], w[2], ALU.add)
            link(dve.reciprocal(w[1], w[1]))
            link(dve.tensor_tensor(w[0], w[0], w[5], ALU.mult))
            link(dve.tensor_tensor(w[0], w[0], w[1], ALU.mult))
            link(dve.scalar_tensor_tensor(w[2], w[3], 0.0, w[0], ALU.max, ALU.add))
            link(dve.tensor_scalar(w[3], w[2], hp3[:, 1:2], -1.0, ALU.mult, ALU.mult))
            for t in range(2):
                cols = slice(t * P, (t + 1) * P)
                dve.tensor_tensor_scan(w[0][:, cols], ones[0:SH, :], w[3][:, cols], 0.0, ALU.mult, ALU.add)
            link(dve.tensor_copy(w[0][:, NP:NT], w[3][:, NP:NT]))
            seq = w[0][:, NP:NT].rearrange("p (b t) -> p b t", t=T)
            for t in range(1, T):
                link(dve.tensor_tensor(seq[:, :, t], seq[:, :, t], seq[:, :, t - 1], ALU.add))
            for t in range(2):
                cols = slice(t * P, (t + 1) * P)
                dve.tensor_scalar(w[4][:, cols], w[0][:, cols], -1.0, w[0][:, (t + 1) * P - 1:(t + 1) * P], ALU.mult, ALU.add)
            dve.tensor_tensor(w[4][:, NP:NT].rearrange("p (b t) -> p b t", t=T), seq[:, :, T - 1:T].to_broadcast([SH, NB, T]),
                              seq, ALU.subtract).then_inc(dt_step, 1)
            dve.tensor_copy(hs[0:SH, :], w[2])
            dve.tensor_copy(hs[2 * SH:3 * SH, :], w[0])
            dve.memset(hs[3 * SH:4 * SH, P:NT], 0.0)
            dve.tensor_copy(decin[:, NB:NB + 1], hp3[:, 2:3])
            dve.wait_ge(dt_act, 5)
            link(dve.tensor_tensor(w[5], w[5], w[2], ALU.mult))
            dve.tensor_copy(decin[:, 0:NB], w[1][:, NP:NT].rearrange("p (b t) -> p b t", t=T)[:, :, T - 1])
            dve.tensor_copy(hs[SH:2 * SH, :], w[5])
            dve.tensor_scalar(hs[3 * SH:4 * SH, 0:P], w[5][:, 0:P], w[1][:, NP - 1:NP], None, ALU.mult).then_inc(hs_made, 1)

            for m in range(CX):
                bank = take()
                free(dve.tensor_tensor(ZS[:, m, :], bank[:, 0:NT], RR[:, :], ALU.mult))

            DT, W1, AC, W0 = (i * SH for i in range(4))
            bank = take()
            dve.tensor_copy(tc[:, 0:2, :], bank[:, 0:2 * P].rearrange("p (t c) -> p t c", c=P))
            free(dve.tensor_copy(tc[0:NS, 2, :], bank[0:NS, 2 * P:3 * P]))
            for t in range(3):
                rows = P if t < 2 else NS
                free(dve.tensor_copy(BT[0:rows, t, :], take()[0:rows, :]))
            dve.wait_ge(acc_free, n_acc[0])
            dve.tensor_tensor(BMASK[Q1, :, :, :],
                              BT[0:NS, 2, :].rearrange("p (g n) -> p g n", n=NST).unsqueeze(2).to_broadcast([NS, G, NB, NST]),
                              bmask01[:, :].unsqueeze(1).unsqueeze(3).to_broadcast([NS, G, NB, NST]), ALU.mult)
            for g in range(G):
                bank = take()
                dve.tensor_tensor(CBM[:, g, 0:NP].rearrange("p (t c) -> p t c", c=P), bank[:, 0:NP].rearrange("p (t c) -> p t c", c=P),
                                  trilT[:, :].unsqueeze(1).to_broadcast([P, 2, P]), ALU.mult)
                free(dve.tensor_tensor(CBM[0:NS, g, NP:NT], bank[0:NS, NP:NT], bd01[:, :], ALU.mult))
            free(dve.tensor_copy(dec[:, :, :], take()[:, 0:CX * (NB + 1)].rearrange("p (k c) -> p k c", c=NB + 1)))

            def by_head(rows, t, first, g):
                return tc[0:rows, t, first + g * HG:first + (g + 1) * HG].unsqueeze(2).to_broadcast([rows, HG, DH])

            def heads(ap):
                return ap.rearrange("p (h d) -> p h d", d=DH)

            for g in range(G):
                bank = take()
                cols = slice(g * HG * DH, (g + 1) * HG * DH)
                dve.tensor_tensor(heads(XDS[0:NS, cols]), heads(bank[0:NS, :]), by_head(NS, 2, DT, g), ALU.mult)
                free(dve.tensor_tensor(heads(XWS[Q1, cols]), heads(bank[0:NS, :]), by_head(NS, 2, W1, g), ALU.mult))
            dve.wait_ge(acc_free, n_acc[0])
            dve.sem_inc(bt_made, 1)

            for b in range(NB):
                st = ring[:, (FIRST_STATE + b) % R, :].rearrange("p (k n) -> p k n", n=NST)
                for m in range(b * G + 1, (b + 1) * G, 2):
                    if m >= 2:
                        dve.wait_ge(s0_used, m - 1)
                    copy_transposed(TR_ST + m, S0T[:, 1, :], trb[1][:, :])
                free(dve.tensor_copy(YOS[:, :, b, :], take()[:, 0:CX * T].rearrange("p (k t) -> p k t", t=T)))
                for q in range(G):
                    bank = take()
                    for hh in range(PG):
                        k = q * PG + hh
                        last = dve.scalar_tensor_tensor(st[:, k, :], st[:, k, :], dec[:, k, b:b + 1],
                                                        bank[:, hh * NST:(hh + 1) * NST], ALU.mult, ALU.add)
                    free(last)
                dve.wait_ge(acc_free, n_acc[0])
                dve.sem_inc(st_made, 1)
            for i in range(1, CC // 4, 2):
                copy_transposed(TR_CO + i, CO1T[CQ:CQ + 3 + 3 * NB, i * 4 * P:(i + 1) * 4 * P], trb[1][0:3 + 3 * NB, :])

            for g in range(G):
                gp = g % 2
                for t in range(2):
                    bank = take()
                    dve.tensor_tensor(heads(XDT[:, gp, t, :]), heads(bank[:, :]), by_head(P, t, DT, g), ALU.mult)
                    if t == 0:
                        dve.tensor_tensor(heads(XW0), heads(bank[:, :]), by_head(P, t, W0, g), ALU.mult)
                    free(dve.tensor_tensor(heads(XW1[:, gp, t, :]), heads(bank[:, :]), by_head(P, t, W1, g), ALU.mult))
                dve.wait_ge(acc_free, n_acc[0])
                dve.sem_inc(g_made, 1)
                free(dve.tensor_copy(SENT[:, :], take()[:, :]))
                dve.wait_ge(acc_free, n_acc[0])
                dve.sem_inc(sent_made, 1)
                if g >= 1:
                    dve.wait_ge(stp_out, 16 * g)
                free(dve.tensor_copy(STP[:, :, :], take()[:, :].rearrange("p (k n) -> p k n", n=NST)))
                dve.wait_ge(acc_free, n_acc[0])
                dve.sem_inc(stp_made, 1)
                for hh in range(HG):
                    h = g * HG + hh
                    bank = take()
                    for t in range(3):
                        rows = P if t < 2 else NS
                        cols = slice(t * P, t * P + rows)
                        last = dve.tensor_scalar(SEG[0:rows, hh, cols], bank[0:rows, cols], tc[0:rows, t, AC + h:AC + h + 1],
                                                 0.0, ALU.subtract, ALU.min)
                    free(last)
                dve.wait_ge(acc_free, n_acc[0])
                dve.sem_inc(seg_in, 1)
                dve.wait_ge(seg_exp, g + 1)
                dve.tensor_tensor(SEG[:, :, :], SEG[:, :, :], CBM[:, g, :].unsqueeze(1).to_broadcast([P, HG, NT]),
                                  ALU.mult).then_inc(seg_made, 1)
                for c in range(PG):
                    k = g * PG + c
                    e = c % 2
                    within, entering, grown = take(), take(), take()
                    y, late = YTMP[:, e, :], XCH[:, e, :]
                    dve.scalar_tensor_tensor(y, BIG[:, k, :], dec[:, k, NB:NB + 1], within[:, 0:NT], ALU.mult, ALU.add).then_inc(acc_free, 1)
                    link(dve.tensor_copy(EBT[:, e, :], grown[:, 0:NT - P]))
                    dve.tensor_tensor(late[:, P:], YOS[:, k, :, :].rearrange("p b t -> p (b t)"), EBT[:, e, P:], ALU.mult)
                    dve.tensor_tensor(late[:, 0:P], entering[:, 0:P], EBT[:, e, 0:P], ALU.mult).then_inc(acc_free, 1)
                    dve.wait_ge(acc_free, n_acc[0] - 1)
                    free(dve.tensor_tensor(y[:, P:], y[:, P:], late, ALU.add))
                    dve.wait_ge(acc_free, n_acc[0])
                    dve.wait_ge(zs_made, k + 1)
                    dve.tensor_tensor(BIG[:, k, :], y, ZS[:, k, :], ALU.mult).then_inc(gy_made, 1)

            reciprocal_root()
            post_norm(PN["mix_post1"], input_norm=True)
            ffn(FM)
            post_norm(PN["ffn_post1"])
            for t in range(3):
                rows = P if t < 2 else NS
                copy_transposed(TR_Y + 2 * t + 1, YT[0:rows, t, 4 * P:8 * P], trb[1][0:rows, :])


_INS = ['x_prompt', 'x_sample', 'cache_k', 'cache_v', 'page_table', 'state_conv_a', 'state_conv_ssm', 'state_ssm',
        'l0_norm_mix_pre', 'l0_w_in', 'l0_conv_w', 'l0_w_out', 'l0_norm_mix_post',
        'l0_norm_ffn_pre', 'l0_ffn_gate', 'l0_ffn_up', 'l0_ffn_down', 'l0_norm_ffn_post',
        'l1_norm_mix_pre', 'l1_w_in', 'l1_conv_w', 'l1_conv_b', 'l1_dt_bias', 'l1_a_log', 'l1_d_skip',
        'l1_norm_gate', 'l1_w_out', 'l1_norm_mix_post',
        'l1_norm_ffn_pre', 'l1_ffn_gate', 'l1_ffn_up', 'l1_ffn_down', 'l1_norm_ffn_post']
_OUTS = [(1, 256, 1024), (8, 4, 1024), (1, 2, 8, 128, 64), (1, 2, 8, 128, 64), (8, 8, 4, 64), (8, 8, 4, 64),
         (1, 2, 512), (8, 2, 512), (1, 3, 3072), (8, 3, 3072), (1, 32, 64, 128), (8, 32, 64, 128)]


def kernel(**inputs):
    import numpy as _np
    import concourse.bacc as _bacc
    from concourse import mybir as _mybir
    from concourse.bass_utils import run_bass_kernel_spmd as _run

    nc = _bacc.Bacc("TRN2", target_bir_lowering=False, num_devices=1)
    arrays, args = {}, []
    for name in _INS:
        a = _np.ascontiguousarray(inputs[name])
        arrays[f"in_{name}_dram"] = a
        args.append(nc.dram_tensor(f"in_{name}_dram", a.shape, _mybir.dt.from_np(a.dtype), kind="ExternalInput").ap())
    for i, shape in enumerate(_OUTS):
        args.append(nc.dram_tensor(f"out_{i}_dram", shape, _mybir.dt.float32, kind="ExternalOutput").ap())
    hybrid_decoder_kernel(nc, *args)
    r = _run(nc, [arrays], core_ids=[0])
    return tuple(r.results[0][f"out_{i}_dram"] for i in range(len(_OUTS)))
```

```python
from contextlib import ExitStack

import concourse.bass as bass
from concourse import mybir

F32 = mybir.dt.float32
I32 = mybir.dt.int32
ACT = mybir.ActivationFunctionType
ALU = mybir.AluOpType
AX = mybir.AxisListType
ds = bass.ds

P = 128
NEG = -1.0e30


def hybrid_decoder_kernel(
    nc, x_prompt, x_sample, cache_k, cache_v, page_table, state_conv_a, state_conv_ssm, state_ssm,
    l0_norm_mix_pre, l0_w_in, l0_conv_w, l0_w_out, l0_norm_mix_post,
    l0_norm_ffn_pre, l0_ffn_gate, l0_ffn_up, l0_ffn_down, l0_norm_ffn_post,
    l1_norm_mix_pre, l1_w_in, l1_conv_w, l1_conv_b, l1_dt_bias, l1_a_log, l1_d_skip,
    l1_norm_gate, l1_w_out, l1_norm_mix_post,
    l1_norm_ffn_pre, l1_ffn_gate, l1_ffn_up, l1_ffn_down, l1_norm_ffn_post,
    y_prompt, y_sample, k_prompt, v_prompt, k_sample, v_sample,
    conv_a_prompt, conv_a_sample, conv_ssm_prompt, conv_ssm_sample, ssm_prompt, ssm_sample,
):
    _, NP, D = x_prompt.shape
    NB, T, _ = x_sample.shape
    NS = NB * T
    NT = NP + NS
    KD = D // P
    NPOOL, H, PAGE, DH = cache_k.shape
    NPAGES = page_table.shape[1]
    BLOCK = 2 * PAGE
    NBLK = NPAGES * PAGE // BLOCK
    TOPK = 3
    SCALE = float(DH) ** -0.5
    CA = state_conv_a.shape[2] // P
    M_IN0 = l0_w_in.shape[1] // P
    MQ, MK, MV = 3 * CA, 3 * CA + H * DH // P, 3 * CA + 2 * H * DH // P
    FM = l0_ffn_gate.shape[1] // P
    SH = l1_a_log.shape[0]
    DI = l1_w_out.shape[0]
    CX = DI // P
    NST = state_ssm.shape[3]
    CC = state_conv_ssm.shape[2] // P
    G = (CC - CX) // 2
    HG = SH // G
    PG = HG // 2
    HB = NB // 2
    HC = HB * H * T
    QT = H * T
    assert HC == P and PAGE == P and 2 * DH == P and NST == P and BLOCK == 2 * P

    UC = 2 * P
    R = 5

    def column_units(w, first, count):
        v = w.rearrange("(k p) n -> p k n", p=P)
        return [(v[:, k:min(k + KD, v.shape[1]), c:c + UC], min(KD, v.shape[1] - k))
                for c in range(first, first + count * UC, UC) for k in range(0, v.shape[1], KD)]

    in0_units = column_units(l0_w_in, MQ * P, (M_IN0 - MQ) // 2) + column_units(l0_w_in, 0, MQ // 2)

    def gate_up(g, u):
        return [x for pair in zip(column_units(g, 0, FM // 2), column_units(u, 0, FM // 2)) for x in pair]

    units_a = in0_units
    units_b = (column_units(l0_w_out, 0, KD // 2) + gate_up(l0_ffn_gate, l0_ffn_up)
               + column_units(l0_ffn_down, 0, KD // 2)
               + column_units(l1_w_in, DI, CC // 2) + column_units(l1_w_in, 0, CX // 2))
    state_units = [(state_ssm[b].rearrange("(k q) p n -> (q p) k n", q=2), CX) for b in range(NB)]
    units_c = (column_units(l1_w_out, 0, KD // 2) + gate_up(l1_ffn_gate, l1_ffn_up)
               + column_units(l1_ffn_down, 0, KD // 2))
    units = units_a + units_b + state_units + units_c
    FIRST_STATE = len(units_a) + len(units_b)

    KVS = 8

    with ExitStack() as ctx:
        def sb(name, shape, dt=F32):
            return ctx.enter_context(nc.sbuf_tensor(name, shape, dt))

        def sem(name):
            return ctx.enter_context(nc.semaphore(name))

        class Area:

            def __init__(self, tensor, at=0):
                self.tensor, self.at = tensor, at

            def take(self, *dims):
                n = 1
                for d in dims:
                    n *= d
                v = self.tensor[:, self.at:self.at + n]
                self.at += n
                assert self.at <= self.tensor.shape[1], self.at
                if len(dims) > 1:
                    names = "abcd"[:len(dims)]
                    v = v.rearrange(f"p ({' '.join(names)}) -> p {' '.join(names)}",
                                    **{m: d for m, d in zip(names[1:], dims[1:])})
                return v

        X = sb("X", [P, KD, NT])
        HX = sb("HX", [P, KD, NT])
        Y = sb("Y", [P, KD, NT])
        BIG = sb("BIG", [P, CC, NT])
        ring = sb("ring", [P, R, KD * UC])
        SQ = sb("SQ", [P, 4, NT])
        arena = sb("arena", [P, 19656])
        MIX = HX

        def flat(t):
            return t[:, :, :].rearrange("p k n -> p (k n)")

        a = Area(arena)
        kv = a.take(KVS, H, 2, DH)
        S = a.take(NB, NBLK // 2, P)
        QB = a.take(H, NB, 2 * T)
        KOUT = a.take(3, H * DH)
        VTOK = a.take(3, H * DH)
        PT = a.take(2, 3 * P)
        POWN = a.take(NB * QT)
        KNZ = a.take(H, NS)
        KNE = a.take(2, H, T)
        QZ = a.take(2, 2, 160)
        DG = a.take(2, P)
        SM = a.take(10, NB * NBLK // 2)

        CUP = a.take(CA, NP + 2)
        CUS = a.take(CA, NB, T + 2)
        SP = Area(flat(SQ)).take(2, 3 * P)
        KTB = [Area(flat(t)).take(2, 2, 4 * P) for t in (Y, HX)]
        OSB = Area(flat(Y)).take(2, H * DH)
        BEATS = Area(flat(HX)).take(2, NB * NBLK * NBLK)
        XIN = Area(arena).take(3, D)
        PARIN = Area(arena, 3 * D).take(2, P)
        HISTA_IN = Area(arena, 3 * D + 2 * P).take(CA * P)
        HISTS_IN = Area(arena, 3 * D + 2 * P + CA * P).take(CC * P)
        HID = Area(arena).take(FM, NT)
        GS = Area(arena, FM * NT).take(2, NT)
        US = Area(arena, (FM + 2) * NT).take(2, NT)
        YT = Area(arena).take(3, D)
        a = Area(arena)
        ZS = a.take(CX, NT)
        SEG = a.take(HG, NT)
        XW0 = a.take(HG * DH)
        SENT = a.take(HG * DH)
        STP = a.take(PG, NST)
        BT = a.take(3, G * NST)
        CBM = a.take(G, NT)
        S0T = a.take(2, 4 * P)
        XDT = Area(flat(HX)).take(2, 2, HG * DH)
        XW1 = Area(flat(Y)).take(2, 2, HG * DH)
        Q1 = slice(NS, 2 * NS)
        q = Area(arena, a.at)
        XDS = q.take(DI)
        E2 = q.take(CX, P)
        hwa = q.take(6, NT)
        hw = hwa[0:SH, :, :]
        q = Area(arena, a.at)
        XWS = q.take(DI)
        BMASK = q.take(G, NB, NST)
        CO1T = Area(arena, a.at).take(CC * P)
        CQ = 2 * NS

        ident = sb("ident", [P, P])
        ones = sb("ones", [P, P])
        tri3 = sb("tri3", [P, 3, P])
        trilT = sb("trilT", [P, P])
        bd01 = sb("bd01", [NS, NS])
        own_all = sb("own_all", [2 * QT, T, QT])
        own_bias = sb("own_bias", [2 * QT, T])
        same = sb("same", [P, 2, P])
        bmask01 = sb("bmask01", [NS, NB])
        tie = sb("tie", [P, NBLK, NBLK])
        sel = sb("sel", [P, QT])
        eps = sb("eps", [P, 1])
        par = sb("par", [P, 2, P])
        hists = sb("hists", [P, CC, NB * 3])
        RT = sb("RT", [P, NT])
        RR = sb("RR", [P, NT])
        coT_a = sb("coT_a", [P, CA * P])
        RMT = sb("RMT", [NB, 3, P])
        pages = sb("pages", [1, NB * NPAGES], I32)
        small = sb("small", [P, 384])
        co_a = sb("co_a", [P, CA, 2 + 2 * NB])
        ext = sb("ext", [P, 2, NP + 3])
        exts = sb("exts", [P, 2, NB, T + 3])
        co_s = sb("co_s", [P, CC, 3 + 3 * NB])
        wdt = sb("wdt", [P, KD, SH])
        hp3 = sb("hp3", [SH, 3])
        hs = sb("hs", [P, NT])
        tc = sb("tc", [P, 3, P])
        dec = sb("dec", [P, CX, NB + 1])
        decin = sb("decin", [SH, NB + 1])
        YOS = sb("YOS", [P, CX, NB, T])
        EBT = sb("EBT", [P, 2, NT - P])
        YTMP = sb("YTMP", [P, 2, NT])
        XCH = sb("XCH", [P, 2, NT - P])

        acc = [ctx.enter_context(nc.psum_tensor(f"acc{i}", [P, 512], F32)) for i in range(4)]
        trb = [ctx.enter_context(nc.psum_tensor(f"trb{i}", [P, 512], F32)) for i in range(2)]
        scb = [ctx.enter_context(nc.psum_tensor(f"scb{i}", [P, 512], F32)) for i in range(2)]
        stat = scb[0]

        PN = {n: i * KD for i, n in enumerate(
            ["mix_pre0", "mix_post0", "ffn_pre0", "ffn_post0", "mix_pre1", "mix_post1", "ffn_pre1", "ffn_post1"])}
        PGATE, PCA, PCB = 8 * KD, 8 * KD + CX, 8 * KD + CX + 3 * CA
        N_PAR0 = PCB + CC

        consts = sem("consts")
        zeroed = sem("zeroed")
        ld_x, ld_par, ld_hist, ld_head, ld_pages = (sem(n) for n in ("ld_x", "ld_par", "ld_hist", "ld_head", "ld_pages"))
        w_in = [sem(f"w_in{i}") for i in range(R)]
        w_used = sem("w_used")
        kv_in = [sem(f"kv_in{i}") for i in range(KVS)]
        v_used = sem("v_used")
        tr_full = sem("tr_full")
        tr_act = sem("tr_act")
        tr_dve = sem("tr_dve")
        acc_full = sem("acc_full")
        acc_free = sem("acc_free")
        sq_made = sem("sq_made")
        sq_used = sem("sq_used")
        rt_made = sem("rt_made")
        r_made = sem("r_made")
        hx_made = sem("hx_made")
        x_made = sem("x_made")
        qz_made = sem("qz_made")
        kt_used = sem("kt_used")
        s0_used = sem("s0_used")
        s_free = sem("s_free")
        d_step = sem("d_step")
        p_made = sem("p_made")
        dg_made = sem("dg_made")
        o_full = sem("o_full")
        o_copied = sem("o_copied")
        o_used = sem("o_used")
        pp_ready = sem("pp_ready")
        pp_exp = sem("pp_exp")
        pp_made = sem("pp_made")
        pt_used = sem("pt_used")
        mix_made = sem("mix_made")
        hid_silu = sem("hid_silu")
        hid_made = sem("hid_made")
        zs_made = sem("zs_made")
        cv_made = sem("cv_made")
        xc_made = sem("xc_made")
        co_made = sem("co_made")
        dt_step = sem("dt_step")
        dt_act = sem("dt_act")
        hs_made = sem("hs_made")
        bt_made = sem("bt_made")
        g_made = sem("g_made")
        sent_made = sem("sent_made")
        stp_made = sem("stp_made")
        stp_out = sem("stp_out")
        seg_in = sem("seg_in")
        seg_exp = sem("seg_exp")
        seg_made = sem("seg_made")
        gy_made = sem("gy_made")
        st_made = sem("st_made")
        st_out = [sem(f"st_out{i}") for i in range(R)]
        vch = sem("vch")
        ach = sem("ach")
        stored = sem("stored")

        def from_rows(bank, j):
            return bank[:, :].rearrange("p (k h j t) -> p k h j t", h=H, j=2, t=T)[:, :, :, j, :]

        def by_token(b, j):
            return S[:, b, :, :].rearrange("p m c -> p (m c)").rearrange("p (k j h t) -> p k j h t", j=2, h=H, t=T)[:, :, j, :, :]

        block = ctx.enter_context(nc.Block())

        TR_X = 0
        TR_PAR = TR_X + KD
        TR_HIST = TR_PAR + 2
        TR_KV = TR_HIST + 4
        TR_K = TR_KV + 6
        N_K = NB * NBLK * 2
        tr_order = [("sample", 0), ("sample", 1)]
        for b in range(1, H + 1):
            tr_order += ([("sample", b + 1)] if b + 1 < NB else []) + [("prompt", b - 1)]
        TR_P = {key: TR_K + N_K + i for i, key in enumerate(tr_order)}
        TR_COA = TR_K + N_K + len(tr_order)
        TR_ST = TR_COA + 2
        TR_CO = TR_ST + NB * 4
        TR_Y = TR_CO + CC // 4

        ACC_MIX = M_IN0
        ACC_OUT0 = ACC_MIX + 5 + 2 * H + NB
        ACC_GU0 = ACC_OUT0 + KD
        ACC_DOWN0 = ACC_GU0 + 2 * FM
        ACC_IN1 = ACC_DOWN0 + KD
        ACC_DT = ACC_IN1 + CC
        ACC_Z = ACC_DT + 1
        ACC_SSD = ACC_Z + CX
        ACC_OUT1 = ACC_SSD + 1 + 3 + G + 1 + G + NB * (1 + G) + G * (2 + 1 + 1 + HG + 3 * PG)
        ACC_GU1 = ACC_OUT1 + KD
        ACC_DOWN1 = ACC_GU1 + 2 * FM
        freed, used = [], 0
        for first, tiles, kparts in ((0, M_IN0, 1), (ACC_OUT0, KD, 1), (ACC_GU0, 2 * FM, 1), (ACC_DOWN0, KD, -(-FM // KD)),
                                     (ACC_IN1, CC, 1), (ACC_Z, CX, 1), (None, NB, 1),
                                     (ACC_OUT1, KD, CX // KD), (ACC_GU1, 2 * FM, 1), (ACC_DOWN1, KD, -(-FM // KD))):
            if first is None:
                freed += [(st_out[(FIRST_STATE + b) % R], 16 * (b // R + 1)) for b in range(NB)]
                continue
            for pair in range(tiles // 2):
                for part in range(kparts - 1):
                    used += 1
                    freed.append((w_used, used))
                freed.append((acc_full, first + 2 * pair + 2))
        assert len(freed) == len(units)
        marks = {}

        @block.sync
        def _(sp):
            def load_units(lo, hi):
                for u in range(lo, hi):
                    src, kb = units[u]
                    if u >= R:
                        sp.wait_ge(*freed[u - R])
                    dst = ring[:, u % R, :].rearrange("p (k n) -> p k n", n=src.shape[2])[:, 0:kb, :]
                    sp.dma_start(dst, src).then_inc(w_in[u % R], 16)

            def load_sequence(cache, b, wait):
                _, page = nc.values_load_multi_w_load_instructions(
                    pages[0:1, ds(b * NPAGES, NPAGES)], engines=[nc.sync.engine], min_val=0, max_val=NPOOL - 1,
                    skip_runtime_bounds_check_because="the page table holds pages of the pool")
                for s in range(KVS):
                    wait(s)
                    for half in range(2):
                        sp.dma_start(
                            kv[half * DH:(half + 1) * DH, s, :, :, :],
                            cache[ds(page[2 * s + half], 1), :, :, :].rearrange("o h (q j) d -> q (o h) j d", j=2),
                        ).then_inc(kv_in[s], 16)

            sp.dma_start(pages[:, :], page_table.rearrange("b n -> (b n)").unsqueeze(0)).then_inc(ld_pages, 16)
            load_units(0, R)
            sp.wait_ge(ld_pages, 16)
            load_units(R, len(units_a))
            sp.wait_ge(tr_full, TR_KV)
            load_sequence(cache_k, 0, lambda s: None)
            with sp.Fori(0, NB - 1) as i:
                load_sequence(cache_k, i + 1, lambda s: sp.wait_ge(tr_full, i * 2 * NBLK + (TR_K + 2 * s + 2)))
            load_sequence(cache_v, 0, lambda s: sp.wait_ge(tr_full, (NB - 1) * 2 * NBLK + TR_K + 2 * s + 2))
            load_units(len(units_a), len(units_a) + R)
            with sp.Fori(0, NB - 1) as i:
                load_sequence(cache_v, i + 1, lambda s: sp.wait_ge(v_used, i * NBLK + (s + 1)))
            load_units(len(units_a) + R, len(units))

        @block.gpsimd
        def _(pool):
            n = [0]

            def step(ins):
                n[0] += 1
                ins.then_inc(consts, 1)
                pool.wait_ge(consts, n[0])

            step(pool.memset(ident[:, :], 0.0))
            step(pool.affine_select(out=ident[:, :], in_=ident[:, :], compare_op=ALU.not_equal, fill=1.0,
                                    base=0, pattern=[[-1, P]], channel_multiplier=1))
            step(pool.memset(ones[:, :], 1.0))
            step(pool.memset(eps[:, :], 1e-6))
            step(pool.memset(tri3[:, :, :], 0.0))
            for i in (0, 2):
                step(pool.affine_select(out=tri3[:, i, :], in_=tri3[:, i, :], compare_op=ALU.is_ge, fill=NEG,
                                        base=0, pattern=[[-1, P]], channel_multiplier=1))
            step(pool.memset(trilT[:, :], 1.0))
            step(pool.affine_select(out=trilT[:, :], in_=trilT[:, :], compare_op=ALU.is_ge, fill=0.0,
                                    base=0, pattern=[[1, P]], channel_multiplier=-1))

            def own_columns(t, fill, mid):
                step(pool.affine_select(out=t, in_=t, compare_op=ALU.is_ge, fill=fill,
                                        base=0, pattern=[[-T, NB]] + mid + [[0, T]], channel_multiplier=1))
                step(pool.affine_select(out=t, in_=t, compare_op=ALU.is_ge, fill=fill,
                                        base=0, pattern=[[T, NB]] + mid + [[1, T]], channel_multiplier=-1))

            step(pool.memset(bd01[:, :], 1.0))
            own_columns(bd01[:, :].rearrange("p (b t) -> p b t", t=T), 0.0, [])
            step(pool.memset(own_all[:, :, :], NEG))
            for s in range(2):
                part = own_all[:, :, s * QT // 2:(s + 1) * QT // 2].rearrange("p k (a t) -> p k a t", t=T)
                step(pool.affine_select(out=part, in_=part, compare_op=ALU.not_equal, fill=0.0, base=-3 * T * s,
                                        pattern=[[0, T], [-4 * T, H // 2], [-1, T]], channel_multiplier=1))
                step(pool.affine_select(out=part, in_=part, compare_op=ALU.is_ge, fill=NEG, base=0,
                                        pattern=[[-1, T], [0, H // 2], [1, T]], channel_multiplier=0))
            marks["own"] = n[0]
            step(pool.memset(same[:, :, :], 0.0))
            for first in range(2):
                for second in range(2):
                    part = same[:, first, second * 2 * QT:(second + 1) * 2 * QT].rearrange("p (h j t) -> p h j t", j=2, t=T)
                    for j in range(2):
                        step(pool.affine_select(out=part, in_=part, compare_op=ALU.not_equal, fill=1.0,
                                                base=-first * 2 * QT - j * T,
                                                pattern=[[-2 * T, H], [0, 2], [-1, T]], channel_multiplier=1))
            marks["same"] = n[0]
            step(pool.memset(bmask01[:, :], 1.0))
            step(pool.affine_select(out=bmask01[:, :], in_=bmask01[:, :], compare_op=ALU.is_ge, fill=0.0,
                                    base=0, pattern=[[-T, NB]], channel_multiplier=1))
            step(pool.affine_select(out=bmask01[:, :], in_=bmask01[:, :], compare_op=ALU.is_ge, fill=0.0,
                                    base=T - 1, pattern=[[T, NB]], channel_multiplier=-1))
            step(pool.memset(tie[:, :, :], 1.0))
            step(pool.affine_select(out=tie[:, :, :], in_=tie[:, :, :], compare_op=ALU.is_gt, fill=0.0,
                                    base=0, pattern=[[1, NBLK], [-1, NBLK]], channel_multiplier=0))
            step(pool.memset(sel[:, :], 0.0))
            for g in range(4):
                step(pool.affine_select(out=sel[:, :], in_=sel[:, :], compare_op=ALU.not_equal, fill=1.0,
                                        base=-QT * g, pattern=[[-1, QT]], channel_multiplier=1))
            pool.memset(QB[:, :, :, :], 0.0)
            pool.memset(QZ[:, :, :, :], 0.0)
            pool.memset(KNZ[:, :, :], 0.0)
            pool.memset(VTOK[:, :, :], 0.0)
            pool.memset(POWN[:, :], 0.0)
            pool.memset(CUP[:, :, 0:2], 0.0)
            pool.memset(ext[:, :, 0:3], 0.0).then_inc(zeroed, 1)

            stores = [0]

            def store(dst, src, s=stored):
                pool.dma_start(dst, src).then_inc(s, 16)
                if s is stored:
                    stores[0] += 1

            pool.wait_ge(tr_act, TR_K // 2)
            pool.wait_ge(tr_dve, TR_K // 2)
            for buf, prompt, sample in ((KOUT, k_prompt, k_sample), (VTOK, v_prompt, v_sample)):
                for t in range(NP // PAGE):
                    store(prompt[0, t].rearrange("h q d -> q h d"),
                          buf[:, t, :].rearrange("p (h d) -> p h d", d=DH))
                for b in range(NB):
                    store(sample[b].rearrange("h t d -> t h d"),
                          buf[b * T:(b + 1) * T, 2, :].rearrange("p (h d) -> p h d", d=DH))
            pool.wait_ge(tr_act, (TR_COA + 2) // 2)
            pool.wait_ge(tr_dve, (TR_COA + 2) // 2)
            store(conv_a_prompt[0], coT_a[0:2, :])
            store(conv_a_sample.rearrange("b j c -> (b j) c"), coT_a[2:2 + 2 * NB, :])

            pool.wait_ge(mix_made, 2)
            pool.wait_ge(acc_full, ACC_IN1)
            pool.wait_ge(stored, 16 * stores[0])
            step(pool.memset(E2[0:SH, :, :], 0.0))
            step(pool.affine_select(out=E2[0:SH, :, :].rearrange("p k (q r) -> p k q r", q=2),
                                    in_=E2[0:SH, :, :].rearrange("p k (q r) -> p k q r", q=2),
                                    compare_op=ALU.not_equal, fill=1.0, base=0,
                                    pattern=[[-2, CX], [-1, 2], [0, DH]], channel_multiplier=1))
            marks["e2"] = n[0]
            step(pool.memset(CBM[:, :, :], 0.0))
            step(pool.memset(SEG[:, :, :], 0.0))
            marks["seg"] = n[0]
            for b in range(NB):
                pool.wait_ge(st_made, b + 1)
                u = FIRST_STATE + b
                store(ssm_sample[b].rearrange("(k q) p n -> (q p) k n", q=2),
                      ring[:, u % R, :].rearrange("p (k n) -> p k n", n=NST), st_out[u % R])
            pool.wait_ge(tr_act, (TR_Y) // 2)
            pool.wait_ge(tr_dve, (TR_Y) // 2)
            store(conv_ssm_prompt[0], CO1T[CQ:CQ + 3, :])
            store(conv_ssm_sample.rearrange("b j c -> (b j) c"), CO1T[CQ + 3:CQ + 3 + 3 * NB, :])
            for g in range(G):
                pool.wait_ge(stp_made, g + 1)
                store(ssm_prompt[0, g * HG:(g + 1) * HG].rearrange("(k q) p n -> (q p) k n", q=2), STP, stp_out)
            pool.wait_ge(tr_act, (TR_Y + 6) // 2)
            pool.wait_ge(tr_dve, (TR_Y + 6) // 2)
            for t in range(2):
                store(y_prompt[0, t * P:(t + 1) * P, :], YT[:, t, :])
            store(y_sample.rearrange("b t d -> (b t) d"), YT[0:NS, 2, :])
            pool.wait_ge(stored, 16 * stores[0])
            for b in range(NB):
                pool.wait_ge(st_out[(FIRST_STATE + b) % R], 16 * (b // R + 1))
            pool.wait_ge(stp_out, 16 * G)

        @block.tensor
        def _(pe):
            n_acc = [0]
            n_sq = [0]
            n_norm = [0]
            n_used = [0]

            def acc_open():
                n = n_acc[0]
                n_acc[0] += 1
                if n >= 4:
                    pe.wait_ge(acc_free, n - 3)
                return acc[n % 4]

            def tr_open(n):
                if n >= 2:
                    pe.wait_ge(tr_act if n % 2 == 0 else tr_dve, n // 2)
                return trb[n % 2]

            def weights(u):
                pe.wait_ge(w_in[u % R], 16 * (u // R + 1))
                return ring[:, u % R, :]

            def sum_square(last_of):
                count, total = last_of
                if count == 0 and n_norm[0] >= 1:
                    pe.wait_ge(rt_made, n_norm[0])
                pe.wait_ge(sq_made, n_sq[0] + 1)
                pe.matmul(stat[:, 0:NT], ones[:, :], SQ[:, n_sq[0] % 4, :],
                          start=(count == 0), stop=(count == total - 1)).then_inc(sq_used, 1)
                n_sq[0] += 1
                if count == total - 1:
                    n_norm[0] += 1

            def project(u, tiles, kdim, rhs, ready, first_pair_only=True, after=None):
                kparts = -(-kdim // KD)
                for pair in range(tiles // 2):
                    banks = [acc_open(), acc_open()]
                    for part in range(kparts):
                        w = weights(u)
                        ks = range(part * KD, min(part * KD + KD, kdim))
                        for i in range(2):
                            for k in ks:
                                if pair == 0 and i == 0:
                                    ready(k)
                                at = (k - part * KD) * UC + i * P
                                last = pe.matmul(banks[i][:, 0:NT], w[:, at:at + P], rhs[:, k, :],
                                                 start=(k == 0), stop=(k == kdim - 1))
                            if part == kparts - 1:
                                last.then_inc(acc_full, 1)
                        if part < kparts - 1:
                            last.then_inc(w_used, 1)
                        u += 1
                    if after:
                        after(pair)
                return u

            def hx_ready(base):
                return lambda k: pe.wait_ge(hx_made, base + k + 1)

            def out_project(u, kdim, rhs, ready):
                done = [0]

                def squares(pair):
                    for _ in range(0 if pair == 0 else 2):
                        sum_square((done[0], KD))
                        done[0] += 1

                u = project(u, KD, kdim, rhs, ready, after=squares)
                while done[0] < KD:
                    squares(1)
                return u

            pe.sem_inc(kt_used, 2)
            pe.wait_ge(consts, 2)
            pe.wait_ge(ld_x, 32)
            for k in range(KD):
                bank = tr_open(TR_X + k)
                for t in range(3):
                    rows = P if t < 2 else NS
                    last = pe.transpose(bank[:, t * P:t * P + rows], XIN[0:rows, t, k * P:(k + 1) * P], ident[0:rows, 0:rows])
                last.then_inc(tr_full, 1)
            pe.wait_ge(ld_par, 16 * 12)
            for i, rows in enumerate((N_PAR0, 4 * CC)):
                pe.transpose(tr_open(TR_PAR + i)[:, 0:rows], PARIN[0:rows, i, :], ident[0:rows, 0:rows]).then_inc(tr_full, 1)
            pe.wait_ge(ld_hist, 32)
            bank = tr_open(TR_HIST)
            for c in range(CA):
                last = pe.transpose(bank[:, c * 2 * NB:(c + 1) * 2 * NB], HISTA_IN[0:2 * NB, c * P:(c + 1) * P], ident[0:2 * NB, 0:2 * NB])
            last.then_inc(tr_full, 1)
            for i in range(3):
                bank = tr_open(TR_HIST + 1 + i)
                for c in range(CC // 3):
                    cc = i * (CC // 3) + c
                    last = pe.transpose(bank[:, c * 3 * NB:(c + 1) * 3 * NB], HISTS_IN[0:3 * NB, cc * P:(cc + 1) * P], ident[0:3 * NB, 0:3 * NB])
                last.then_inc(tr_full, 1)

            pe.wait_ge(consts, 3)
            for k in range(KD):
                sum_square((k, KD))
            u = project(0, M_IN0, KD, HX, hx_ready(0))
            for i, m in enumerate((MK, MV)):
                for t in range(3):
                    rows = P if t < 2 else NS
                    bank = tr_open(TR_KV + 3 * i + t)
                    for c in range(H * DH // P):
                        last = pe.transpose(bank[0:rows, c * P:(c + 1) * P], BIG[:, m + c, t * P:t * P + rows], ident[:, :])
                    last.then_inc(tr_full, 1)

            def k_phase():
                with pe.Fori(0, NB // 2) as i:

                    def turn(p, bp, q):
                        s = 2 * p + bp
                        if q == 0:
                            pe.wait_ge(kv_in[s % KVS], i * 64 + 32 * (s // KVS + 1))
                        pe.wait_ge(tr_dve if q else tr_act, i * 2 * KVS + (TR_K // 2 + s))
                        for hh in range(4):
                            last = pe.transpose(trb[q][:, hh * P:(hh + 1) * P],
                                                kv[:, s % KVS, 4 * q + hh, :, :].rearrange("p j d -> p (j d)"), ident[:, :])
                        last.then_inc(tr_full, 1)

                    def scores(p, hh):
                        e, pair = p // 4, p % 4
                        if hh == 0:
                            if pair == 0:
                                if e == 0:
                                    pe.wait_ge(qz_made, i + 1)
                                pe.wait_ge(s_free, i * 2 + (e + 1))
                            pe.wait_ge(tr_act, i * 2 * KVS + (TR_K // 2 + 2 * p + 2))
                            pe.wait_ge(tr_dve, i * 2 * KVS + (TR_K // 2 + 2 * p + 2))
                        if pair == 3:
                            for q in range(2):
                                pe.matmul(acc[e][q * QT:(q + 1) * QT, 0:T], QZ[:, e, q, hh * QT:(hh + 1) * QT],
                                          KNE[:, e, 4 * q + hh, :], start=(hh == 0), stop=(hh == 3))
                        for bp in range(2):
                            for q in range(2):
                                g = 2 * bp + q
                                last = pe.matmul(scb[e][g * QT:(g + 1) * QT, pair * P:(pair + 1) * P],
                                                 QZ[:, e, q, hh * QT:(hh + 1) * QT],
                                                 KTB[p % 2][:, bp, q, hh * P:(hh + 1) * P],
                                                 start=(hh == 0), stop=(hh == 3))
                        if hh == 3:
                            last.then_inc(kt_used, 1)

                    for p in range(KVS + 1):
                        for step in ("T00", "T01", "S0", "T10", "S1", "T11", "S2", "S3"):
                            if step[0] == "T" and p < KVS:
                                turn(p, int(step[1]), int(step[2]))
                            if step[0] == "S" and p > 0:
                                scores(p - 1, int(step[1]))

            def same_rows(first, src, bank, cols, start=True, stop=True):
                return pe.matmul(bank[:, cols], same[:, first, :], src, start=start, stop=stop)

            def gate():
                pe.wait_ge(consts, marks["same"])
                pe.wait_ge(d_step, 1)
                bank = acc_open()
                n = NB * NBLK // 2
                for first in range(2):
                    last = same_rows(first, SM[:, 0, :], bank, slice(first * n, (first + 1) * n))
                last.then_inc(acc_full, 1)

            def turn_max():
                pe.wait_ge(d_step, 2)
                pe.transpose(acc_open()[0:NB, 0:P], SM[:, 3, 0:NB], ident[:, :]).then_inc(acc_full, 1)

            def return_max():
                pe.wait_ge(d_step, 3)
                pe.transpose(acc_open()[:, 0:NB], RMT[:, 2, :], ident[0:NB, 0:NB]).then_inc(acc_full, 1)

            def denominators():
                pe.wait_ge(d_step, 5)
                bank = acc_open()
                same_rows(0, SM[:, 6, 0:NB], bank, slice(0, NB), stop=False)
                same_rows(1, SM[:, 6, 0:NB], bank, slice(0, NB), start=False).then_inc(acc_full, 1)

            def turn_own():
                pe.wait_ge(d_step, 6)
                pe.transpose(acc_open()[0:NS, 0:2 * QT], SM[0:2 * QT, 9, :], ident[0:2 * QT, 0:2 * QT]).then_inc(acc_full, 1)

            def turn_sample(b):
                pe.wait_ge(dg_made, b + 1)
                bank = tr_open(TR_P["sample", b])
                for m in range(NBLK // 2):
                    last = pe.matmul(bank[:, m * P:(m + 1) * P], S[:, b, m, :], DG[:, b % 2, :], start=True, stop=True)
                last.then_inc(tr_full, 1)

            def prompt_scores(h):
                rows = slice((h % 2) * DH, (h % 2 + 1) * DH)
                q, k = BIG[rows, MQ + h // 2, :], BIG[rows, MK + h // 2, :]
                bank = acc_open()
                pe.matmul(bank[:, 0:P], q[:, 0:P], k[:, 0:P], start=True, stop=True)
                pe.matmul(bank[:, P:3 * P], q[:, P:2 * P], k[:, 0:2 * P], start=True, stop=True).then_inc(acc_full, 1)

            def prompt_turn(h):
                pe.wait_ge(pp_made, h + 1)
                bank = tr_open(TR_P["prompt", h])
                for i in range(3):
                    last = pe.transpose(bank[:, i * P:(i + 1) * P], SP[:, h % 2, i * P:(i + 1) * P], ident[:, :])
                last.then_inc(tr_full, 1)

            def prompt_values(h):
                n = TR_P["prompt", h]
                pe.wait_ge(tr_act if n % 2 == 0 else tr_dve, n // 2 + 1)
                rows = slice((h % 2) * DH, (h % 2 + 1) * DH)
                cols = slice(h * DH, (h + 1) * DH)
                bank = acc_open()
                marks["pv", h] = n_acc[0]
                pe.matmul(bank[rows, 0:P], VTOK[:, 0, cols], PT[:, h % 2, 0:P], start=True, stop=True)
                pe.matmul(bank[rows, P:2 * P], VTOK[:, 0, cols], PT[:, h % 2, P:2 * P], start=True, stop=False)
                pe.matmul(bank[rows, P:2 * P], VTOK[:, 1, cols], PT[:, h % 2, 2 * P:3 * P], start=False,
                          stop=True).then_inc(acc_full, 1)

            def prompt_step(i):
                if i < H:
                    prompt_scores(i)
                if 1 <= i <= H:
                    prompt_turn(i - 1)
                if 2 <= i:
                    prompt_values(i - 2)

            pe.wait_ge(rt_made, 1)
            k_phase()
            gate()
            turn_max()
            return_max()
            prompt_step(0)
            denominators()
            turn_own()

            def values(b):
                bank = scb[b % 2]
                n = TR_P["sample", b]
                pe.wait_ge(tr_act if n % 2 == 0 else tr_dve, n // 2 + 1)
                if b >= 2:
                    pe.wait_ge(o_copied, b - 1)
                for i in range(2 * NBLK):
                    blk, j = i // 2, i % 2
                    s = blk
                    if j == 0:
                        pe.wait_ge(kv_in[s], 32 * (NB + b + 1))
                    g = i % 4
                    last = pe.matmul(bank[g * QT:(g + 1) * QT, :], S[:, b, i // 4, g * QT:(g + 1) * QT], kv[:, s, :, j, :],
                                     start=(i < 4), stop=(i >= 2 * NBLK - 4 and g != 0))
                    if j == 1:
                        last.then_inc(v_used, 1)
                if b == 0:
                    pe.wait_ge(d_step, 7)
                pe.matmul(bank[0:QT, :], POWN[:, b * QT:(b + 1) * QT], VTOK[:, 2, :],
                          start=False, stop=True).then_inc(o_full, 1)

            def turn_values(b):
                pe.wait_ge(o_copied, b + 1)
                bank = acc_open()
                marks["o", b] = n_acc[0]
                for h in range(H):
                    last = pe.matmul(bank[(h % 2) * DH:(h % 2 + 1) * DH, (h // 2) * T:(h // 2 + 1) * T],
                                     OSB[:, b % 2, h * DH:(h + 1) * DH], sel[:, h * T:(h + 1) * T], start=True, stop=True)
                last.then_inc(acc_full, 1)

            turn_sample(0)
            turn_sample(1)
            for b in range(NB):
                if 1 <= b < NB - 1:
                    turn_sample(b + 1)
                if b:
                    prompt_step(b)
                values(b)
                if b:
                    turn_values(b - 1)
            prompt_step(NB)
            turn_values(NB - 1)
            prompt_step(NB + 1)

            pe.wait_ge(mix_made, 1)
            for i in range(2):
                bank = tr_open(TR_COA + i)
                for c in range(CA // 2):
                    last = pe.transpose(bank[0:2 + 2 * NB, c * P:(c + 1) * P], co_a[:, i * (CA // 2) + c, :], ident[:, :])
                last.then_inc(tr_full, 1)

            assert n_acc[0] == ACC_OUT0
            u = out_project(u, KD, MIX, lambda k: pe.wait_ge(mix_made, 2) if k == 0 else None)

            def ffn(u, base, hid_base):
                u = project(u, 2 * FM, KD, HX, hx_ready(base), after=ffn_square)
                return out_project(u, FM, HID, lambda k: pe.wait_ge(hid_made, hid_base + k + 1))

            def ffn_square(pair):
                if pair == 0:
                    for k in range(KD):
                        sum_square((k, KD))

            u = ffn(u, KD, 0)

            u = project(u, CC, KD, HX, hx_ready(2 * KD), after=ffn_square)
            bank = acc_open()
            pe.wait_ge(ld_head, 64)
            for k in range(KD):
                last = pe.matmul(bank[0:SH, 0:NT], wdt[:, k, :], HX[:, k, :], start=(k == 0), stop=(k == KD - 1))
            last.then_inc(acc_full, 1)
            u = project(u, CX, KD, HX, lambda k: None)
            assert n_acc[0] == ACC_SSD

            pe.wait_ge(hs_made, 1)
            bank = acc_open()
            for t in range(3):
                rows = P if t < 2 else NS
                last = pe.transpose(bank[0:rows, t * P:(t + 1) * P], hs[:, t * P:t * P + rows], ident[:, :])
            last.then_inc(acc_full, 1)
            pe.wait_ge(xc_made, CC)
            for t in range(3):
                rows = P if t < 2 else NS
                bank = acc_open()
                for g in range(G):
                    last = pe.transpose(bank[0:rows, g * NST:(g + 1) * NST], BIG[:, CX + g, t * P:t * P + rows], ident[:, :])
                last.then_inc(acc_full, 1)
            for g in range(G):
                bank = acc_open()
                for t in range(3):
                    rows = P if t < 2 else NS
                    cols = slice(t * P, t * P + rows)
                    last = pe.matmul(bank[0:rows, cols], BIG[:, CX + g, cols], BIG[:, CX + G + g, cols], start=True, stop=True)
                last.then_inc(acc_full, 1)
            bank = acc_open()
            pe.wait_ge(consts, marks["e2"])
            for k in range(CX):
                last = pe.matmul(bank[:, k * (NB + 1):(k + 1) * (NB + 1)], E2[0:SH, k, :], decin[:, :], start=True, stop=True)
            last.then_inc(acc_full, 1)
            for g in range(G):
                bank = acc_open()
                for c in range(PG):
                    last = pe.transpose(bank[0:NS, c * P:(c + 1) * P], BIG[:, g * PG + c, NP:NT], ident[:, :])
                last.then_inc(acc_full, 1)

            pe.wait_ge(bt_made, 1)
            for b in range(NB):
                st = weights(u)
                u += 1
                yb = acc_open()
                for q in range(G):
                    n = TR_ST + b * G + q
                    bank = tr_open(n)
                    for hh in range(PG):
                        last = pe.transpose(bank[:, hh * P:(hh + 1) * P], st[:, (q * PG + hh) * NST:(q * PG + hh + 1) * NST], ident[:, :])
                    last.then_inc(tr_full, 1)
                    pe.wait_ge(tr_act if n % 2 == 0 else tr_dve, n // 2 + 1)
                    for hh in range(PG):
                        k = q * PG + hh
                        last = pe.matmul(yb[:, k * T:(k + 1) * T], S0T[:, q % 2, hh * P:(hh + 1) * P],
                                         BIG[:, CX + G + q, NP + b * T:NP + (b + 1) * T], start=True, stop=True)
                    last.then_inc(s0_used, 1)
                for q in range(G):
                    bank = acc_open()
                    for hh in range(PG):
                        k = q * PG + hh
                        last = pe.matmul(bank[:, hh * NST:(hh + 1) * NST], XWS[Q1, k * P:(k + 1) * P],
                                         BMASK[Q1, q, b, :], start=True, stop=True)
                        if q == 0 and hh == 0:
                            last.then_inc(acc_full, 1)
                    last.then_inc(acc_full, 1)

            pe.wait_ge(co_made, 1)
            for i in range(CC // 4):
                bank = tr_open(TR_CO + i)
                for c in range(4):
                    last = pe.transpose(bank[0:3 + 3 * NB, c * P:(c + 1) * P], co_s[:, 4 * i + c, :], ident[:, :])
                last.then_inc(tr_full, 1)

            for g in range(G):
                for t in range(2):
                    bank = acc_open()
                    for c in range(PG):
                        last = pe.transpose(bank[:, c * P:(c + 1) * P], BIG[:, g * PG + c, t * P:(t + 1) * P], ident[:, :])
                    last.then_inc(acc_full, 1)
                pe.wait_ge(g_made, g + 1)
                gp = g % 2
                bank = acc_open()
                pe.matmul(bank[:, :], BT[:, 0, g * NST:(g + 1) * NST], XW1[:, gp, 0, :], start=True, stop=True).then_inc(acc_full, 1)
                bank = acc_open()
                for c in range(PG):
                    cols = slice(c * P, (c + 1) * P)
                    pe.matmul(bank[:, cols], XW0[:, cols], BT[:, 0, g * NST:(g + 1) * NST], start=True, stop=False)
                    last = pe.matmul(bank[:, cols], XW1[:, gp, 1, cols], BT[:, 1, g * NST:(g + 1) * NST], start=False, stop=True)
                last.then_inc(acc_full, 1)
                for hh in range(HG):
                    h = g * HG + hh
                    pe.matmul(acc_open()[:, 0:NT], ident[0:SH, h:h + 1].to_broadcast([SH, P]), hw[:, 0, :],
                              start=True, stop=True).then_inc(acc_full, 1)
                pe.wait_ge(seg_made, g + 1)
                pe.wait_ge(sent_made, g + 1)
                for c in range(PG):
                    k = g * PG + c
                    bank = acc_open()
                    for r in range(2):
                        hh = 2 * c + r
                        rows = slice(r * DH, (r + 1) * DH)
                        cols = slice(hh * DH, (hh + 1) * DH)
                        for t in range(2):
                            pe.matmul(bank[rows, t * P:(t + 1) * P], XDT[:, gp, t, cols], SEG[:, hh, t * P:(t + 1) * P], start=True, stop=True)
                        last = pe.matmul(bank[rows, NP:NT], XDS[0:NS, g * HG * DH + hh * DH:g * HG * DH + (hh + 1) * DH],
                                         SEG[0:NS, hh, NP:NT], start=True, stop=True)
                    last.then_inc(acc_full, 1)
                    bank = acc_open()
                    pe.matmul(bank[:, 0:P], SENT[:, c * P:(c + 1) * P], BIG[:, CX + G + g, P:2 * P],
                              start=True, stop=True).then_inc(acc_full, 1)
                    bank = acc_open()
                    last = pe.matmul(bank[:, 0:NT - P], E2[0:SH, k, :], hw[:, 1, P:NT], start=True, stop=True)
                    last.then_inc(acc_full, 1)

                if g > 0:
                    for c in range(PG):
                        sum_square(((g - 1) * PG + c, CX))

            for c in range(PG):
                sum_square(((G - 1) * PG + c, CX))
            assert n_acc[0] == ACC_OUT1, (n_acc[0], ACC_OUT1)
            u = out_project(u, CX, BIG, lambda k: pe.wait_ge(hx_made, 3 * KD + k + 1))
            u = ffn(u, 3 * KD + CX, FM)

            for t in range(3):
                rows = P if t < 2 else NS
                for i in range(2):
                    bank = tr_open(TR_Y + 2 * t + i)
                    for c in range(4):
                        k = 4 * i + c
                        pe.wait_ge(x_made, 3 * KD + k + 1)
                        last = pe.transpose(bank[0:rows, c * P:(c + 1) * P], X[:, k, t * P:t * P + rows], ident[:, :])
                    last.then_inc(tr_full, 1)

        @block.scalar
        def _(act):
            n_sq, n_rt, n_hx, chain = [0], [0], [0], [0]

            def link(ins):
                chain[0] += 1
                ins.then_inc(ach, 1)
                act.wait_ge(ach, chain[0])

            def square(src):
                n = n_sq[0]
                n_sq[0] += 1
                if n >= 4:
                    act.wait_ge(sq_used, n - 3)
                act.activation(SQ[:, n % 4, :], src, ACT.Square).then_inc(sq_made, 1)

            def root(total):
                act.wait_ge(sq_used, n_sq[0])
                if n_rt[0] >= 1:
                    act.wait_ge(r_made, n_rt[0])
                n_rt[0] += 1
                act.activation(RT[:, :], stat[:, 0:NT], ACT.Sqrt, bias=eps[:, :], scale=1.0 / total).then_inc(rt_made, 1)

            def scaled(dst, src, col):
                act.activation(dst, src, ACT.Copy, scale=par[:, 0, col:col + 1]).then_inc(hx_made, 1)

            def copy_transposed(n, dst, src):
                act.wait_ge(tr_full, n + 1)
                act.activation(dst, src, ACT.Copy).then_inc(tr_act, 1)

            loads = [(x_prompt[0].rearrange("(t p) d -> p t d", p=P), XIN[:, 0:2, :], ld_x),
                     (x_sample.rearrange("b t d -> (b t) d"), XIN[0:NS, 2, :], ld_x)]
            row = 0
            for w in (l0_norm_mix_pre, l0_norm_mix_post, l0_norm_ffn_pre, l0_norm_ffn_post,
                      l1_norm_mix_pre, l1_norm_mix_post, l1_norm_ffn_pre, l1_norm_ffn_post, l1_norm_gate):
                k = w.shape[0] // P
                loads.append((w.rearrange("(k p) -> k p", p=P), PARIN[row:row + k, 0, :], ld_par))
                row += k
            loads.append((l0_conv_w.rearrange("j (k p) -> (j k) p", p=P), PARIN[row:row + 3 * CA, 0, :], ld_par))
            loads.append((l1_conv_b.rearrange("(k p) -> k p", p=P), PARIN[row + 3 * CA:row + 3 * CA + CC, 0, :], ld_par))
            loads.append((l1_conv_w.rearrange("j (k p) -> (j k) p", p=P), PARIN[0:4 * CC, 1, :], ld_par))
            loads.append((state_conv_a.rearrange("b j c -> (b j) c"), HISTA_IN[0:2 * NB, :], ld_hist))
            loads.append((state_conv_ssm.rearrange("b j c -> (b j) c"), HISTS_IN[0:3 * NB, :], ld_hist))
            loads.append((l1_w_in[:, DI + CC * P:].rearrange("(k p) n -> p k n", p=P), wdt[:, :, :], ld_head))
            for i, v in enumerate((l1_dt_bias, l1_a_log, l1_d_skip)):
                loads.append((v.unsqueeze(1), hp3[:, i:i + 1], ld_head))
            for src, dst, s in loads:
                act.dma_start(dst, src).then_inc(s, 16)

            for k in range(0, KD, 2):
                copy_transposed(TR_X + k, X[:, k, :], trb[0][:, 0:NT])
            copy_transposed(TR_PAR, par[:, 0, 0:N_PAR0], trb[0][:, 0:N_PAR0])
            copy_transposed(TR_HIST, CUS[:, :, :, 0:2], trb[0][:, 0:CA * 2 * NB].rearrange("p (c b j) -> p c b j", b=NB, j=2))
            n = 3 * NB * CC // 3
            copy_transposed(TR_HIST + 2, hists[:, CC // 3:2 * CC // 3, :], trb[0][:, 0:n].rearrange("p (c j) -> p c j", j=3 * NB))
            act.wait_ge(tr_act, (TR_HIST + 4) // 2)
            act.wait_ge(tr_dve, KD // 2)
            act.wait_ge(consts, 4)
            for k in range(KD):
                scaled(HX[:, k, :], X[:, k, :], PN["mix_pre0"] + k)
            for k in range(KD):
                square(X[:, k, :])
            root(D)

            for i, (dst, t) in enumerate(((KOUT, 0), (KOUT, 1), (KOUT, 2), (VTOK, 0), (VTOK, 1), (VTOK, 2))):
                if i % 2 == 0:
                    rows = P if t < 2 else NS
                    if i == 0:
                        act.wait_ge(zeroed, 1)
                    copy_transposed(TR_KV + i, dst[0:rows, t, :], trb[0][0:rows, :])

            with act.Fori(0, NB // 2) as i:
                for s in range(2 * KVS):
                    act.wait_ge(kt_used, i * KVS + (s // 2 + 1))
                    act.wait_ge(tr_full, i * 4 * KVS + (TR_K + 2 * s + 1))
                    act.activation(KTB[s // 2 % 2][:, s % 2, 0, :], trb[0][:, :], ACT.Copy).then_inc(tr_act, 1)

            def prompt_exp(h):
                col = h * 12
                act.wait_ge(pp_ready, h + 1)
                act.activation(SP[:, h % 2, 0:P], SP[:, h % 2, 0:P], ACT.Exp, bias=small[:, col + 4:col + 5],
                               scale=SCALE, accum_out=small[:, col + 6:col + 7])
                act.activation(SP[:, h % 2, P:3 * P], SP[:, h % 2, P:3 * P], ACT.Exp, bias=small[:, col + 5:col + 6],
                               scale=SCALE, accum_out=small[:, col + 7:col + 8]).then_inc(pp_exp, 1)

            def prompt_step(i):
                if i < H:
                    prompt_exp(i)
                if 1 <= i <= H and TR_P["prompt", i - 1] % 2 == 0:
                    if i >= 3:
                        act.wait_ge(acc_full, marks["pv", i - 3])
                    copy_transposed(TR_P["prompt", i - 1], PT[:, (i - 1) % 2, :], trb[0][:, 0:3 * P])

            def sample_exp(b):
                for m in range(NBLK // 2):
                    at = b * NBLK // 2 + m
                    ins = act.activation(S[:, b, m, :], S[:, b, m, :], ACT.Exp, bias=SM[:, 4, at:at + 1], scale=SCALE,
                                         accum_out=SM[:, 5, at:at + 1])
                ins.then_inc(p_made, 1)

            def copy_sample(b):
                n = TR_P["sample", b]
                if n % 2 == 0:
                    act.wait_ge(tr_full, n + 1)
                    for j in range(2):
                        last = act.activation(by_token(b, j), from_rows(trb[0], j), ACT.Copy)
                    last.then_inc(tr_act, 1)

            def copy_output(b):
                act.wait_ge(o_full, b + 1)
                if b >= 2:
                    act.wait_ge(acc_full, marks["o", b - 2])
                act.activation(OSB[:, b % 2, :], scb[b % 2][:, :], ACT.Copy).then_inc(o_copied, 1)

            act.wait_ge(d_step, 4)
            for b in range(NB):
                sample_exp(b)
            own = SM[0:2 * QT, 8, :]
            act.activation(own, own, ACT.Exp, scale=SCALE).then_inc(p_made, 1)
            prompt_step(0)
            copy_sample(0)
            copy_sample(1)
            for b in range(NB):
                if 1 <= b < NB - 1:
                    copy_sample(b + 1)
                if b:
                    prompt_step(b)
                copy_output(b)
            prompt_step(NB)
            copy_transposed(TR_COA, coT_a[0:2 + 2 * NB, 0:2 * P], trb[0][0:2 + 2 * NB, 0:2 * P])
            prompt_step(NB + 1)
            def post_norm(first_acc):
                for k in range(KD):
                    act.wait_ge(acc_free, first_acc + k + 1)
                    square(Y[:, k, :])
                root(D)

            def pre_norm(col, x_base):
                for k in range(KD):
                    act.wait_ge(x_made, x_base + k + 1)
                    scaled(HX[:, k, :], X[:, k, :], col + k)
                for k in range(KD):
                    square(X[:, k, :])
                root(D)

            def silus(first_acc):
                for m in range(FM):
                    act.wait_ge(acc_free, first_acc + 4 * (m // 2) + m % 2 + 1)
                    act.activation(GS[:, m % 2, :], GS[:, m % 2, :], ACT.Silu).then_inc(hid_silu, 1)

            post_norm(ACC_OUT0)
            pre_norm(PN["ffn_pre0"], 0)
            silus(ACC_GU0)
            post_norm(ACC_DOWN0)
            pre_norm(PN["mix_pre1"], KD)
            for c in range(CC):
                act.wait_ge(cv_made, c + 1)
                act.activation(BIG[:, c, :], BIG[:, c, :], ACT.Silu, bias=par[:, 0, PCB + c:PCB + c + 1]).then_inc(xc_made, 1)

            def dt_function(step, dst, src, func, scale=1.0):
                act.wait_ge(dt_step, step)
                act.activation(dst, src, func, scale=scale).then_inc(dt_act, 1)

            act.wait_ge(ld_head, 64)
            dt_function(1, hw[:, 5, :], hw[:, 4, :], ACT.Exp, -1.0)
            dt_function(1, hp3[:, 1:2], hp3[:, 1:2], ACT.Exp)
            dt_function(2, hw[:, 0, :], hw[:, 4, :], ACT.Ln)
            dt_function(3, hw[:, 1, :], hw[:, 0, :], ACT.Exp)
            dt_function(3, hw[:, 5, :], hw[:, 4, :], ACT.Exp)
            for m in range(CX):
                act.wait_ge(acc_free, ACC_Z + m + 1)
                act.activation(ZS[:, m, :], ZS[:, m, :], ACT.Silu).then_inc(zs_made, 1)

            for m in range(NB * G):
                if m % 2 == 0:
                    if m >= 2:
                        act.wait_ge(s0_used, m - 1)
                    copy_transposed(TR_ST + m, S0T[:, 0, :], trb[0][:, :])
            for i in range(0, CC // 4, 2):
                copy_transposed(TR_CO + i, CO1T[CQ:CQ + 3 + 3 * NB, i * 4 * P:(i + 1) * 4 * P], trb[0][0:3 + 3 * NB, :])
            for g in range(G):
                act.wait_ge(seg_in, g + 1)
                act.activation(SEG[:, :, :], SEG[:, :, :], ACT.Exp).then_inc(seg_exp, 1)
                for c in range(PG):
                    k = g * PG + c
                    act.wait_ge(gy_made, k + 1)
                    square(BIG[:, k, :])
                    scaled(BIG[:, k, :], BIG[:, k, :], PGATE + k)
            root(DI)
            post_norm(ACC_OUT1)
            pre_norm(PN["ffn_pre1"], 2 * KD)
            silus(ACC_GU1)
            post_norm(ACC_DOWN1)
            for t in range(3):
                rows = P if t < 2 else NS
                copy_transposed(TR_Y + 2 * t, YT[0:rows, t, 0:4 * P], trb[0][0:rows, :])

        @block.vector
        def _(dve):
            n_acc, chain, n_r = [0], [0], [0]

            def take():
                n = n_acc[0]
                n_acc[0] += 1
                dve.wait_ge(acc_full, n + 1)
                return acc[n % 4]

            def free(ins):
                ins.then_inc(acc_free, 1)

            def mark(ins):
                chain[0] += 1
                ins.then_inc(vch, 1)
                return chain[0]

            def link(ins):
                dve.wait_ge(vch, mark(ins))

            def copy_transposed(n, dst, src):
                dve.wait_ge(tr_full, n + 1)
                dve.tensor_copy(dst, src).then_inc(tr_dve, 1)

            def reciprocal_root():
                n_r[0] += 1
                dve.wait_ge(rt_made, n_r[0])
                dve.reciprocal(RR[:, :], RT[:, :]).then_inc(r_made, 1)
                dve.wait_ge(r_made, n_r[0])

            dve.sem_inc(s_free, 2)
            for k in range(1, KD, 2):
                copy_transposed(TR_X + k, X[:, k, :], trb[1][:, 0:NT])
            copy_transposed(TR_PAR + 1, par[:, 1, 0:4 * CC], trb[1][:, 0:4 * CC])
            third = CC // 3
            for i, n in ((0, TR_HIST + 1), (2, TR_HIST + 3)):
                copy_transposed(n, hists[:, i * third:(i + 1) * third, :],
                                trb[1][:, 0:third * 3 * NB].rearrange("p (c j) -> p c j", j=3 * NB))
            reciprocal_root()
            for m in list(range(MQ, M_IN0)) + list(range(MQ)):
                bank = take()
                free(dve.tensor_tensor(BIG[:, m, :], bank[:, 0:NT], RR[:, :], ALU.mult))

            dve.wait_ge(consts, marks["own"])
            dve.tensor_reduce(own_bias[:, :], own_all[:, :, :], AX.X, ALU.max)
            dve.wait_ge(zeroed, 1)
            dve.wait_ge(acc_free, M_IN0)
            for h in range(H):
                for j in range(2):
                    last = dve.tensor_copy(
                        QB[j * DH:(j + 1) * DH, h, :, j * T:(j + 1) * T],
                        BIG[(h % 2) * DH:(h % 2 + 1) * DH, MQ + h // 2, NP:NT].rearrange("p (b t) -> p b t", t=T))
            for r in range(2):
                rows = slice(r * DH, (r + 1) * DH)
                last = dve.tensor_copy(KNZ[rows, :, :].rearrange("p (c r) n -> p c r n", r=2)[:, :, r, :],
                                       BIG[rows, MK:MK + H // 2, NP:NT])
            link(last)
            for i, (dst, t) in enumerate(((KOUT, 0), (KOUT, 1), (KOUT, 2), (VTOK, 0), (VTOK, 1), (VTOK, 2))):
                if i % 2 == 1:
                    rows = P if t < 2 else NS
                    copy_transposed(TR_KV + i, dst[0:rows, t, :], trb[1][0:rows, :])

            def k_copies():
                with dve.Fori(0, NB // 2) as i:
                    def move_scores(e):
                        dve.wait_ge(kt_used, i * KVS + (4 * e + 6))
                        dve.tensor_tensor(SM[0:2 * QT, 7, ds(i * 2 * T + e * T, T)], acc[e][0:2 * QT, 0:T], own_bias[:, :], ALU.add)
                        dve.tensor_copy(S[:, ds(i * 2 + e, 1), :, :].rearrange("p o m c -> p (o m c)"), scb[e][:, :]).then_inc(s_free, 1)
                        dve.wait_ge(s_free, i * 2 + (e + 3))
                        of_b = S[:, ds(i * 2 + e, 1), :, :].rearrange("p o m c -> p (o m) c")
                        dve.tensor_reduce(SM[:, 0, ds(i * NBLK + e * (NBLK // 2), NBLK // 2)], of_b, AX.X, ALU.add)
                        return dve.tensor_reduce(SM[:, 1, ds(i * NBLK + e * (NBLK // 2), NBLK // 2)], of_b, AX.X, ALU.max)

                    dve.wait_ge(kt_used, i * KVS + 2)
                    for e in range(2):
                        for q in range(2):
                            last = dve.tensor_copy(
                                QZ[:, e, q, :].rearrange("p (a c) -> p a c", c=QT + 2 * T)[:, :, 0:2 * T],
                                QB[:, 4 * q:4 * q + 4, ds(i * 2 + e, 1), :].rearrange("p h o c -> p (h o) c"))
                        last = dve.tensor_copy(KNE[:, e, :, :], KNZ[:, :, ds(i * 2 * T + e * T, T)])
                    last.then_inc(qz_made, 1)
                    for s in range(2 * KVS):
                        dve.wait_ge(kt_used, i * KVS + (s // 2 + 1))
                        dve.wait_ge(tr_full, i * 4 * KVS + (TR_K + 2 * s + 2))
                        dve.tensor_copy(KTB[s // 2 % 2][:, s % 2, 1, :], trb[1][:, :]).then_inc(tr_dve, 1)
                        if s == KVS + 1:
                            move_scores(0)
                    last = move_scores(1)
                return last

            n = NBLK // 2
            SUMS, MAXS, BIAS, RMAX, EXPB, DENS, DEN, OWN_S, OWN_E, OWN_P = (SM[:, i, :] for i in range(10))
            OWN_S, OWN_E, OWN_P = (v[0:2 * QT, :].rearrange("p (b k) -> p b k", k=T) for v in (OWN_S, OWN_E, OWN_P))
            gates = small[:, 100:100 + NB * NBLK]
            rank = small[:, 164:164 + NB * NBLK]
            beats, ties = (BEATS[:, i, :].rearrange("p (b j i) -> p b j i", j=NBLK, i=NBLK) for i in range(2))
            own_max = small[0:2 * QT, 228:228 + NB]
            own_sum = small[0:2 * QT, 236:236 + NB]
            rden = small[:, 244:244 + NB]

            def choose():
                bank = take()
                by_b = gates.rearrange("p (b m f) -> p b m f", m=n, f=2)
                for first in range(2):
                    last = dve.tensor_copy(by_b[:, :, :, first],
                                           bank[:, first * NB * n:(first + 1) * NB * n].rearrange("p (b m) -> p b m", m=n))
                free(last)
                dve.wait_ge(acc_free, n_acc[0])
                g = gates.rearrange("p (b k) -> p b k", k=NBLK)
                of_i = g.unsqueeze(2).to_broadcast([P, NB, NBLK, NBLK])
                of_j = g.unsqueeze(3).to_broadcast([P, NB, NBLK, NBLK])
                dve.tensor_tensor(beats, of_i, of_j, ALU.is_gt)
                link(dve.tensor_tensor(ties, of_i, of_j, ALU.is_equal))
                link(dve.tensor_tensor(ties, ties, tie[:, :, :].unsqueeze(1).to_broadcast([P, NB, NBLK, NBLK]), ALU.mult))
                link(dve.tensor_tensor(BEATS[:, 0, :], BEATS[:, 0, :], BEATS[:, 1, :], ALU.add))
                link(dve.tensor_reduce(rank, BEATS[:, 0, :].rearrange("p (k i) -> p k i", i=NBLK), AX.X, ALU.add))
                for first in range(2):
                    rows = slice(first * 2 * QT, (first + 1) * 2 * QT)
                    last = dve.tensor_scalar(BIAS[rows, :].rearrange("p (b m) -> p b m", m=n),
                                             rank[rows, :].rearrange("p (b m f) -> p b m f", m=n, f=2)[:, :, :, first],
                                             TOPK - 0.5, NEG, ALU.is_gt, ALU.mult)
                link(last)

            def row_max():
                link(dve.tensor_tensor(MAXS, MAXS, BIAS, ALU.add))
                dve.tensor_reduce(own_max, OWN_S, AX.X, ALU.max)
                link(dve.tensor_reduce(RMAX[:, 0:NB], MAXS.rearrange("p (b m) -> p b m", m=n), AX.X, ALU.max))
                dve.tensor_tensor(RMAX[0:2 * QT, 0:NB], RMAX[0:2 * QT, 0:NB], own_max, ALU.max).then_inc(d_step, 1)

            def query_max():
                ins = dve.tensor_copy(RMT[:, 0, :], take()[0:NB, 0:P])
                free(ins)
                dve.wait_ge(acc_free, n_acc[0])
                half = RMT[:, 1, 0:2 * QT]
                link(dve.tensor_tensor(half, RMT[:, 0, 0:2 * QT], RMT[:, 0, 2 * QT:4 * QT], ALU.max))
                hjt = half.rearrange("p (h j t) -> p h j t", j=2, t=T)
                best = RMT[:, 1, 2 * QT:3 * QT].rearrange("p (h t) -> p h t", t=T)
                link(dve.tensor_tensor(best, hjt[:, :, 0, :], hjt[:, :, 1, :], ALU.max))
                for first in range(2):
                    last = dve.tensor_copy(RMT[:, 2, first * 2 * QT:(first + 1) * 2 * QT].rearrange("p (h j t) -> p h j t", j=2, t=T),
                                           best.unsqueeze(2).to_broadcast([NB, H, 2, T]))
                last.then_inc(d_step, 1)

            def exp_bias():
                bank = take()
                dve.tensor_tensor(OWN_E, OWN_S, bank[0:2 * QT, 0:NB].unsqueeze(2).to_broadcast([2 * QT, NB, T]), ALU.subtract)
                ins = dve.tensor_scalar(RMAX[:, NB:2 * NB], bank[:, 0:NB], -SCALE, None, ALU.mult)
                free(ins)
                dve.wait_ge(acc_free, n_acc[0])
                dve.tensor_tensor(EXPB.rearrange("p (b m) -> p b m", m=n), BIAS.rearrange("p (b m) -> p b m", m=n),
                                  RMAX[:, NB:2 * NB].unsqueeze(2).to_broadcast([P, NB, n]), ALU.add).then_inc(d_step, 1)

            def sum_exponentials():
                dve.wait_ge(p_made, NB + 1)
                dve.tensor_reduce(own_sum, OWN_E, AX.X, ALU.add)
                link(dve.tensor_reduce(DEN[:, 0:NB], DENS.rearrange("p (b m) -> p b m", m=n), AX.X, ALU.add))
                dve.tensor_tensor(DEN[0:2 * QT, 0:NB], DEN[0:2 * QT, 0:NB], own_sum, ALU.add).then_inc(d_step, 1)
                ins = dve.reciprocal(rden, take()[:, 0:NB])
                free(ins)
                dve.wait_ge(acc_free, n_acc[0])
                dve.tensor_tensor(OWN_P, OWN_E, rden[0:2 * QT, :].unsqueeze(2).to_broadcast([2 * QT, NB, T]),
                                  ALU.mult).then_inc(d_step, 1)

            def diagonal(b):
                if b >= 2:
                    dve.wait_ge(tr_full, TR_P["sample", b - 2] + 1)
                dve.tensor_scalar(DG[:, b % 2, :], ident[:, :], rden[:, b:b + 1], None, ALU.mult).then_inc(dg_made, 1)

            def own_probabilities():
                bank = take()
                by_j = bank[0:NS, 0:2 * QT].rearrange("p (h j t) -> p h j t", j=2, t=T)
                own = small[0:NS, 256:256 + QT]
                link(dve.tensor_copy(own.rearrange("p (h t) -> p h t", t=T), by_j[:, :, 0, :]))
                free(dve.tensor_tensor(own.rearrange("p (h t) -> p h t", t=T), by_j[:, :, 1, :],
                                       own.rearrange("p (h t) -> p h t", t=T), ALU.add))
                dve.wait_ge(acc_free, n_acc[0])
                dve.tensor_tensor(POWN[0:NS, :].rearrange("p (b q) -> p b q", q=QT), own.unsqueeze(1).to_broadcast([NS, NB, QT]),
                                  bmask01[:, :].unsqueeze(2).to_broadcast([NS, NB, QT]), ALU.mult).then_inc(d_step, 1)

            def copy_sample(b):
                k = TR_P["sample", b]
                if k % 2 == 1:
                    dve.wait_ge(tr_full, k + 1)
                    for j in range(2):
                        last = dve.tensor_copy(by_token(b, j), from_rows(trb[1], j))
                    last.then_inc(tr_dve, 1)

            def prompt_scores(h):
                col = h * 12
                bank = take()
                if h >= 2:
                    dve.wait_ge(tr_full, TR_P["prompt", h - 2] + 1)
                sp = SP[:, h % 2, :]
                free(dve.tensor_tensor(sp, bank[:, 0:3 * P], tri3[:, :, :].rearrange("p a b -> p (a b)"), ALU.add))
                dve.wait_ge(acc_free, n_acc[0])
                link(dve.tensor_reduce(small[:, col:col + 3], sp.rearrange("p (a b) -> p a b", a=3), AX.X, ALU.max))
                link(dve.tensor_tensor(small[:, col + 1:col + 2], small[:, col + 1:col + 2], small[:, col + 2:col + 3], ALU.max))
                dve.tensor_scalar(small[:, col + 4:col + 6], small[:, col:col + 2], -SCALE, None, ALU.mult).then_inc(pp_ready, 1)

            def prompt_normalise(h):
                col = h * 12
                dve.wait_ge(pp_exp, h + 1)
                link(dve.reciprocal(small[:, col + 8:col + 10], small[:, col + 6:col + 8]))
                sp = SP[:, h % 2, :]
                dve.tensor_scalar(sp[:, 0:P], sp[:, 0:P], small[:, col + 8:col + 9], None, ALU.mult)
                dve.tensor_scalar(sp[:, P:3 * P], sp[:, P:3 * P], small[:, col + 9:col + 10], None, ALU.mult).then_inc(pp_made, 1)

            def prompt_step(i):
                if i < H:
                    prompt_scores(i)
                    prompt_normalise(i)
                if 1 <= i <= H and TR_P["prompt", i - 1] % 2 == 1:
                    copy_transposed(TR_P["prompt", i - 1], PT[:, (i - 1) % 2, :], trb[1][:, 0:3 * P])
                if i >= 2:
                    h = i - 2
                    bank = take()
                    rows = slice((h % 2) * DH, (h % 2 + 1) * DH)
                    free(dve.tensor_copy(MIX[rows, CA + h // 2, 0:NP], bank[rows, 0:NP]))

            k_copies()
            link(dve.tensor_copy(SM[:, 2, 0:1], SM[:, 1, 0:1]))
            dve.sem_inc(d_step, 1)
            def conv_a():
                dve.wait_ge(tr_act, TR_HIST // 2 + 1)
                dve.tensor_tensor(CUP[:, :, 2:], BIG[:, CA:2 * CA, 0:NP], BIG[:, 2 * CA:3 * CA, 0:NP], ALU.mult)
                link(dve.tensor_tensor(CUS[:, :, :, 2:], BIG[:, CA:2 * CA, NP:NT].rearrange("p c (b t) -> p c b t", t=T),
                                       BIG[:, 2 * CA:3 * CA, NP:NT].rearrange("p c (b t) -> p c b t", t=T), ALU.mult))
                for j in range(3):
                    for c in range(CA):
                        w = par[:, 0, PCA + j * CA + c:PCA + j * CA + c + 1]
                        for dst, src in ((MIX[:, c, 0:NP], CUP[:, c, j:j + NP]),
                                         (MIX[:, c, NP:NT].rearrange("p (b t) -> p b t", t=T), CUS[:, c, :, j:j + T])):
                            if j == 0:
                                last = dve.tensor_scalar(dst, src, w, None, ALU.mult)
                            else:
                                last = dve.scalar_tensor_tensor(dst, src, w, dst, ALU.mult, ALU.add)
                    link(last)
                dve.tensor_tensor(MIX[:, 0:CA, :], MIX[:, 0:CA, :], BIG[:, 0:CA, :], ALU.mult)
                dve.tensor_copy(co_a[:, :, 0:2], CUP[:, :, NP:NP + 2])
                dve.tensor_copy(co_a[:, :, 2:].rearrange("p c (b j) -> p c b j", j=2), CUS[:, :, :, T:T + 2]).then_inc(mix_made, 1)

            def sample_output(b):
                bank = take()
                free(dve.tensor_copy(MIX[:, CA:, NP + b * T:NP + (b + 1) * T],
                                     bank[:, 0:H // 2 * T].rearrange("p (h t) -> p h t", t=T)))

            choose()
            row_max()
            query_max()
            exp_bias()
            prompt_step(0)
            sum_exponentials()
            diagonal(0)
            diagonal(1)
            own_probabilities()
            copy_sample(0)
            copy_sample(1)
            conv_a()
            for b in range(NB):
                if 1 <= b < NB - 1:
                    diagonal(b + 1)
                    copy_sample(b + 1)
                if b:
                    prompt_step(b)
                    sample_output(b - 1)
            prompt_step(NB)
            sample_output(NB - 1)
            prompt_step(NB + 1)
            dve.wait_ge(acc_free, n_acc[0])
            dve.sem_inc(mix_made, 1)
            copy_transposed(TR_COA + 1, coT_a[0:2 + 2 * NB, 2 * P:4 * P], trb[1][0:2 + 2 * NB, 0:2 * P])

            def post_norm(col, input_norm=False):
                for k in range(KD):
                    if input_norm:
                        free(dve.tensor_tensor(Y[:, k, :], take()[:, 0:NT], RR[:, :], ALU.mult))
                    else:
                        free(dve.tensor_copy(Y[:, k, :], take()[:, 0:NT]))
                reciprocal_root()
                dve.wait_ge(acc_free, n_acc[0])
                marked = []
                for k in range(KD):
                    marked.append(mark(dve.scalar_tensor_tensor(Y[:, k, :], Y[:, k, :], par[:, 0, col + k:col + k + 1],
                                                                RR[:, :], ALU.mult, ALU.mult)))
                    if k:
                        dve.wait_ge(vch, marked[k - 1])
                        dve.tensor_tensor(X[:, k - 1, :], X[:, k - 1, :], Y[:, k - 1, :], ALU.add).then_inc(x_made, 1)
                dve.wait_ge(vch, marked[-1])
                dve.tensor_tensor(X[:, KD - 1, :], X[:, KD - 1, :], Y[:, KD - 1, :], ALU.add).then_inc(x_made, 1)

            def ffn(base):
                reciprocal_root()
                for pair in range(FM // 2):
                    for i in range(2):
                        bank = take()
                        if pair:
                            dve.wait_ge(hid_made, base + 2 * pair - 1 + i)
                        free(dve.tensor_tensor(GS[:, i, :], bank[:, 0:NT], RR[:, :], ALU.mult))
                    for i in range(2):
                        bank = take()
                        free(dve.tensor_tensor(US[:, i, :], bank[:, 0:NT], RR[:, :], ALU.mult))
                        dve.wait_ge(acc_free, n_acc[0])
                        dve.wait_ge(hid_silu, base + 2 * pair + i + 1)
                        dve.tensor_tensor(HID[:, 2 * pair + i, :], GS[:, i, :], US[:, i, :], ALU.mult).then_inc(hid_made, 1)

            post_norm(PN["mix_post0"])
            ffn(0)
            post_norm(PN["ffn_post0"])

            reciprocal_root()
            for c in range(CC):
                e = c % 2
                bank = take()
                new = exts[:, e, :, 3:]
                dve.tensor_tensor(ext[:, e, 3:], bank[:, 0:NP], RR[:, 0:NP], ALU.mult)
                dve.tensor_copy(exts[:, e, :, 0:3], hists[:, c, :].rearrange("p (b j) -> p b j", j=3))
                free(dve.tensor_tensor(new, bank[:, NP:NT].rearrange("p (b t) -> p b t", t=T),
                                       RR[:, NP:NT].rearrange("p (b t) -> p b t", t=T), ALU.mult))
                dve.wait_ge(acc_free, n_acc[0])
                dve.tensor_copy(co_s[:, c, 0:3], ext[:, e, NP:NP + 3])
                dve.tensor_copy(co_s[:, c, 3:].rearrange("p (b j) -> p b j", j=3), exts[:, e, :, T:T + 3])
                dst_p, dst_s = BIG[:, c, 0:NP], BIG[:, c, NP:NT].rearrange("p (b t) -> p b t", t=T)
                for j in range(4):
                    w = par[:, 1, j * CC + c:j * CC + c + 1]
                    for dst, src in ((dst_p, ext[:, e, j:j + NP]), (dst_s, exts[:, e, :, j:j + T])):
                        if j == 0:
                            last = dve.tensor_scalar(dst, src, w, None, ALU.mult)
                        else:
                            last = dve.scalar_tensor_tensor(dst, src, w, dst, ALU.mult, ALU.add)
                    if j < 3:
                        link(last)
                    else:
                        last.then_inc(cv_made, 1)
            dve.sem_inc(co_made, 1)

            dve.wait_ge(consts, marks["seg"])
            bank = take()
            w = [hw[:, i, :] for i in range(6)]
            ins = dve.tensor_tensor(w[3], bank[0:SH, 0:NT], RR[0:SH, :], ALU.mult)
            free(ins)
            dve.wait_ge(acc_free, n_acc[0])
            dve.wait_ge(ld_head, 64)
            link(dve.tensor_scalar(w[3], w[3], hp3[:, 0:1], None, ALU.add))
            link(dve.tensor_scalar(w[4], w[3], -1.0, None, ALU.mult))
            dve.tensor_tensor(w[4], w[4], w[3], ALU.max).then_inc(dt_step, 1)
            dve.wait_ge(dt_act, 2)
            dve.tensor_scalar(w[4], w[5], 1.0, None, ALU.add).then_inc(dt_step, 1)
            dve.wait_ge(dt_step, 2)
            link(dve.tensor_scalar(w[1], w[4], -1.0, None, ALU.add))
            link(dve.tensor_scalar(w[2], w[1], 0.0, None, ALU.is_equal))
            link(dve.tensor_tensor(w[1], w[1], w[2], ALU.add))
            dve.wait_ge(dt_act, 3)
            dve.tensor_tensor(w[0], w[0], w[2], ALU.add)
            link(dve.reciprocal(w[1], w[1]))
            link(dve.tensor_tensor(w[0], w[0], w[5], ALU.mult))
            link(dve.tensor_tensor(w[0], w[0], w[1], ALU.mult))
            link(dve.scalar_tensor_tensor(w[2], w[3], 0.0, w[0], ALU.max, ALU.add))
            link(dve.tensor_scalar(w[3], w[2], hp3[:, 1:2], -1.0, ALU.mult, ALU.mult))
            for t in range(2):
                cols = slice(t * P, (t + 1) * P)
                dve.tensor_tensor_scan(w[0][:, cols], ones[0:SH, :], w[3][:, cols], 0.0, ALU.mult, ALU.add)
            link(dve.tensor_copy(w[0][:, NP:NT], w[3][:, NP:NT]))
            seq = w[0][:, NP:NT].rearrange("p (b t) -> p b t", t=T)
            for t in range(1, T):
                link(dve.tensor_tensor(seq[:, :, t], seq[:, :, t], seq[:, :, t - 1], ALU.add))
            for t in range(2):
                cols = slice(t * P, (t + 1) * P)
                dve.tensor_scalar(w[4][:, cols], w[0][:, cols], -1.0, w[0][:, (t + 1) * P - 1:(t + 1) * P], ALU.mult, ALU.add)
            dve.tensor_tensor(w[4][:, NP:NT].rearrange("p (b t) -> p b t", t=T), seq[:, :, T - 1:T].to_broadcast([SH, NB, T]),
                              seq, ALU.subtract).then_inc(dt_step, 1)
            dve.tensor_copy(hs[0:SH, :], w[2])
            dve.tensor_copy(hs[2 * SH:3 * SH, :], w[0])
            dve.memset(hs[3 * SH:4 * SH, P:NT], 0.0)
            dve.tensor_copy(decin[:, NB:NB + 1], hp3[:, 2:3])
            dve.wait_ge(dt_act, 5)
            link(dve.tensor_tensor(w[5], w[5], w[2], ALU.mult))
            dve.tensor_copy(decin[:, 0:NB], w[1][:, NP:NT].rearrange("p (b t) -> p b t", t=T)[:, :, T - 1])
            dve.tensor_copy(hs[SH:2 * SH, :], w[5])
            dve.tensor_scalar(hs[3 * SH:4 * SH, 0:P], w[5][:, 0:P], w[1][:, NP - 1:NP], None, ALU.mult).then_inc(hs_made, 1)

            for m in range(CX):
                bank = take()
                free(dve.tensor_tensor(ZS[:, m, :], bank[:, 0:NT], RR[:, :], ALU.mult))

            DT, W1, AC, W0 = (i * SH for i in range(4))
            bank = take()
            dve.tensor_copy(tc[:, 0:2, :], bank[:, 0:2 * P].rearrange("p (t c) -> p t c", c=P))
            free(dve.tensor_copy(tc[0:NS, 2, :], bank[0:NS, 2 * P:3 * P]))
            for t in range(3):
                rows = P if t < 2 else NS
                free(dve.tensor_copy(BT[0:rows, t, :], take()[0:rows, :]))
            dve.wait_ge(acc_free, n_acc[0])
            dve.tensor_tensor(BMASK[Q1, :, :, :],
                              BT[0:NS, 2, :].rearrange("p (g n) -> p g n", n=NST).unsqueeze(2).to_broadcast([NS, G, NB, NST]),
                              bmask01[:, :].unsqueeze(1).unsqueeze(3).to_broadcast([NS, G, NB, NST]), ALU.mult)
            for g in range(G):
                bank = take()
                dve.tensor_tensor(CBM[:, g, 0:NP].rearrange("p (t c) -> p t c", c=P), bank[:, 0:NP].rearrange("p (t c) -> p t c", c=P),
                                  trilT[:, :].unsqueeze(1).to_broadcast([P, 2, P]), ALU.mult)
                free(dve.tensor_tensor(CBM[0:NS, g, NP:NT], bank[0:NS, NP:NT], bd01[:, :], ALU.mult))
            free(dve.tensor_copy(dec[:, :, :], take()[:, 0:CX * (NB + 1)].rearrange("p (k c) -> p k c", c=NB + 1)))

            def by_head(rows, t, first, g):
                return tc[0:rows, t, first + g * HG:first + (g + 1) * HG].unsqueeze(2).to_broadcast([rows, HG, DH])

            def heads(ap):
                return ap.rearrange("p (h d) -> p h d", d=DH)

            for g in range(G):
                bank = take()
                cols = slice(g * HG * DH, (g + 1) * HG * DH)
                dve.tensor_tensor(heads(XDS[0:NS, cols]), heads(bank[0:NS, :]), by_head(NS, 2, DT, g), ALU.mult)
                free(dve.tensor_tensor(heads(XWS[Q1, cols]), heads(bank[0:NS, :]), by_head(NS, 2, W1, g), ALU.mult))
            dve.wait_ge(acc_free, n_acc[0])
            dve.sem_inc(bt_made, 1)

            for b in range(NB):
                st = ring[:, (FIRST_STATE + b) % R, :].rearrange("p (k n) -> p k n", n=NST)
                for m in range(b * G + 1, (b + 1) * G, 2):
                    if m >= 2:
                        dve.wait_ge(s0_used, m - 1)
                    copy_transposed(TR_ST + m, S0T[:, 1, :], trb[1][:, :])
                free(dve.tensor_copy(YOS[:, :, b, :], take()[:, 0:CX * T].rearrange("p (k t) -> p k t", t=T)))
                for q in range(G):
                    bank = take()
                    for hh in range(PG):
                        k = q * PG + hh
                        last = dve.scalar_tensor_tensor(st[:, k, :], st[:, k, :], dec[:, k, b:b + 1],
                                                        bank[:, hh * NST:(hh + 1) * NST], ALU.mult, ALU.add)
                    free(last)
                dve.wait_ge(acc_free, n_acc[0])
                dve.sem_inc(st_made, 1)
            for i in range(1, CC // 4, 2):
                copy_transposed(TR_CO + i, CO1T[CQ:CQ + 3 + 3 * NB, i * 4 * P:(i + 1) * 4 * P], trb[1][0:3 + 3 * NB, :])

            for g in range(G):
                gp = g % 2
                for t in range(2):
                    bank = take()
                    dve.tensor_tensor(heads(XDT[:, gp, t, :]), heads(bank[:, :]), by_head(P, t, DT, g), ALU.mult)
                    if t == 0:
                        dve.tensor_tensor(heads(XW0), heads(bank[:, :]), by_head(P, t, W0, g), ALU.mult)
                    free(dve.tensor_tensor(heads(XW1[:, gp, t, :]), heads(bank[:, :]), by_head(P, t, W1, g), ALU.mult))
                dve.wait_ge(acc_free, n_acc[0])
                dve.sem_inc(g_made, 1)
                free(dve.tensor_copy(SENT[:, :], take()[:, :]))
                dve.wait_ge(acc_free, n_acc[0])
                dve.sem_inc(sent_made, 1)
                if g >= 1:
                    dve.wait_ge(stp_out, 16 * g)
                free(dve.tensor_copy(STP[:, :, :], take()[:, :].rearrange("p (k n) -> p k n", n=NST)))
                dve.wait_ge(acc_free, n_acc[0])
                dve.sem_inc(stp_made, 1)
                for hh in range(HG):
                    h = g * HG + hh
                    bank = take()
                    for t in range(3):
                        rows = P if t < 2 else NS
                        cols = slice(t * P, t * P + rows)
                        last = dve.tensor_scalar(SEG[0:rows, hh, cols], bank[0:rows, cols], tc[0:rows, t, AC + h:AC + h + 1],
                                                 0.0, ALU.subtract, ALU.min)
                    free(last)
                dve.wait_ge(acc_free, n_acc[0])
                dve.sem_inc(seg_in, 1)
                dve.wait_ge(seg_exp, g + 1)
                dve.tensor_tensor(SEG[:, :, :], SEG[:, :, :], CBM[:, g, :].unsqueeze(1).to_broadcast([P, HG, NT]),
                                  ALU.mult).then_inc(seg_made, 1)
                for c in range(PG):
                    k = g * PG + c
                    e = c % 2
                    within, entering, grown = take(), take(), take()
                    y, late = YTMP[:, e, :], XCH[:, e, :]
                    dve.scalar_tensor_tensor(y, BIG[:, k, :], dec[:, k, NB:NB + 1], within[:, 0:NT], ALU.mult, ALU.add).then_inc(acc_free, 1)
                    link(dve.tensor_copy(EBT[:, e, :], grown[:, 0:NT - P]))
                    dve.tensor_tensor(late[:, P:], YOS[:, k, :, :].rearrange("p b t -> p (b t)"), EBT[:, e, P:], ALU.mult)
                    dve.tensor_tensor(late[:, 0:P], entering[:, 0:P], EBT[:, e, 0:P], ALU.mult).then_inc(acc_free, 1)
                    dve.wait_ge(acc_free, n_acc[0] - 1)
                    free(dve.tensor_tensor(y[:, P:], y[:, P:], late, ALU.add))
                    dve.wait_ge(acc_free, n_acc[0])
                    dve.wait_ge(zs_made, k + 1)
                    dve.tensor_tensor(BIG[:, k, :], y, ZS[:, k, :], ALU.mult).then_inc(gy_made, 1)

            reciprocal_root()
            post_norm(PN["mix_post1"], input_norm=True)
            ffn(FM)
            post_norm(PN["ffn_post1"])
            for t in range(3):
                rows = P if t < 2 else NS
                copy_transposed(TR_Y + 2 * t + 1, YT[0:rows, t, 4 * P:8 * P], trb[1][0:rows, :])


_INS = ['x_prompt', 'x_sample', 'cache_k', 'cache_v', 'page_table', 'state_conv_a', 'state_conv_ssm', 'state_ssm',
        'l0_norm_mix_pre', 'l0_w_in', 'l0_conv_w', 'l0_w_out', 'l0_norm_mix_post',
        'l0_norm_ffn_pre', 'l0_ffn_gate', 'l0_ffn_up', 'l0_ffn_down', 'l0_norm_ffn_post',
        'l1_norm_mix_pre', 'l1_w_in', 'l1_conv_w', 'l1_conv_b', 'l1_dt_bias', 'l1_a_log', 'l1_d_skip',
        'l1_norm_gate', 'l1_w_out', 'l1_norm_mix_post',
        'l1_norm_ffn_pre', 'l1_ffn_gate', 'l1_ffn_up', 'l1_ffn_down', 'l1_norm_ffn_post']
_OUTS = [(1, 256, 1024), (8, 4, 1024), (1, 2, 8, 128, 64), (1, 2, 8, 128, 64), (8, 8, 4, 64), (8, 8, 4, 64),
         (1, 2, 512), (8, 2, 512), (1, 3, 3072), (8, 3, 3072), (1, 32, 64, 128), (8, 32, 64, 128)]


def kernel(**inputs):
    import numpy as _np
    import concourse.bacc as _bacc
    from concourse import mybir as _mybir
    from concourse.bass_utils import run_bass_kernel_spmd as _run

    nc = _bacc.Bacc("TRN2", target_bir_lowering=False, num_devices=1)
    arrays, args = {}, []
    for name in _INS:
        a = _np.ascontiguousarray(inputs[name])
        arrays[f"in_{name}_dram"] = a
        args.append(nc.dram_tensor(f"in_{name}_dram", a.shape, _mybir.dt.from_np(a.dtype), kind="ExternalInput").ap())
    for i, shape in enumerate(_OUTS):
        args.append(nc.dram_tensor(f"out_{i}_dram", shape, _mybir.dt.float32, kind="ExternalOutput").ap())
    hybrid_decoder_kernel(nc, *args)
    r = _run(nc, [arrays], core_ids=[0])
    return tuple(r.results[0][f"out_{i}_dram"] for i in range(len(_OUTS)))
```

```python
from contextlib import ExitStack

import concourse.bass as bass
from concourse import mybir

F32 = mybir.dt.float32
F32R = mybir.dt.float32r
I32 = mybir.dt.int32
ACT = mybir.ActivationFunctionType
ALU = mybir.AluOpType
AX = mybir.AxisListType
ds = bass.ds

P = 128
NEG = -1.0e30


def hybrid_decoder_kernel(
    nc, x_prompt, x_sample, cache_k, cache_v, page_table, state_conv_a, state_conv_ssm, state_ssm,
    l0_norm_mix_pre, l0_w_in, l0_conv_w, l0_w_out, l0_norm_mix_post,
    l0_norm_ffn_pre, l0_ffn_gate, l0_ffn_up, l0_ffn_down, l0_norm_ffn_post,
    l1_norm_mix_pre, l1_w_in, l1_conv_w, l1_conv_b, l1_dt_bias, l1_a_log, l1_d_skip,
    l1_norm_gate, l1_w_out, l1_norm_mix_post,
    l1_norm_ffn_pre, l1_ffn_gate, l1_ffn_up, l1_ffn_down, l1_norm_ffn_post,
    y_prompt, y_sample, k_prompt, v_prompt, k_sample, v_sample,
    conv_a_prompt, conv_a_sample, conv_ssm_prompt, conv_ssm_sample, ssm_prompt, ssm_sample,
):
    _, NP, D = x_prompt.shape
    NB, T, _ = x_sample.shape
    NS = NB * T
    NT = NP + NS
    KD = D // P
    NPOOL, H, PAGE, DH = cache_k.shape
    NPAGES = page_table.shape[1]
    BLOCK = 2 * PAGE
    NBLK = NPAGES * PAGE // BLOCK
    TOPK = 3
    SCALE = float(DH) ** -0.5
    WARM = 8
    CA = state_conv_a.shape[2] // P
    M_IN0 = l0_w_in.shape[1] // P
    MQ, MK, MV = 3 * CA, 3 * CA + H * DH // P, 3 * CA + 2 * H * DH // P
    FM = l0_ffn_gate.shape[1] // P
    SH = l1_a_log.shape[0]
    DI = l1_w_out.shape[0]
    CX = DI // P
    NST = state_ssm.shape[3]
    CC = state_conv_ssm.shape[2] // P
    G = (CC - CX) // 2
    HG = SH // G
    PG = HG // 2
    HB = NB // 2
    HC = HB * H * T
    QT = H * T
    assert HC == P and PAGE == P and 2 * DH == P and NST == P and BLOCK == 2 * P

    UC = 2 * P
    R = 5

    def column_units(w, first, count):
        v = w.rearrange("(k p) n -> p k n", p=P)
        return [(v[:, k:min(k + KD, v.shape[1]), c:c + UC], min(KD, v.shape[1] - k))
                for c in range(first, first + count * UC, UC) for k in range(0, v.shape[1], KD)]

    in0_units = column_units(l0_w_in, MQ * P, (M_IN0 - MQ) // 2) + column_units(l0_w_in, 0, MQ // 2)

    def gate_up(g, u):
        return [x for pair in zip(column_units(g, 0, FM // 2), column_units(u, 0, FM // 2)) for x in pair]

    units_a = in0_units
    units_b = (column_units(l0_w_out, 0, KD // 2) + gate_up(l0_ffn_gate, l0_ffn_up)
               + column_units(l0_ffn_down, 0, KD // 2)
               + column_units(l1_w_in, DI, CC // 2) + column_units(l1_w_in, 0, CX // 2))
    state_units = [(state_ssm[b].rearrange("(k q) p n -> (q p) k n", q=2), CX) for b in range(NB)]
    units_c = (column_units(l1_w_out, 0, KD // 2) + gate_up(l1_ffn_gate, l1_ffn_up)
               + column_units(l1_ffn_down, 0, KD // 2))
    units = units_a + units_b + state_units + units_c
    FIRST_STATE = len(units_a) + len(units_b)

    KVS = 8

    with ExitStack() as ctx:
        def sb(name, shape, dt=F32):
            return ctx.enter_context(nc.sbuf_tensor(name, shape, dt))

        def sem(name):
            return ctx.enter_context(nc.semaphore(name))

        class Area:

            def __init__(self, tensor, at=0):
                self.tensor, self.at = tensor, at

            def take(self, *dims):
                n = 1
                for d in dims:
                    n *= d
                v = self.tensor[:, self.at:self.at + n]
                self.at += n
                assert self.at <= self.tensor.shape[1], self.at
                if len(dims) > 1:
                    names = "abcd"[:len(dims)]
                    v = v.rearrange(f"p ({' '.join(names)}) -> p {' '.join(names)}",
                                    **{m: d for m, d in zip(names[1:], dims[1:])})
                return v

        X = sb("X", [P, KD, NT])
        Y = sb("Y", [P, KD, NT])
        ring = sb("ring", [P, R, KD * UC])
        SQ = sb("SQ", [P, 4, NT])

        Z_SIZE = 28872
        W_SIZE = 2 * 2 * KD * UC
        HX_SIZE = KD * 2 * NT
        AT_W = [CC * NT + KVS * H * 2 * DH, HX_SIZE, Z_SIZE - 3272 - W_SIZE]
        AT_HX0 = AT_W[0] + W_SIZE
        AT_L1 = HX_SIZE + W_SIZE
        AT_HID = [AT_L1, HX_SIZE]
        AT_GS = [AT_L1 + FM * 2 * NT, AT_W[2] + W_SIZE]
        assert AT_W[2] >= AT_L1 + CX * NT and AT_HID[1] + FM * 2 * NT <= AT_W[2] and 2 * CX * NT <= AT_L1

        def laid_over(name, at, *shape):
            with nc.sbuf_tensor("under_" + name, [P, at if at else 1], F32) as _:
                if at:
                    with nc.sbuf_tensor(name, [P, *shape], F32R) as t:
                        return t
            with nc.sbuf_tensor(name, [P, *shape], F32R) as t:
                return t

        WHL = [laid_over(f"WHL{i}", AT_W[i], 2, 2, KD * UC) for i in range(3)]
        HX0 = laid_over("HX0", AT_HX0, KD, 2, NT)
        HX1 = laid_over("HX1", 0, KD, 2, NT)
        G1 = laid_over("G1", 0, CX, 2, NT)
        HID = [laid_over(f"HID{i}", AT_HID[i], FM, 2, NT) for i in range(2)]
        Z = sb("Z", [P, Z_SIZE])

        def flat(t):
            return t[:, :, :].rearrange("p k n -> p (k n)")

        BIG = Area(Z).take(CC, NT)
        a = Area(Z, CC * NT)
        kv = a.take(KVS, H, 2, DH)
        kv2 = Area(ring[:, :, :].rearrange("p r n -> p (r n)")).take(KVS, H, 2, DH)
        S = a.take(NB, NBLK // 2, P)
        MIX = a.take(KD, NT)
        KOUT = a.take(3, H * DH)
        VTOK = a.take(3, H * DH)
        PT = a.take(2, 3 * P)
        POWN = a.take(NB * QT)
        z = Area(Z, AT_HX0 + HX_SIZE)
        KNZ = z.take(H, NS)
        KNE = z.take(2, H, T)
        QZ = z.take(2, 2, 160)
        DG = a.take(2, P)
        SM = a.take(10, NB * NBLK // 2)

        CUP = a.take(CA, NP + 2)
        CUS = a.take(CA, NB, T + 2)
        assert a.at <= AT_HX0 + HX_SIZE
        SP = Area(flat(SQ)).take(2, 3 * P)
        KTB = [Area(flat(t)).take(2, 2, 4 * P) for t in (Y, MIX)]
        OSB = Area(flat(Y)).take(2, H * DH)
        BEATS = Area(flat(MIX)).take(2, NB * NBLK * NBLK)
        a = Area(Z, CC * NT)
        XIN = a.take(3, D)
        PARIN = a.take(2, P)
        HISTA_IN = a.take(CA * P)
        HISTS_IN = a.take(CC * P)
        gu = [Area(Z, at) for at in AT_GS]
        GS = [a.take(2, NT) for a in gu]
        US = [a.take(2, NT) for a in gu]
        HT = [a.take(2, NT) for a in gu]
        YT = Area(Z, AT_GS[1]).take(3, D)
        a = Area(Z, AT_L1)
        XBC = a.take(CC, NT)
        ZS = a.take(CX, NT)
        hwa = a.take(6, NT)
        exts = Area(Z, a.at).take(CC, NB, T + 3)
        EXTMP = Area(flat(Y)).take(CC, NB, T)
        XDT = a.take(2, 2, HG * DH)
        a = Area(Z)
        SEG = a.take(HG, NT)
        XW0 = a.take(HG * DH)
        SENT = [a.take(HG * DH), Area(Z, Z_SIZE - HG * DH).take(HG * DH)]
        STP = a.take(PG, NST)
        BT = a.take(3, G * NST)
        CBM = a.take(G, NT)
        AT_S0 = AT_L1 + (CC + CX + 6) * NT
        XW1 = Area(flat(Y)).take(2, 2, HG * DH)
        S0T = [Area(Z, AT_S0).take(G, 4 * P), Area(flat(Y)).take(G, 4 * P)]
        YSB = Area(flat(SQ)).take(2, PG * P)
        Q1 = slice(NS, 2 * NS)
        q = Area(Z, a.at)
        XDS = q.take(DI)
        E2 = q.take(CX, P)
        hw = hwa[0:SH, :, :]
        q = Area(Z, a.at)
        XWS = q.take(DI)
        BMASK = q.take(G, NB, NST)
        CO1T = Area(Z, a.at).take(CC * P)
        CQ = 2 * NS

        ident = sb("ident", [P, P])
        ones = sb("ones", [P, P])
        tri3 = sb("tri3", [P, 3, P])
        trilT = sb("trilT", [P, P])
        bd01 = sb("bd01", [NS, NS])
        own_all = sb("own_all", [2 * QT, T, QT])
        own_bias = sb("own_bias", [2 * QT, T])
        same = sb("same", [P, 2, P])
        bmask01 = sb("bmask01", [NS, NB])
        tie = sb("tie", [P, NBLK, NBLK])
        sel = sb("sel", [P, QT])
        eps = sb("eps", [P, 1])
        root_of_eps = sb("root_of_eps", [P, 1])
        par = sb("par", [P, 2, P])
        hists = sb("hists", [P, CC, NB * 3])
        RT = sb("RT", [P, NT])
        RR = sb("RR", [P, NT])
        coT_a = sb("coT_a", [P, CA * P])
        RMT = sb("RMT", [NB, 3, P])
        pages = sb("pages", [1, NB * NPAGES], I32)
        small = sb("small", [P, 384])
        co_a = sb("co_a", [P, CA, 2 + 2 * NB])
        ext = sb("ext", [P, 2, NP + 3])
        co_s = sb("co_s", [P, CC, 3 + 3 * NB])
        wdt = sb("wdt", [P, KD, SH])
        hp3 = sb("hp3", [SH, 3])
        hs = sb("hs", [P, NT])
        tc = sb("tc", [P, 3, P])
        dec = sb("dec", [P, CX, NB + 1])
        decin = sb("decin", [SH, NB + 1])
        YOS = sb("YOS", [P, CX, NB, T])
        hista = YOS[:, 0:CA, :, 0:2]
        EBT = sb("EBT", [P, 2, NT - P])
        YTMP = sb("YTMP", [P, 2, NT])
        XCH = sb("XCH", [P, 2, NT - P])

        acc = [ctx.enter_context(nc.psum_tensor(f"acc{i}", [P, 512], F32)) for i in range(4)]
        trb = [ctx.enter_context(nc.psum_tensor(f"trb{i}", [P, 512], F32)) for i in range(2)]
        scb = [ctx.enter_context(nc.psum_tensor(f"scb{i}", [P, 512], F32)) for i in range(2)]
        stat = scb[0]

        PN = {n: i * KD for i, n in enumerate(
            ["mix_pre0", "mix_post0", "ffn_pre0", "ffn_post0", "mix_pre1", "mix_post1", "ffn_pre1", "ffn_post1"])}
        PGATE, PCA, PCB = 8 * KD, 8 * KD + CX, 8 * KD + CX + 3 * CA
        N_PAR0 = PCB + CC

        consts = sem("consts")
        zeroed = sem("zeroed")
        ld_x, ld_par, ld_hist, ld_head, ld_pages = (sem(n) for n in ("ld_x", "ld_par", "ld_hist", "ld_head", "ld_pages"))
        w_in = [sem(f"w_in{i}") for i in range(R)]
        w_hi = sem("w_hi")
        w_lo = sem("w_lo")
        w_lo_pool = sem("w_lo_pool")
        w_used = sem("w_used")
        kv_in = [sem(f"kv_in{i}") for i in range(KVS)]
        kv2_in = [sem(f"kv2_in{i}") for i in range(KVS)]
        v_used = sem("v_used")
        tr_full = sem("tr_full")
        tr_act = sem("tr_act")
        tr_dve = sem("tr_dve")
        acc_full = sem("acc_full")
        acc_free = sem("acc_free")
        sq_made = sem("sq_made")
        sq_used = sem("sq_used")
        rt_made = sem("rt_made")
        r_made = sem("r_made")
        hx_hi = sem("hx_hi")
        hx_made = sem("hx_made")
        g_scaled = sem("g_scaled")
        x_made = sem("x_made")
        qz_made = sem("qz_made")
        kt_used = sem("kt_used")
        s_free = sem("s_free")
        d_step = sem("d_step")
        p_made = sem("p_made")
        dg_made = sem("dg_made")
        o_full = sem("o_full")
        o_copied = sem("o_copied")
        o_used = sem("o_used")
        pp_ready = sem("pp_ready")
        pp_exp = sem("pp_exp")
        pp_made = sem("pp_made")
        pt_used = sem("pt_used")
        mix_made = sem("mix_made")
        hid_silu = sem("hid_silu")
        ht_made = sem("ht_made")
        hid_hi = sem("hid_hi")
        hid_made = sem("hid_made")
        zs_made = sem("zs_made")
        cv_made = sem("cv_made")
        xc_made = sem("xc_made")
        co_made = sem("co_made")
        dt_step = sem("dt_step")
        dt_act = sem("dt_act")
        hs_made = sem("hs_made")
        bt_made = sem("bt_made")
        bmask_made = sem("bmask_made")
        g_made = sem("g_made")
        sent_made = sem("sent_made")
        stp_made = sem("stp_made")
        stp_out = sem("stp_out")
        seg_in = sem("seg_in")
        seg_exp = sem("seg_exp")
        seg_made = sem("seg_made")
        gy_made = sem("gy_made")
        st_made = sem("st_made")
        st_out = [sem(f"st_out{i}") for i in range(R)]
        vch = sem("vch")
        ach = sem("ach")
        kv_stored = sem("kv_stored")
        y_stored = sem("y_stored")
        stored = sem("stored")

        def from_rows(bank, j):
            return bank[:, :].rearrange("p (k h j t) -> p k h j t", h=H, j=2, t=T)[:, :, :, j, :]

        def by_token(b, j):
            return S[:, b, :, :].rearrange("p m c -> p (m c)").rearrange("p (k j h t) -> p k j h t", j=2, h=H, t=T)[:, :, j, :, :]

        def load_block(cache, page, s, second=False):
            dst, arrived = (kv2, kv2_in) if second else (kv, kv_in)
            return [(dst[half * DH:(half + 1) * DH, s, :, :, :],
                     cache[ds(page[half], 1), :, :, :].rearrange("o h (q j) d -> q (o h) j d", j=2),
                     arrived[s]) for half in range(2)]

        def page_numbers(engine, b, first, count):
            return nc.values_load_multi_w_load_instructions(
                pages[0:1, ds(b * NPAGES + first, count)], engines=[engine], min_val=0, max_val=NPOOL - 1,
                skip_runtime_bounds_check_because="the page table holds pages of the pool")[1]

        PARTS = (slice(0, 2), slice(2, NB))
        ACT_SLOTS = (KVS // 2 - 1, KVS - 1)
        IN_KV2 = [b % 2 == 1 and b < NB - 1 for b in range(NB)]
        ARRIVALS = [32 * (IN_KV2[:b + 1].count(True) if IN_KV2[b] else NB + IN_KV2[:b + 1].count(False)) for b in range(NB)]

        block = ctx.enter_context(nc.Block())

        TR_X = 0
        TR_PAR = TR_X + KD
        TR_HIST = TR_PAR + 2
        TR_KV = TR_HIST + 4
        TR_K = TR_KV + 6
        N_K = NB * NBLK * 2
        tr_order = [("sample", 0), ("sample", 1)]
        for b in range(1, H + 1):
            tr_order += ([("sample", b + 1)] if b + 1 < NB else []) + [("prompt", b - 1)]
        TR_P = {key: TR_K + N_K + i for i, key in enumerate(tr_order)}
        TR_COA = TR_K + N_K + len(tr_order)
        TR_ST = TR_COA + 2
        TR_CO = TR_ST + NB * 4
        TR_Y = TR_CO + CC // 4

        ACC_MIX = M_IN0
        ACC_OUT0 = ACC_MIX + 6 + 2 * H + NB
        ACC_GU0 = ACC_OUT0 + KD
        ACC_DOWN0 = ACC_GU0 + 2 * FM
        ACC_IN1 = ACC_DOWN0 + KD
        ACC_DT = ACC_IN1 + CC
        ACC_Z = ACC_DT + 1
        ACC_SSD = ACC_Z + CX
        ACC_OUT1 = ACC_SSD + 1 + 3 + G + 1 + G + NB * (1 + G) + G * (2 + 1 + 1 + HG + 3 * PG)
        ACC_GU1 = ACC_OUT1 + KD
        ACC_DOWN1 = ACC_GU1 + 2 * FM
        done, used, unit_of = [], 0, []
        for first, tiles, kparts in ((0, M_IN0, 1), (ACC_OUT0, KD, 1), (ACC_GU0, 2 * FM, 1), (ACC_DOWN0, KD, -(-FM // KD)),
                                     (ACC_IN1, CC, 1), (ACC_Z, CX, 1),
                                     (ACC_OUT1, KD, CX // KD), (ACC_GU1, 2 * FM, 1), (ACC_DOWN1, KD, -(-FM // KD))):
            for pair in range(tiles // 2):
                for part in range(kparts):
                    unit_of.append(len(unit_of) + (NB if len(unit_of) >= FIRST_STATE else 0))
                    if part < kparts - 1:
                        used += 1
                        done.append((w_used, used))
                    else:
                        done.append((acc_full, first + 2 * pair + 2))
        assert len(done) == len(units) - NB
        N_IN0, N_OUT0, N_OUT1, N_PROJ = 0, len(units_a), FIRST_STATE, len(done)
        N_GU0 = N_OUT0 + KD // 2
        N_DOWN0 = N_GU0 + FM
        N_IN1 = N_DOWN0 + 3 * KD // 2
        N_GU1 = N_OUT1 + CX // KD * KD // 2
        N_DOWN1 = N_GU1 + FM
        assert FM > 2 * KD and N_DOWN1 + 3 * KD // 2 == N_PROJ and N_IN1 + (CC + CX) // 2 == N_OUT1
        pool_units = range(N_IN1, N_IN1 + CC // 2)
        lo, n_lo, n_pool = [], 0, 0
        for i in range(N_PROJ):
            n_lo += 1
            first = (w_lo, n_lo)
            if i in pool_units:
                n_pool += 1
                lo.append((first, (w_lo_pool, n_pool)))
            else:
                n_lo += 1
                lo.append((first, (w_lo, n_lo)))
        part_of = [(i >= N_OUT0) + (i >= N_OUT1) for i in range(N_PROJ)]

        def halves(i):
            kb = units[unit_of[i]][1]
            return (slice(0, 4 * UC), slice(4 * UC, kb * UC))

        freed = [None] * len(units)
        for i in range(N_PROJ):
            freed[unit_of[i]] = lo[i]
        for b in range(NB):
            freed[FIRST_STATE + b] = ((st_out[(FIRST_STATE + b) % R], 16 * (b // R + 1)),)
        marks = {}

        @block.sync
        def _(sp):
            def load_units(lo, hi):
                for u in range(lo, hi):
                    src, kb = units[u]
                    if u >= R:
                        for wait in freed[u - R]:
                            sp.wait_ge(*wait)
                    dst = ring[:, u % R, :].rearrange("p (k n) -> p k n", n=src.shape[2])[:, 0:kb, :]
                    sp.dma_start(dst, src).then_inc(w_in[u % R], 16)

            def load_sequence(cache, b, wait, second=False):
                page = page_numbers(nc.sync.engine, b, 0, NPAGES)
                for s in range(KVS):
                    if cache is cache_k or s not in ACT_SLOTS:
                        wait(s)
                        for dst, src, arrived in load_block(cache, page[2 * s:2 * s + 2], s, second):
                            sp.dma_start(dst, src).then_inc(arrived, 16)

            sp.dma_start(pages[:, :], page_table.rearrange("b n -> (b n)").unsqueeze(0)).then_inc(ld_pages, 16)
            sp.dma_start(XIN[:, 0:2, :], x_prompt[0].rearrange("(t p) d -> p t d", p=P)).then_inc(ld_x, 16)
            sp.dma_start(XIN[0:NS, 2, :], x_sample.rearrange("b t d -> (b t) d")).then_inc(ld_x, 16)
            load_units(0, 2)
            sp.wait_ge(ld_par, 16 * 12)
            load_units(2, R)
            sp.wait_ge(ld_pages, 16)
            load_units(R, len(units_a))
            sp.wait_ge(tr_full, TR_KV)
            load_sequence(cache_k, 0, lambda s: None)
            with sp.Fori(0, NB - 1) as i:
                load_sequence(cache_k, i + 1, lambda s: sp.wait_ge(tr_full, i * 2 * NBLK + (TR_K + 2 * s + 2)))
            load_sequence(cache_v, 0, lambda s: sp.wait_ge(tr_full, (NB - 1) * 2 * NBLK + TR_K + 2 * s + 2))
            sp.wait_ge(*lo[len(units_a) - 1][1])
            load_sequence(cache_v, 1, lambda s: None, second=True)
            with sp.Fori(0, (NB - 4) // 2) as i:
                load_sequence(cache_v, i * 2 + 2, lambda s: sp.wait_ge(v_used, i * 2 * NBLK + (s + 1)))
                load_sequence(cache_v, i * 2 + 3, lambda s: sp.wait_ge(v_used, i * 2 * NBLK + (NBLK + s + 1)), second=True)
            load_sequence(cache_v, NB - 2, lambda s: sp.wait_ge(v_used, (NB - 4) * NBLK + s + 1))
            sp.wait_ge(v_used, (NB - 2) * NBLK)
            load_units(len(units_a), len(units_a) + 2)
            load_sequence(cache_v, NB - 1, lambda s: sp.wait_ge(v_used, (NB - 2) * NBLK + s + 1))
            load_units(len(units_a) + 2, len(units))

            for t in range(3):
                sp.wait_ge(tr_act, (TR_Y + 2 * t + 2) // 2)
                sp.wait_ge(tr_dve, (TR_Y + 2 * t + 2) // 2)
                dst = y_prompt[0, t * P:(t + 1) * P, :] if t < 2 else y_sample.rearrange("b t d -> (b t) d")
                sp.dma_start(dst, YT[0:P if t < 2 else NS, t, :]).then_inc(y_stored, 16)
            sp.wait_ge(y_stored, 3 * 16)

        @block.gpsimd
        def _(pool):
            n = [0]

            def step(ins):
                n[0] += 1
                ins.then_inc(consts, 1)
                pool.wait_ge(consts, n[0])

            step(pool.memset(ident[:, :], 0.0))
            step(pool.affine_select(out=ident[:, :], in_=ident[:, :], compare_op=ALU.not_equal, fill=1.0,
                                    base=0, pattern=[[-1, P]], channel_multiplier=1))
            step(pool.memset(ones[:, :], 1.0))
            step(pool.memset(eps[:, :], 1e-6))
            step(pool.memset(tri3[:, :, :], 0.0))
            for i in (0, 2):
                step(pool.affine_select(out=tri3[:, i, :], in_=tri3[:, i, :], compare_op=ALU.is_ge, fill=NEG,
                                        base=0, pattern=[[-1, P]], channel_multiplier=1))
            step(pool.memset(trilT[:, :], 1.0))
            step(pool.affine_select(out=trilT[:, :], in_=trilT[:, :], compare_op=ALU.is_ge, fill=0.0,
                                    base=0, pattern=[[1, P]], channel_multiplier=-1))

            def own_columns(t, fill, mid):
                step(pool.affine_select(out=t, in_=t, compare_op=ALU.is_ge, fill=fill,
                                        base=0, pattern=[[-T, NB]] + mid + [[0, T]], channel_multiplier=1))
                step(pool.affine_select(out=t, in_=t, compare_op=ALU.is_ge, fill=fill,
                                        base=0, pattern=[[T, NB]] + mid + [[1, T]], channel_multiplier=-1))

            step(pool.memset(bd01[:, :], 1.0))
            own_columns(bd01[:, :].rearrange("p (b t) -> p b t", t=T), 0.0, [])
            step(pool.memset(own_all[:, :, :], NEG))
            for s in range(2):
                part = own_all[:, :, s * QT // 2:(s + 1) * QT // 2].rearrange("p k (a t) -> p k a t", t=T)
                step(pool.affine_select(out=part, in_=part, compare_op=ALU.not_equal, fill=0.0, base=-3 * T * s,
                                        pattern=[[0, T], [-4 * T, H // 2], [-1, T]], channel_multiplier=1))
                step(pool.affine_select(out=part, in_=part, compare_op=ALU.is_ge, fill=NEG, base=0,
                                        pattern=[[-1, T], [0, H // 2], [1, T]], channel_multiplier=0))
            marks["own"] = n[0]
            step(pool.memset(same[:, :, :], 0.0))
            for first in range(2):
                for second in range(2):
                    part = same[:, first, second * 2 * QT:(second + 1) * 2 * QT].rearrange("p (h j t) -> p h j t", j=2, t=T)
                    for j in range(2):
                        step(pool.affine_select(out=part, in_=part, compare_op=ALU.not_equal, fill=1.0,
                                                base=-first * 2 * QT - j * T,
                                                pattern=[[-2 * T, H], [0, 2], [-1, T]], channel_multiplier=1))
            marks["same"] = n[0]
            step(pool.memset(bmask01[:, :], 1.0))
            step(pool.affine_select(out=bmask01[:, :], in_=bmask01[:, :], compare_op=ALU.is_ge, fill=0.0,
                                    base=0, pattern=[[-T, NB]], channel_multiplier=1))
            step(pool.affine_select(out=bmask01[:, :], in_=bmask01[:, :], compare_op=ALU.is_ge, fill=0.0,
                                    base=T - 1, pattern=[[T, NB]], channel_multiplier=-1))
            step(pool.memset(tie[:, :, :], 1.0))
            step(pool.affine_select(out=tie[:, :, :], in_=tie[:, :, :], compare_op=ALU.is_gt, fill=0.0,
                                    base=0, pattern=[[1, NBLK], [-1, NBLK]], channel_multiplier=0))
            step(pool.memset(sel[:, :], 0.0))
            for g in range(4):
                step(pool.affine_select(out=sel[:, :], in_=sel[:, :], compare_op=ALU.not_equal, fill=1.0,
                                        base=-QT * g, pattern=[[-1, QT]], channel_multiplier=1))
            pool.memset(QZ[:, :, :, :], 0.0)
            pool.memset(KNZ[:, :, :], 0.0)
            pool.memset(ext[:, :, 0:3], 0.0).then_inc(zeroed, 1)
            pool.wait_ge(acc_full, M_IN0)
            pool.memset(VTOK[:, :, :], 0.0)
            pool.memset(POWN[:, :], 0.0)
            pool.memset(CUP[:, :, 0:2], 0.0).then_inc(zeroed, 1)

            stores = [0]

            def store(dst, src, s=stored):
                pool.dma_start(dst, src).then_inc(s, 16)
                if s is stored:
                    stores[0] += 1

            pool.wait_ge(tr_act, TR_K // 2)
            pool.wait_ge(tr_dve, TR_K // 2)
            for buf, prompt, sample in ((KOUT, k_prompt, k_sample), (VTOK, v_prompt, v_sample)):
                for t in range(NP // PAGE):
                    store(prompt[0, t].rearrange("h q d -> q h d"),
                          buf[:, t, :].rearrange("p (h d) -> p h d", d=DH), kv_stored)
                for b in range(NB):
                    store(sample[b].rearrange("h t d -> t h d"),
                          buf[b * T:(b + 1) * T, 2, :].rearrange("p (h d) -> p h d", d=DH), kv_stored)
            marks["kv_stored"] = 16 * 2 * (NP // PAGE + NB)
            pool.wait_ge(tr_act, (TR_COA + 2) // 2)
            pool.wait_ge(tr_dve, (TR_COA + 2) // 2)
            store(conv_a_prompt[0], coT_a[0:2, :])
            store(conv_a_sample.rearrange("b j c -> (b j) c"), coT_a[2:2 + 2 * NB, :])

            for i in pool_units:
                half = halves(i)[1]
                pool.wait_ge(w_hi, 2 * i + 2)
                if i - 2 >= pool_units[0] - 2:
                    pool.wait_ge(*done[i - 2])
                w = WHL[part_of[i]]
                pool.tensor_tensor(w[:, i % 2, 1, half], ring[:, unit_of[i] % R, half], w[:, i % 2, 0, half],
                                   ALU.subtract).then_inc(w_lo_pool, 1)

            pool.wait_ge(acc_full, ACC_SSD)
            step(pool.memset(E2[0:SH, :, :], 0.0))
            step(pool.affine_select(out=E2[0:SH, :, :].rearrange("p k (q r) -> p k q r", q=2),
                                    in_=E2[0:SH, :, :].rearrange("p k (q r) -> p k q r", q=2),
                                    compare_op=ALU.not_equal, fill=1.0, base=0,
                                    pattern=[[-2, CX], [-1, 2], [0, DH]], channel_multiplier=1))
            marks["e2"] = n[0]
            step(pool.memset(CBM[:, :, NP:NT], 0.0))
            step(pool.memset(SEG[:, :, NP:NT], 0.0))
            marks["seg"] = n[0]
            for b in range(NB):
                pool.wait_ge(st_made, b + 1)
                u = FIRST_STATE + b
                store(ssm_sample[b].rearrange("(k q) p n -> (q p) k n", q=2),
                      ring[:, u % R, :].rearrange("p (k n) -> p k n", n=NST), st_out[u % R])
            pool.wait_ge(tr_act, (TR_Y) // 2)
            pool.wait_ge(tr_dve, (TR_Y) // 2)
            store(conv_ssm_prompt[0], CO1T[CQ:CQ + 3, :])
            store(conv_ssm_sample.rearrange("b j c -> (b j) c"), CO1T[CQ + 3:CQ + 3 + 3 * NB, :])
            for g in range(G):
                pool.wait_ge(stp_made, g + 1)
                store(ssm_prompt[0, g * HG:(g + 1) * HG].rearrange("(k q) p n -> (q p) k n", q=2), STP, stp_out)
            pool.wait_ge(stored, 16 * stores[0])
            pool.wait_ge(kv_stored, marks["kv_stored"])
            for b in range(NB):
                pool.wait_ge(st_out[(FIRST_STATE + b) % R], 16 * (b // R + 1))
            pool.wait_ge(stp_out, 16 * G)

        @block.tensor
        def _(pe):
            n_acc = [0]
            n_sq = [0]
            n_norm = [0]

            def acc_open():
                n = n_acc[0]
                n_acc[0] += 1
                if n >= 4:
                    pe.wait_ge(acc_free, n - 3)
                return acc[n % 4]

            def tr_open(n):
                if n >= 2:
                    pe.wait_ge(tr_act if n % 2 == 0 else tr_dve, n // 2)
                return trb[n % 2]

            def weights(u):
                pe.wait_ge(w_in[u % R], 16 * (u // R + 1))
                return ring[:, u % R, :]

            def sum_square(last_of):
                count, total = last_of
                if count == 0 and n_norm[0] >= 1:
                    pe.wait_ge(rt_made, n_norm[0])
                pe.wait_ge(sq_made, n_sq[0] + 1)
                pe.matmul(stat[:, 0:NT], ones[:, :], SQ[:, n_sq[0] % 4, :],
                          start=(count == 0), stop=(count == total - 1)).then_inc(sq_used, 1)
                n_sq[0] += 1
                if count == total - 1:
                    n_norm[0] += 1

            def project(i, tiles, kdim, rhs, ready, after=None):
                kparts = -(-kdim // KD)
                for pair in range(tiles // 2):
                    banks = [acc_open(), acc_open()]
                    for part in range(kparts):
                        w = WHL[part_of[i]][:, i % 2, :, :]
                        ks = range(part * KD, min(part * KD + KD, kdim))
                        for tile, k in ([(t, k) for k in ks for t in range(2)] if pair == 0 else
                                        [(t, k) for t in range(2) for k in ks]):
                            if tile == 0 and k % 4 == 0:
                                pe.wait_ge(*lo[i][k % KD // 4])
                            if pair == 0 and tile == 0:
                                ready(k)
                            at = (k - part * KD) * UC + tile * P
                            out = banks[tile][:, 0:NT]
                            pe.matmul(out, w[:, 0, at:at + P], rhs[:, k, 0, :], start=(k == 0), stop=False)
                            pe.matmul(out, w[:, 0, at:at + P], rhs[:, k, 1, :], start=False, stop=False)
                            last = pe.matmul(out, w[:, 1, at:at + P], rhs[:, k, 0, :], start=False, stop=(k == kdim - 1))
                            if k == kdim - 1:
                                last.then_inc(acc_full, 1)
                        if part < kparts - 1:
                            last.then_inc(w_used, 1)
                        i += 1
                    if after:
                        after(pair)
                return i

            def hx_ready(base):
                return lambda k: pe.wait_ge(hx_made, base + k + 1)

            def out_project(i, kdim, rhs, ready):
                done = [0]

                def squares(pair):
                    for _ in range(0 if pair == 0 else 2):
                        sum_square((done[0], KD))
                        done[0] += 1

                project(i, KD, kdim, rhs, ready, after=squares)
                while done[0] < KD:
                    squares(1)

            pe.sem_inc(kt_used, 2)
            pe.wait_ge(consts, 2)
            pe.wait_ge(ld_x, 32)
            for k in range(KD):
                bank = tr_open(TR_X + k)
                for t in range(3):
                    rows = P if t < 2 else NS
                    last = pe.transpose(bank[:, t * P:t * P + rows], XIN[0:rows, t, k * P:(k + 1) * P], ident[0:rows, 0:rows])
                last.then_inc(tr_full, 1)
            pe.wait_ge(ld_par, 16 * 12)
            for i, rows in enumerate((N_PAR0, 4 * CC)):
                pe.transpose(tr_open(TR_PAR + i)[:, 0:rows], PARIN[0:rows, i, :], ident[0:rows, 0:rows]).then_inc(tr_full, 1)
            def turn_histories():
                pe.wait_ge(ld_hist, 32)
                bank = tr_open(TR_HIST)
                for c in range(CA):
                    last = pe.transpose(bank[:, c * 2 * NB:(c + 1) * 2 * NB], HISTA_IN[0:2 * NB, c * P:(c + 1) * P], ident[0:2 * NB, 0:2 * NB])
                last.then_inc(tr_full, 1)
                for i in range(3):
                    bank = tr_open(TR_HIST + 1 + i)
                    for c in range(CC // 3):
                        cc = i * (CC // 3) + c
                        last = pe.transpose(bank[:, c * 3 * NB:(c + 1) * 3 * NB], HISTS_IN[0:3 * NB, cc * P:(cc + 1) * P], ident[0:3 * NB, 0:3 * NB])
                    last.then_inc(tr_full, 1)

            def ffn_square(pair):
                if pair == 0:
                    for k in range(KD):
                        sum_square((k, KD))

            def after_first(pair):
                ffn_square(pair)
                if pair == 1:
                    turn_histories()

            pe.wait_ge(consts, 3)
            project(N_IN0, M_IN0, KD, HX0, hx_ready(0), after=after_first)
            for i, m in enumerate((MK, MV)):
                for t in range(3):
                    rows = P if t < 2 else NS
                    bank = tr_open(TR_KV + 3 * i + t)
                    for c in range(H * DH // P):
                        last = pe.transpose(bank[0:rows, c * P:(c + 1) * P], BIG[:, m + c, t * P:t * P + rows], ident[:, :])
                    last.then_inc(tr_full, 1)

            def k_phase():
                def k_step(i, p, last=False):

                    def turn(p, bp, q):
                        s = 2 * p + bp
                        if q == 0:
                            pe.wait_ge(kv_in[s % KVS], i * 64 + 32 * (s // KVS + 1))
                        pe.wait_ge(tr_dve if q else tr_act, i * 2 * KVS + (TR_K // 2 + s))
                        for hh in range(4):
                            last = pe.transpose(trb[q][:, hh * P:(hh + 1) * P],
                                                kv[:, s % KVS, 4 * q + hh, :, :].rearrange("p j d -> p (j d)"), ident[:, :])
                        last.then_inc(tr_full, 1)

                    def scores(p, hh):
                        e, pair = p // 4, p % 4
                        if hh == 0:
                            if pair == 0:
                                pe.wait_ge(qz_made, i * 2 + (e + 1))
                                pe.wait_ge(s_free, i * 2 + (e + 1))
                            pe.wait_ge(tr_act, i * 2 * KVS + (TR_K // 2 + 2 * p + 2))
                            pe.wait_ge(tr_dve, i * 2 * KVS + (TR_K // 2 + 2 * p + 2))
                        if pair == 3:
                            for q in range(2):
                                pe.matmul(acc[e][q * QT:(q + 1) * QT, 0:T], QZ[:, e, q, hh * QT:(hh + 1) * QT],
                                          KNE[:, e, 4 * q + hh, :], start=(hh == 0), stop=(hh == 3))
                        for bp in range(2):
                            for q in range(2):
                                g = 2 * bp + q
                                last = pe.matmul(scb[e][g * QT:(g + 1) * QT, pair * P:(pair + 1) * P],
                                                 QZ[:, e, q, hh * QT:(hh + 1) * QT],
                                                 KTB[p % 2][:, bp, q, hh * P:(hh + 1) * P],
                                                 start=(hh == 0), stop=(hh == 3))
                        if hh == 3:
                            last.then_inc(kt_used, 1)

                    for part in ("T00", "T01", "S0", "T10", "S1", "T11", "S2", "S3"):
                        if part[0] == "T" and not (last and p == KVS):
                            turn(p, int(part[1]), int(part[2]))
                        if part[0] == "S" and p > 0:
                            scores(p - 1, int(part[1]))

                k_step(0, 0)
                with pe.Fori(0, NB // 2 - 1) as i:
                    for p in range(1, KVS + 1):
                        k_step(i, p)
                for p in range(1, KVS + 1):
                    k_step(NB // 2 - 1, p, last=True)

            def same_rows(first, src, bank, cols, start=True, stop=True):
                return pe.matmul(bank[:, cols], same[:, first, :], src, start=start, stop=stop)

            def gate():
                pe.wait_ge(consts, marks["same"])
                pe.wait_ge(d_step, 1)
                bank = acc_open()
                n = NB * NBLK // 2
                for first in range(2):
                    last = same_rows(first, SM[:, 0, :], bank, slice(first * n, (first + 1) * n))
                last.then_inc(acc_full, 1)

            def turn_max():
                pe.wait_ge(d_step, 2)
                pe.transpose(acc_open()[0:NB, 0:P], SM[:, 3, 0:NB], ident[:, :]).then_inc(acc_full, 1)

            def return_max():
                pe.wait_ge(d_step, 3)
                pe.transpose(acc_open()[:, 0:NB], RMT[:, 2, :], ident[0:NB, 0:NB]).then_inc(acc_full, 1)

            def denominators(part):
                pe.wait_ge(d_step, 5 + part)
                bank = acc_open()
                cols = PARTS[part]
                same_rows(0, SM[:, 6, cols], bank, cols, stop=False)
                same_rows(1, SM[:, 6, cols], bank, cols, start=False).then_inc(acc_full, 1)

            def turn_own():
                pe.wait_ge(d_step, 7)
                pe.transpose(acc_open()[0:NS, 0:2 * QT], SM[0:2 * QT, 9, :], ident[0:2 * QT, 0:2 * QT]).then_inc(acc_full, 1)

            def turn_sample(b):
                pe.wait_ge(dg_made, b + 1)
                bank = tr_open(TR_P["sample", b])
                for m in range(NBLK // 2):
                    last = pe.matmul(bank[:, m * P:(m + 1) * P], S[:, b, m, :], DG[:, b % 2, :], start=True, stop=True)
                last.then_inc(tr_full, 1)

            def prompt_scores(h):
                rows = slice((h % 2) * DH, (h % 2 + 1) * DH)
                q, k = BIG[rows, MQ + h // 2, :], BIG[rows, MK + h // 2, :]
                bank = acc_open()
                pe.matmul(bank[:, 0:P], q[:, 0:P], k[:, 0:P], start=True, stop=True)
                pe.matmul(bank[:, P:3 * P], q[:, P:2 * P], k[:, 0:2 * P], start=True, stop=True).then_inc(acc_full, 1)

            def prompt_turn(h):
                pe.wait_ge(pp_made, h + 1)
                bank = tr_open(TR_P["prompt", h])
                for i in range(3):
                    last = pe.transpose(bank[:, i * P:(i + 1) * P], SP[:, h % 2, i * P:(i + 1) * P], ident[:, :])
                last.then_inc(tr_full, 1)

            def prompt_values(h):
                n = TR_P["prompt", h]
                pe.wait_ge(tr_act if n % 2 == 0 else tr_dve, n // 2 + 1)
                rows = slice((h % 2) * DH, (h % 2 + 1) * DH)
                cols = slice(h * DH, (h + 1) * DH)
                bank = acc_open()
                marks["pv", h] = n_acc[0]
                pe.matmul(bank[rows, 0:P], VTOK[:, 0, cols], PT[:, h % 2, 0:P], start=True, stop=True)
                pe.matmul(bank[rows, P:2 * P], VTOK[:, 0, cols], PT[:, h % 2, P:2 * P], start=True, stop=False)
                pe.matmul(bank[rows, P:2 * P], VTOK[:, 1, cols], PT[:, h % 2, 2 * P:3 * P], start=False,
                          stop=True).then_inc(acc_full, 1)

            def prompt_step(i):
                if i < H:
                    prompt_scores(i)
                if 1 <= i <= H:
                    prompt_turn(i - 1)
                if 2 <= i:
                    prompt_values(i - 2)

            pe.wait_ge(rt_made, 1)
            k_phase()
            gate()
            turn_max()
            return_max()
            denominators(0)

            def values(b):
                bank = scb[b % 2]
                n = TR_P["sample", b]
                pe.wait_ge(tr_act if n % 2 == 0 else tr_dve, n // 2 + 1)
                if b >= 2:
                    pe.wait_ge(o_copied, b - 1)
                for i in range(2 * NBLK):
                    blk, j = i // 2, i % 2
                    s = blk
                    if j == 0:
                        pe.wait_ge((kv2_in if IN_KV2[b] else kv_in)[s], ARRIVALS[b])
                    g = i % 4
                    last = pe.matmul(bank[g * QT:(g + 1) * QT, :], S[:, b, i // 4, g * QT:(g + 1) * QT],
                                     (kv2 if IN_KV2[b] else kv)[:, s, :, j, :],
                                     start=(i < 4), stop=(i >= 2 * NBLK - 4 and g != 0))
                    if j == 1:
                        last.then_inc(v_used, 1)
                if b == 0:
                    denominators(1)
                    turn_own()
                    pe.wait_ge(d_step, 8)
                pe.matmul(bank[0:QT, :], POWN[:, b * QT:(b + 1) * QT], VTOK[:, 2, :],
                          start=False, stop=True).then_inc(o_full, 1)

            def turn_values(b):
                pe.wait_ge(o_copied, b + 1)
                bank = acc_open()
                marks["o", b] = n_acc[0]
                for h in range(H):
                    last = pe.matmul(bank[(h % 2) * DH:(h % 2 + 1) * DH, (h // 2) * T:(h // 2 + 1) * T],
                                     OSB[:, b % 2, h * DH:(h + 1) * DH], sel[:, h * T:(h + 1) * T], start=True, stop=True)
                last.then_inc(acc_full, 1)

            turn_sample(0)
            turn_sample(1)
            for b in range(NB):
                if 1 <= b < NB - 1:
                    turn_sample(b + 1)
                if b:
                    prompt_step(b)
                values(b)
                if b == 0:
                    prompt_step(0)
                else:
                    turn_values(b - 1)
            prompt_step(NB)
            turn_values(NB - 1)
            prompt_step(NB + 1)

            pe.wait_ge(mix_made, 1)
            for i in range(2):
                bank = tr_open(TR_COA + i)
                for c in range(CA // 2):
                    last = pe.transpose(bank[0:2 + 2 * NB, c * P:(c + 1) * P], co_a[:, i * (CA // 2) + c, :], ident[:, :])
                last.then_inc(tr_full, 1)

            assert n_acc[0] == ACC_OUT0
            out_project(N_OUT0, KD, HX1, hx_ready(KD))

            def ffn(i, hx, base, hid, hid_base):
                project(i, 2 * FM, KD, hx, hx_ready(base), after=ffn_square)
                out_project(i + FM, FM, hid, lambda k: pe.wait_ge(hid_made, hid_base + k + 1))

            ffn(N_GU0, HX1, 2 * KD, HID[0], 0)

            project(N_IN1, CC, KD, HX1, hx_ready(3 * KD), after=ffn_square)
            bank = acc_open()
            pe.wait_ge(ld_head, 64)
            for k in range(KD):
                for r in range(2):
                    last = pe.matmul(bank[0:SH, 0:NT], wdt[:, k, :], HX1[:, k, r, :].bitcast(F32),
                                     start=(k == 0 and r == 0), stop=(k == KD - 1 and r == 1))
            last.then_inc(acc_full, 1)
            project(N_IN1 + CC // 2, CX, KD, HX1, lambda k: None)
            assert n_acc[0] == ACC_SSD

            pe.wait_ge(hs_made, 1)
            bank = acc_open()
            for t in range(3):
                rows = P if t < 2 else NS
                last = pe.transpose(bank[0:rows, t * P:(t + 1) * P], hs[:, t * P:t * P + rows], ident[:, :])
            last.then_inc(acc_full, 1)
            pe.wait_ge(xc_made, CC + 1)
            for t in range(3):
                rows = P if t < 2 else NS
                bank = acc_open()
                for g in range(G):
                    last = pe.transpose(bank[0:rows, g * NST:(g + 1) * NST], XBC[:, CX + g, t * P:t * P + rows], ident[:, :])
                last.then_inc(acc_full, 1)
            for g in range(G):
                bank = acc_open()
                for t in range(3):
                    rows = P if t < 2 else NS
                    cols = slice(t * P, t * P + rows)
                    last = pe.matmul(bank[0:rows, cols], XBC[:, CX + g, cols], XBC[:, CX + G + g, cols], start=True, stop=True)
                last.then_inc(acc_full, 1)
            bank = acc_open()
            pe.wait_ge(consts, marks["e2"])
            for k in range(CX):
                last = pe.matmul(bank[:, k * (NB + 1):(k + 1) * (NB + 1)], E2[0:SH, k, :], decin[:, :], start=True, stop=True)
            last.then_inc(acc_full, 1)
            for g in range(G):
                bank = acc_open()
                for c in range(PG):
                    last = pe.transpose(bank[0:NS, c * P:(c + 1) * P], XBC[:, g * PG + c, NP:NT], ident[:, :])
                last.then_inc(acc_full, 1)

            def turn_state(b, q):
                st = weights(FIRST_STATE + b)
                bank = tr_open(TR_ST + b * G + q)
                for hh in range(PG):
                    last = pe.transpose(bank[:, hh * P:(hh + 1) * P], st[:, (q * PG + hh) * NST:(q * PG + hh + 1) * NST], ident[:, :])
                last.then_inc(tr_full, 1)

            def new_state(b, q):
                bank = acc_open()
                for hh in range(PG):
                    k = q * PG + hh
                    last = pe.matmul(bank[:, hh * NST:(hh + 1) * NST], XWS[Q1, k * P:(k + 1) * P],
                                     BMASK[Q1, q, b, :], start=True, stop=True)
                last.then_inc(acc_full, 1)

            def from_state(b):
                n = TR_ST + (b + 1) * G
                pe.wait_ge(tr_act, n // 2)
                pe.wait_ge(tr_dve, n // 2)
                pe.wait_ge(o_copied, NB + b - 1)
                for q in range(G):
                    last = pe.matmul(scb[b % 2][q * NS:(q + 1) * NS, :], XBC[:, CX + G + q, NP:NT], S0T[b % 2][:, q, :],
                                     start=True, stop=True)
                last.then_inc(o_full, 1)

            def turn_from_state(b):
                pe.wait_ge(o_copied, NB + b + 1)
                bank = acc_open()
                own = ident[:, :].rearrange("p (g n) -> p g n", n=NS)[:, :, b * T:(b + 1) * T]
                for c in range(PG):
                    last = pe.matmul(bank[:, c * G * T:(c + 1) * G * T].rearrange("p (g t) -> p g t", t=T),
                                     YSB[:, b % 2, c * P:(c + 1) * P], own, start=True, stop=True)
                last.then_inc(acc_full, 1)
                marks["ysb", b] = n_acc[0]

            for q in range(G):
                turn_state(0, q)
            pe.wait_ge(bt_made, 2)
            pe.wait_ge(bmask_made, 1)
            for _ in range(WARM):
                pe.matmul(scb[0][:, 0:3 * P], ones[:, :], tri3[:, :, :].rearrange("p a b -> p (a b)"), start=True, stop=True)
            for b in range(NB):
                for q in range(G):
                    if q == 3:
                        turn_from_state(b)
                    new_state(b, q)
                    if b + 1 < NB:
                        turn_state(b + 1, q)
                    if q == 1:
                        from_state(b)

            pe.wait_ge(co_made, 1)
            for i in range(CC // 4):
                bank = tr_open(TR_CO + i)
                for c in range(4):
                    last = pe.transpose(bank[0:3 + 3 * NB, c * P:(c + 1) * P], co_s[:, 4 * i + c, :], ident[:, :])
                last.then_inc(tr_full, 1)

            def turn_x(g):
                for t in range(2):
                    bank = acc_open()
                    for c in range(PG):
                        last = pe.transpose(bank[:, c * P:(c + 1) * P], XBC[:, g * PG + c, t * P:(t + 1) * P], ident[:, :])
                    last.then_inc(acc_full, 1)

            def prompt_states(g):
                pe.wait_ge(g_made, g + 1)
                gp = g % 2
                bank = acc_open()
                pe.matmul(bank[:, :], BT[:, 0, g * NST:(g + 1) * NST], XW1[:, gp, 0, :], start=True, stop=True).then_inc(acc_full, 1)
                bank = acc_open()
                for c in range(PG):
                    cols = slice(c * P, (c + 1) * P)
                    pe.matmul(bank[:, cols], XW0[:, cols], BT[:, 0, g * NST:(g + 1) * NST], start=True, stop=False)
                    last = pe.matmul(bank[:, cols], XW1[:, gp, 1, cols], BT[:, 1, g * NST:(g + 1) * NST], start=False, stop=True)
                last.then_inc(acc_full, 1)

            turn_x(0)
            prompt_states(0)
            for g in range(G):
                gp = g % 2
                for hh in range(HG):
                    h = g * HG + hh
                    pe.matmul(acc_open()[:, 0:NT], ident[0:SH, h:h + 1].to_broadcast([SH, P]), hw[:, 0, :],
                              start=True, stop=True).then_inc(acc_full, 1)
                if g + 1 < G:
                    turn_x(g + 1)
                    prompt_states(g + 1)
                pe.wait_ge(seg_made, g + 1)
                pe.wait_ge(sent_made, g + 1)
                for c in range(PG):
                    k = g * PG + c
                    bank = acc_open()
                    for r in range(2):
                        hh = 2 * c + r
                        rows = slice(r * DH, (r + 1) * DH)
                        cols = slice(hh * DH, (hh + 1) * DH)
                        for t in range(2):
                            pe.matmul(bank[rows, t * P:(t + 1) * P], XDT[:, gp, t, cols], SEG[:, hh, t * P:(t + 1) * P], start=True, stop=True)
                        last = pe.matmul(bank[rows, NP:NT], XDS[0:NS, g * HG * DH + hh * DH:g * HG * DH + (hh + 1) * DH],
                                         SEG[0:NS, hh, NP:NT], start=True, stop=True)
                    last.then_inc(acc_full, 1)
                    bank = acc_open()
                    pe.matmul(bank[:, 0:P], SENT[gp][:, c * P:(c + 1) * P], XBC[:, CX + G + g, P:2 * P],
                              start=True, stop=True).then_inc(acc_full, 1)
                    bank = acc_open()
                    last = pe.matmul(bank[:, 0:NT - P], E2[0:SH, k, :], hw[:, 1, P:NT], start=True, stop=True)
                    last.then_inc(acc_full, 1)

                if g > 0:
                    for c in range(PG):
                        sum_square(((g - 1) * PG + c, CX))

            for c in range(PG):
                sum_square(((G - 1) * PG + c, CX))
            assert n_acc[0] == ACC_OUT1, (n_acc[0], ACC_OUT1)
            out_project(N_OUT1, CX, G1, hx_ready(4 * KD))
            ffn(N_GU1, G1, 4 * KD + CX, HID[1], FM)

            for t in range(3):
                rows = P if t < 2 else NS
                for i in range(2):
                    bank = tr_open(TR_Y + 2 * t + i)
                    for c in range(4):
                        k = 4 * i + c
                        pe.wait_ge(x_made, 3 * KD + k + 1)
                        last = pe.transpose(bank[0:rows, c * P:(c + 1) * P], X[:, k, t * P:t * P + rows], ident[:, :])
                    last.then_inc(tr_full, 1)

        @block.scalar
        def _(act):
            n_sq, n_rt, n_hx, chain = [0], [0], [0], [0]

            def link(ins):
                chain[0] += 1
                ins.then_inc(ach, 1)
                act.wait_ge(ach, chain[0])

            def square(src):
                n = n_sq[0]
                n_sq[0] += 1
                if n >= 4:
                    act.wait_ge(sq_used, n - 3)
                act.activation(SQ[:, n % 4, :], src, ACT.Square).then_inc(sq_made, 1)

            def root(total):
                act.wait_ge(sq_used, n_sq[0])
                if n_rt[0] >= 1:
                    act.wait_ge(r_made, n_rt[0])
                n_rt[0] += 1
                act.activation(RT[:, :], stat[:, 0:NT], ACT.Sqrt, bias=eps[:, :], scale=1.0 / total).then_inc(rt_made, 1)

            def scaled(hx, k, col):
                act.activation(hx[:, k, 0, :], X[:, k, :], ACT.Copy, scale=par[:, 0, col:col + 1]).then_inc(hx_hi, 1)

            def split(i):
                u = unit_of[i]
                act.wait_ge(w_in[u % R], 16 * (u // R + 1))
                if i >= 2 and part_of[i] == part_of[i - 2]:
                    act.wait_ge(*done[i - 2])
                for half in halves(i):
                    act.activation(WHL[part_of[i]][:, i % 2, 0, half], ring[:, u % R, half], ACT.Copy).then_inc(w_hi, 1)

            def next_split(i):
                if i + 2 < N_PROJ and part_of[i + 2] == part_of[i]:
                    split(i + 2)

            def copy_transposed(n, dst, src):
                act.wait_ge(tr_full, n + 1)
                act.activation(dst, src, ACT.Copy).then_inc(tr_act, 1)

            loads = []
            row = 0
            for w in (l0_norm_mix_pre, l0_norm_mix_post, l0_norm_ffn_pre, l0_norm_ffn_post,
                      l1_norm_mix_pre, l1_norm_mix_post, l1_norm_ffn_pre, l1_norm_ffn_post, l1_norm_gate):
                k = w.shape[0] // P
                loads.append((w.rearrange("(k p) -> k p", p=P), PARIN[row:row + k, 0, :], ld_par))
                row += k
            loads.append((l0_conv_w.rearrange("j (k p) -> (j k) p", p=P), PARIN[row:row + 3 * CA, 0, :], ld_par))
            loads.append((l1_conv_b.rearrange("(k p) -> k p", p=P), PARIN[row + 3 * CA:row + 3 * CA + CC, 0, :], ld_par))
            loads.append((l1_conv_w.rearrange("j (k p) -> (j k) p", p=P), PARIN[0:4 * CC, 1, :], ld_par))
            loads.append((state_conv_a.rearrange("b j c -> (b j) c"), HISTA_IN[0:2 * NB, :], ld_hist))
            loads.append((state_conv_ssm.rearrange("b j c -> (b j) c"), HISTS_IN[0:3 * NB, :], ld_hist))
            loads.append((l1_w_in[:, DI + CC * P:].rearrange("(k p) n -> p k n", p=P), wdt[:, :, :], ld_head))
            for i, v in enumerate((l1_dt_bias, l1_a_log, l1_d_skip)):
                loads.append((v.unsqueeze(1), hp3[:, i:i + 1], ld_head))
            for src, dst, s in loads:
                act.dma_start(dst, src).then_inc(s, 16)

            for k in range(0, KD, 2):
                copy_transposed(TR_X + k, X[:, k, :], trb[0][:, 0:NT])
            copy_transposed(TR_PAR, par[:, 0, 0:N_PAR0], trb[0][:, 0:N_PAR0])
            split(0)
            act.wait_ge(tr_act, TR_PAR // 2 + 1)
            act.wait_ge(tr_dve, KD // 2)
            act.wait_ge(consts, 4)
            for k in range(KD):
                scaled(HX0, k, PN["mix_pre0"] + k)
            split(1)
            for k in range(KD):
                square(X[:, k, :])
            root(D)
            for i in range(N_OUT0):
                next_split(i)
                if i == 1:
                    copy_transposed(TR_HIST, hista[:, :, :, :], trb[0][:, 0:CA * 2 * NB].rearrange("p (c b j) -> p c b j", b=NB, j=2))
                    n = 3 * NB * CC // 3
                    copy_transposed(TR_HIST + 2, hists[:, CC // 3:2 * CC // 3, :], trb[0][:, 0:n].rearrange("p (c j) -> p c j", j=3 * NB))

            for i, (dst, t) in enumerate(((KOUT, 0), (KOUT, 1), (KOUT, 2), (VTOK, 0), (VTOK, 1), (VTOK, 2))):
                if i % 2 == 0:
                    rows = P if t < 2 else NS
                    if i == 0:
                        act.wait_ge(zeroed, 2)
                    copy_transposed(TR_KV + i, dst[0:rows, t, :], trb[0][0:rows, :])

            def load(cache, b, s, second=False):
                page = page_numbers(nc.scalar.engine, b, 2 * s, 2)
                for dst, src, arrived in load_block(cache, page, s, second):
                    act.dma_start(dst, src).then_inc(arrived, 16)

            def k_copies(i, last=False):
                for s in range(2 * KVS):
                    act.wait_ge(kt_used, i * KVS + (s // 2 + 1))
                    act.wait_ge(tr_full, i * 4 * KVS + (TR_K + 2 * s + 1))
                    act.activation(KTB[s // 2 % 2][:, s % 2, 0, :], trb[0][:, :], ACT.Copy).then_inc(tr_act, 1)
                    if last and s - KVS in ACT_SLOTS:
                        act.wait_ge(tr_full, i * 4 * KVS + (TR_K + 2 * s + 2))
                        load(cache_v, 0, s % KVS)

            with act.Fori(0, NB // 2 - 1) as i:
                k_copies(i)
            act.wait_ge(ld_pages, 16)
            k_copies(NB // 2 - 1, last=True)
            act.wait_ge(*lo[len(units_a) - 1][1])
            for s in ACT_SLOTS:
                load(cache_v, 1, s, second=True)

            def prompt_exp(h):
                col = h * 12
                act.wait_ge(pp_ready, h + 1)
                act.activation(SP[:, h % 2, 0:P], SP[:, h % 2, 0:P], ACT.Exp, bias=small[:, col + 4:col + 5],
                               scale=SCALE, accum_out=small[:, col + 6:col + 7])
                act.activation(SP[:, h % 2, P:3 * P], SP[:, h % 2, P:3 * P], ACT.Exp, bias=small[:, col + 5:col + 6],
                               scale=SCALE, accum_out=small[:, col + 7:col + 8]).then_inc(pp_exp, 1)

            def prompt_step(i):
                if i < H:
                    prompt_exp(i)
                if 1 <= i <= H and TR_P["prompt", i - 1] % 2 == 0:
                    if i >= 3:
                        act.wait_ge(acc_full, marks["pv", i - 3])
                    copy_transposed(TR_P["prompt", i - 1], PT[:, (i - 1) % 2, :], trb[0][:, 0:3 * P])

            def sample_exp(b):
                for m in range(NBLK // 2):
                    at = b * NBLK // 2 + m
                    ins = act.activation(S[:, b, m, :], S[:, b, m, :], ACT.Exp, bias=SM[:, 4, at:at + 1], scale=SCALE,
                                         accum_out=SM[:, 5, at:at + 1])
                ins.then_inc(p_made, 1)

            def copy_sample(b):
                n = TR_P["sample", b]
                if n % 2 == 0:
                    act.wait_ge(tr_full, n + 1)
                    for j in range(2):
                        last = act.activation(by_token(b, j), from_rows(trb[0], j), ACT.Copy)
                    last.then_inc(tr_act, 1)

            def copy_output(b):
                act.wait_ge(o_full, b + 1)
                if b >= 2:
                    act.wait_ge(acc_full, marks["o", b - 2])
                act.activation(OSB[:, b % 2, :], scb[b % 2][:, :], ACT.Copy).then_inc(o_copied, 1)

            act.wait_ge(d_step, 4)
            own = SM[0:2 * QT, 8, :]
            act.activation(own, own, ACT.Exp, scale=SCALE).then_inc(p_made, 1)
            for b in range(NB):
                sample_exp(b)
                if b == 3:
                    copy_sample(0)
            copy_sample(1)
            prompt_step(0)
            for b in range(NB):
                if 1 <= b < NB - 1:
                    copy_sample(b + 1)
                if b:
                    prompt_step(b)
                after = {NB - 3: None, NB - 2: NB - 1, NB - 1: None}.get(b, b + 2)
                for s in ACT_SLOTS:
                    if after is not None:
                        act.wait_ge(v_used, b * NBLK + s + 1)
                        load(cache_v, after, s, IN_KV2[after])
                copy_output(b)
            prompt_step(NB)
            copy_transposed(TR_COA, coT_a[0:2 + 2 * NB, 0:2 * P], trb[0][0:2 + 2 * NB, 0:2 * P])
            prompt_step(NB + 1)
            def post_norm(i, first_acc, kparts):
                act.activation(root_of_eps[:, :], eps[:, :], ACT.Sqrt)
                for k in range(0, KD, 2):
                    for _ in range(kparts if k < KD - 2 else kparts - 1):
                        next_split(i)
                        i += 1
                    for r in range(2):
                        act.wait_ge(acc_free, first_acc + k + r + 1)
                        square(Y[:, k + r, :])
                root(D)
                next_split(i)

            def pre_norm(hx, col, x_base):
                for k in range(KD):
                    act.wait_ge(x_made, x_base + k + 1)
                    scaled(hx, k, col + k)
                for k in range(KD):
                    square(X[:, k, :])
                root(D)

            def hiddens(layer, i, first_acc):
                for pair in range(FM // 2):
                    next_split(i + 2 * pair)
                    for r in range(2):
                        act.wait_ge(acc_free, first_acc + 4 * pair + r + 1)
                        act.activation(GS[layer][:, r, :], GS[layer][:, r, :], ACT.Silu).then_inc(hid_silu, 1)
                    next_split(i + 2 * pair + 1)
                    for r in range(2):
                        m = 2 * pair + r
                        act.wait_ge(ht_made, layer * FM + m + 1)
                        if layer == 0 and pair == 0:
                            act.wait_ge(kv_stored, marks["kv_stored"])
                        act.activation(HID[layer][:, m, 0, :], HT[layer][:, r, :], ACT.Copy).then_inc(hid_hi, 1)

            act.wait_ge(mix_made, 2)
            for k in range(KD):
                act.activation(HX1[:, k, 0, :], MIX[:, k, :], ACT.Copy).then_inc(hx_hi, 1)
            split(N_OUT0)
            split(N_OUT0 + 1)
            post_norm(N_OUT0, ACC_OUT0, 1)
            pre_norm(HX1, PN["ffn_pre0"], 0)
            hiddens(0, N_GU0, ACC_GU0)
            post_norm(N_DOWN0, ACC_DOWN0, 3)
            pre_norm(HX1, PN["mix_pre1"], KD)
            for c in range(CC):
                if c % 2 == 0:
                    next_split(N_IN1 + c // 2)
                act.wait_ge(cv_made, c + 1)
                act.activation(XBC[:, c, 0:NP], XBC[:, c, 0:NP], ACT.Silu, bias=par[:, 0, PCB + c:PCB + c + 1]).then_inc(xc_made, 1)

            def dt_function(step, dst, src, func, scale=1.0):
                act.wait_ge(dt_step, step)
                act.activation(dst, src, func, scale=scale).then_inc(dt_act, 1)

            act.wait_ge(ld_head, 64)
            for m in range(CX):
                if m % 2 == 0:
                    next_split(N_IN1 + (CC + m) // 2)
                if m == 1:
                    dt_function(1, hw[:, 5, :], hw[:, 4, :], ACT.Exp, -1.0)
                    dt_function(1, hp3[:, 1:2], hp3[:, 1:2], ACT.Exp)
                if m == 3:
                    dt_function(2, hw[:, 0, :], hw[:, 4, :], ACT.Ln)
                if m == 5:
                    dt_function(3, hw[:, 1, :], hw[:, 0, :], ACT.Exp)
                    dt_function(3, hw[:, 5, :], hw[:, 4, :], ACT.Exp)
            act.wait_ge(cv_made, CC + 1)
            new = XBC[:, :, NP:NT]
            act.activation(new, new, ACT.Silu).then_inc(xc_made, 1)
            for m in range(0, CX, 4):
                act.wait_ge(acc_free, ACC_Z + m + 4)
                act.activation(ZS[:, m:m + 4, :], ZS[:, m:m + 4, :], ACT.Silu).then_inc(zs_made, 1)

            act.wait_ge(bt_made, 1)
            for b in range(NB):
                last = act.activation(BMASK[Q1, :, b, :], BT[0:NS, 2, :].rearrange("p (g n) -> p g n", n=NST), ACT.Copy,
                                      scale=bmask01[:, b:b + 1])
            last.then_inc(bmask_made, 1)

            for b in range(NB + 1):
                for q in (0, 2):
                    if q == 2 and b:
                        act.wait_ge(o_full, NB + b)
                        if b >= 3:
                            act.wait_ge(acc_full, marks["ysb", b - 3])
                        act.activation(YSB[:, (b - 1) % 2, :], scb[(b - 1) % 2][:, :], ACT.Copy).then_inc(o_copied, 1)
                    if b < NB:
                        if b >= 2:
                            act.wait_ge(o_full, NB + b - 1)
                        copy_transposed(TR_ST + b * G + q, S0T[b % 2][:, q, :], trb[0][:, :])
            for i in range(0, CC // 4, 2):
                copy_transposed(TR_CO + i, CO1T[CQ:CQ + 3 + 3 * NB, i * 4 * P:(i + 1) * 4 * P], trb[0][0:3 + 3 * NB, :])
            for g in range(G):
                act.wait_ge(seg_in, g + 1)
                act.activation(SEG[:, :, :], SEG[:, :, :], ACT.Exp).then_inc(seg_exp, 1)
                for c in range(PG):
                    k = g * PG + c
                    act.wait_ge(gy_made, k + 1)
                    square(XBC[:, k, :])
                    act.activation(XBC[:, k, :], XBC[:, k, :], ACT.Copy, scale=par[:, 0, PGATE + k:PGATE + k + 1]).then_inc(g_scaled, 1)
            act.wait_ge(stp_out, 16 * G)
            for k in range(CX):
                act.wait_ge(g_scaled, k + 1)
                act.activation(G1[:, k, 0, :], XBC[:, k, :], ACT.Copy).then_inc(hx_hi, 1)
                if k == 0:
                    split(N_OUT1)
                    split(N_OUT1 + 1)
            root(DI)
            post_norm(N_OUT1, ACC_OUT1, CX // KD)
            pre_norm(G1, PN["ffn_pre1"], 2 * KD)
            hiddens(1, N_GU1, ACC_GU1)
            post_norm(N_DOWN1, ACC_DOWN1, 3)
            for t in range(3):
                rows = P if t < 2 else NS
                copy_transposed(TR_Y + 2 * t, YT[0:rows, t, 0:4 * P], trb[0][0:rows, :])

        @block.vector
        def _(dve):
            n_acc, chain, n_r = [0], [0], [0]

            def take():
                n = n_acc[0]
                n_acc[0] += 1
                dve.wait_ge(acc_full, n + 1)
                return acc[n % 4]

            def free(ins):
                ins.then_inc(acc_free, 1)

            def mark(ins):
                chain[0] += 1
                ins.then_inc(vch, 1)
                return chain[0]

            def link(ins):
                dve.wait_ge(vch, mark(ins))

            def copy_transposed(n, dst, src):
                dve.wait_ge(tr_full, n + 1)
                dve.tensor_copy(dst, src).then_inc(tr_dve, 1)

            def reciprocal_root():
                n_r[0] += 1
                dve.wait_ge(rt_made, n_r[0])
                dve.reciprocal(RR[:, :], RT[:, :]).then_inc(r_made, 1)
                dve.wait_ge(r_made, n_r[0])

            n_hx = [0]

            def rest(hx, k, col, src=None):
                n_hx[0] += 1
                dve.wait_ge(hx_hi, n_hx[0])
                if col is None:
                    ins = dve.tensor_tensor(hx[:, k, 1, :], src, hx[:, k, 0, :], ALU.subtract)
                else:
                    ins = dve.scalar_tensor_tensor(hx[:, k, 1, :], X[:, k, :], par[:, 0, col:col + 1], hx[:, k, 0, :],
                                                   ALU.mult, ALU.subtract)
                ins.then_inc(hx_made, 1)

            def split(i):
                for j, half in enumerate(halves(i)):
                    if j == 1 and i in pool_units:
                        continue
                    dve.wait_ge(w_hi, 2 * i + j + 1)
                    w = WHL[part_of[i]]
                    dve.tensor_tensor(w[:, i % 2, 1, half], ring[:, unit_of[i] % R, half], w[:, i % 2, 0, half],
                                      ALU.subtract).then_inc(w_lo, 1)

            def next_split(i):
                if i + 2 < N_PROJ and part_of[i + 2] == part_of[i]:
                    split(i + 2)

            dve.sem_inc(s_free, 2)
            for k in range(1, KD, 2):
                copy_transposed(TR_X + k, X[:, k, :], trb[1][:, 0:NT])
            copy_transposed(TR_PAR + 1, par[:, 1, 0:4 * CC], trb[1][:, 0:4 * CC])
            split(0)
            for k in range(KD):
                rest(HX0, k, PN["mix_pre0"] + k)
            split(1)
            reciprocal_root()
            for i, m in enumerate(list(range(MQ, M_IN0)) + list(range(MQ))):
                bank = take()
                free(dve.tensor_tensor(BIG[:, m, :], bank[:, 0:NT], RR[:, :], ALU.mult))
                if i % 2 == 1:
                    next_split(i // 2)
                if i == 3:
                    third = CC // 3
                    for i, n in ((0, TR_HIST + 1), (2, TR_HIST + 3)):
                        copy_transposed(n, hists[:, i * third:(i + 1) * third, :],
                                        trb[1][:, 0:third * 3 * NB].rearrange("p (c j) -> p c j", j=3 * NB))

            dve.wait_ge(consts, marks["own"])
            dve.tensor_reduce(own_bias[:, :], own_all[:, :, :], AX.X, ALU.max)
            dve.wait_ge(zeroed, 1)
            dve.wait_ge(acc_free, M_IN0)
            for r in range(2):
                rows = slice(r * DH, (r + 1) * DH)
                last = dve.tensor_copy(KNZ[rows, :, :].rearrange("p (c r) n -> p c r n", r=2)[:, :, r, :],
                                       BIG[rows, MK:MK + H // 2, NP:NT])
            link(last)
            for i, (dst, t) in enumerate(((KOUT, 0), (KOUT, 1), (KOUT, 2), (VTOK, 0), (VTOK, 1), (VTOK, 2))):
                if i % 2 == 1:
                    rows = P if t < 2 else NS
                    copy_transposed(TR_KV + i, dst[0:rows, t, :], trb[1][0:rows, :])

            def k_copies():
                def move_scores(i, e):
                    dve.wait_ge(kt_used, i * KVS + (4 * e + 6))
                    dve.tensor_tensor(SM[0:2 * QT, 7, ds(i * 2 * T + e * T, T)], acc[e][0:2 * QT, 0:T], own_bias[:, :], ALU.add)
                    dve.tensor_copy(S[:, ds(i * 2 + e, 1), :, :].rearrange("p o m c -> p (o m c)"), scb[e][:, :]).then_inc(s_free, 1)
                    dve.wait_ge(s_free, i * 2 + (e + 3))
                    of_b = S[:, ds(i * 2 + e, 1), :, :].rearrange("p o m c -> p (o m) c")
                    dve.tensor_reduce(SM[:, 0, ds(i * NBLK + e * (NBLK // 2), NBLK // 2)], of_b, AX.X, ALU.add)
                    dve.tensor_reduce(SM[:, 1, ds(i * NBLK + e * (NBLK // 2), NBLK // 2)], of_b, AX.X, ALU.max)

                def queries(i, b):
                    e = b % 2
                    dve.tensor_copy(KNE[:, e, :, :], KNZ[:, :, ds(i * 2 * T + b * T, T)])
                    cells = QZ[:, e, :, :].rearrange("p q c -> p (q c)").rearrange("p (c r n) -> p c r n", r=2, n=QT + 2 * T)
                    for j in range(2):
                        for r in range(2):
                            last = dve.tensor_copy(cells[j * DH:(j + 1) * DH, :, r, j * T:(j + 1) * T],
                                                   BIG[r * DH:(r + 1) * DH, MQ:MQ + H // 2, ds(i * 2 * T + (NP + b * T), T)])
                    last.then_inc(qz_made, 1)

                def k_step(i, p, last=False):
                    for s in (2 * p, 2 * p + 1):
                        dve.wait_ge(kt_used, i * KVS + (p + 1))
                        dve.wait_ge(tr_full, i * 4 * KVS + (TR_K + 2 * s + 2))
                        dve.tensor_copy(KTB[p % 2][:, s % 2, 1, :], trb[1][:, :]).then_inc(tr_dve, 1)
                    if p % 4 == 0 and p > 0:
                        move_scores(i, p // 4 - 1)
                    if p % 4 == 2 and not (last and p == 6):
                        queries(i, p // 4 + 1)

                queries(0, 0)
                k_step(0, 0)
                with dve.Fori(0, NB // 2 - 1) as i:
                    for p in range(1, KVS + 1):
                        k_step(i, p)
                for p in range(1, KVS):
                    k_step(NB // 2 - 1, p, last=True)
                move_scores(NB // 2 - 1, 1)

            n = NBLK // 2
            SUMS, MAXS, BIAS, RMAX, EXPB, DENS, DEN, OWN_S, OWN_E, OWN_P = (SM[:, i, :] for i in range(10))
            OWN_S, OWN_E, OWN_P = (v[0:2 * QT, :].rearrange("p (b k) -> p b k", k=T) for v in (OWN_S, OWN_E, OWN_P))
            gates = small[:, 100:100 + NB * NBLK]
            rank = small[:, 164:164 + NB * NBLK]
            beats, ties = (BEATS[:, i, :].rearrange("p (b j i) -> p b j i", j=NBLK, i=NBLK) for i in range(2))
            own_max = small[0:2 * QT, 228:228 + NB]
            own_sum = small[0:2 * QT, 236:236 + NB]
            rden = small[:, 244:244 + NB]

            def choose():
                bank = take()
                by_b = gates.rearrange("p (b m f) -> p b m f", m=n, f=2)
                for first in range(2):
                    last = dve.tensor_copy(by_b[:, :, :, first],
                                           bank[:, first * NB * n:(first + 1) * NB * n].rearrange("p (b m) -> p b m", m=n))
                free(last)
                dve.wait_ge(acc_free, n_acc[0])
                g = gates.rearrange("p (b k) -> p b k", k=NBLK)
                of_i = g.unsqueeze(2).to_broadcast([P, NB, NBLK, NBLK])
                of_j = g.unsqueeze(3).to_broadcast([P, NB, NBLK, NBLK])
                dve.tensor_tensor(beats, of_i, of_j, ALU.is_gt)
                link(dve.tensor_tensor(ties, of_i, of_j, ALU.is_equal))
                link(dve.tensor_tensor(ties, ties, tie[:, :, :].unsqueeze(1).to_broadcast([P, NB, NBLK, NBLK]), ALU.mult))
                link(dve.tensor_tensor(BEATS[:, 0, :], BEATS[:, 0, :], BEATS[:, 1, :], ALU.add))
                link(dve.tensor_reduce(rank, BEATS[:, 0, :].rearrange("p (k i) -> p k i", i=NBLK), AX.X, ALU.add))
                for first in range(2):
                    rows = slice(first * 2 * QT, (first + 1) * 2 * QT)
                    last = dve.tensor_scalar(BIAS[rows, :].rearrange("p (b m) -> p b m", m=n),
                                             rank[rows, :].rearrange("p (b m f) -> p b m f", m=n, f=2)[:, :, :, first],
                                             TOPK - 0.5, NEG, ALU.is_gt, ALU.mult)
                link(last)

            def row_max():
                link(dve.tensor_tensor(MAXS, MAXS, BIAS, ALU.add))
                dve.tensor_reduce(own_max, OWN_S, AX.X, ALU.max)
                link(dve.tensor_reduce(RMAX[:, 0:NB], MAXS.rearrange("p (b m) -> p b m", m=n), AX.X, ALU.max))
                dve.tensor_tensor(RMAX[0:2 * QT, 0:NB], RMAX[0:2 * QT, 0:NB], own_max, ALU.max).then_inc(d_step, 1)

            def query_max():
                ins = dve.tensor_copy(RMT[:, 0, :], take()[0:NB, 0:P])
                free(ins)
                dve.wait_ge(acc_free, n_acc[0])
                half = RMT[:, 1, 0:2 * QT]
                link(dve.tensor_tensor(half, RMT[:, 0, 0:2 * QT], RMT[:, 0, 2 * QT:4 * QT], ALU.max))
                hjt = half.rearrange("p (h j t) -> p h j t", j=2, t=T)
                best = RMT[:, 1, 2 * QT:3 * QT].rearrange("p (h t) -> p h t", t=T)
                link(dve.tensor_tensor(best, hjt[:, :, 0, :], hjt[:, :, 1, :], ALU.max))
                for first in range(2):
                    last = dve.tensor_copy(RMT[:, 2, first * 2 * QT:(first + 1) * 2 * QT].rearrange("p (h j t) -> p h j t", j=2, t=T),
                                           best.unsqueeze(2).to_broadcast([NB, H, 2, T]))
                last.then_inc(d_step, 1)

            def exp_bias():
                bank = take()
                dve.tensor_tensor(OWN_E, OWN_S, bank[0:2 * QT, 0:NB].unsqueeze(2).to_broadcast([2 * QT, NB, T]), ALU.subtract)
                ins = dve.tensor_scalar(RMAX[:, NB:2 * NB], bank[:, 0:NB], -SCALE, None, ALU.mult)
                free(ins)
                dve.wait_ge(acc_free, n_acc[0])
                dve.tensor_tensor(EXPB.rearrange("p (b m) -> p b m", m=n), BIAS.rearrange("p (b m) -> p b m", m=n),
                                  RMAX[:, NB:2 * NB].unsqueeze(2).to_broadcast([P, NB, n]), ALU.add).then_inc(d_step, 1)

            def sum_exponentials(part):
                cols = PARTS[part]
                dve.wait_ge(p_made, 1 + cols.stop)
                if part == 0:
                    dve.tensor_reduce(own_sum, OWN_E, AX.X, ALU.add)
                link(dve.tensor_reduce(DEN[:, cols], DENS.rearrange("p (b m) -> p b m", m=n)[:, cols, :], AX.X, ALU.add))
                dve.tensor_tensor(DEN[0:2 * QT, cols], DEN[0:2 * QT, cols], own_sum[:, cols], ALU.add).then_inc(d_step, 1)
                ins = dve.reciprocal(rden[:, cols], take()[:, cols])
                free(ins)
                dve.wait_ge(acc_free, n_acc[0])

            def weigh_own():
                dve.tensor_tensor(OWN_P, OWN_E, rden[0:2 * QT, :].unsqueeze(2).to_broadcast([2 * QT, NB, T]),
                                  ALU.mult).then_inc(d_step, 1)

            def diagonal(b):
                if b >= 2:
                    dve.wait_ge(tr_full, TR_P["sample", b - 2] + 1)
                dve.tensor_scalar(DG[:, b % 2, :], ident[:, :], rden[:, b:b + 1], None, ALU.mult).then_inc(dg_made, 1)

            def own_probabilities():
                bank = take()
                by_j = bank[0:NS, 0:2 * QT].rearrange("p (h j t) -> p h j t", j=2, t=T)
                own = small[0:NS, 256:256 + QT]
                link(dve.tensor_copy(own.rearrange("p (h t) -> p h t", t=T), by_j[:, :, 0, :]))
                free(dve.tensor_tensor(own.rearrange("p (h t) -> p h t", t=T), by_j[:, :, 1, :],
                                       own.rearrange("p (h t) -> p h t", t=T), ALU.add))
                dve.wait_ge(acc_free, n_acc[0])
                dve.tensor_tensor(POWN[0:NS, :].rearrange("p (b q) -> p b q", q=QT), own.unsqueeze(1).to_broadcast([NS, NB, QT]),
                                  bmask01[:, :].unsqueeze(2).to_broadcast([NS, NB, QT]), ALU.mult).then_inc(d_step, 1)

            def copy_sample(b):
                k = TR_P["sample", b]
                if k % 2 == 1:
                    dve.wait_ge(tr_full, k + 1)
                    for j in range(2):
                        last = dve.tensor_copy(by_token(b, j), from_rows(trb[1], j))
                    last.then_inc(tr_dve, 1)

            def prompt_scores(h):
                col = h * 12
                bank = take()
                if h >= 2:
                    dve.wait_ge(tr_full, TR_P["prompt", h - 2] + 1)
                sp = SP[:, h % 2, :]
                free(dve.tensor_tensor(sp, bank[:, 0:3 * P], tri3[:, :, :].rearrange("p a b -> p (a b)"), ALU.add))
                dve.wait_ge(acc_free, n_acc[0])
                link(dve.tensor_reduce(small[:, col:col + 3], sp.rearrange("p (a b) -> p a b", a=3), AX.X, ALU.max))
                link(dve.tensor_tensor(small[:, col + 1:col + 2], small[:, col + 1:col + 2], small[:, col + 2:col + 3], ALU.max))
                dve.tensor_scalar(small[:, col + 4:col + 6], small[:, col:col + 2], -SCALE, None, ALU.mult).then_inc(pp_ready, 1)

            def prompt_normalise(h):
                col = h * 12
                dve.wait_ge(pp_exp, h + 1)
                link(dve.reciprocal(small[:, col + 8:col + 10], small[:, col + 6:col + 8]))
                sp = SP[:, h % 2, :]
                dve.tensor_scalar(sp[:, 0:P], sp[:, 0:P], small[:, col + 8:col + 9], None, ALU.mult)
                dve.tensor_scalar(sp[:, P:3 * P], sp[:, P:3 * P], small[:, col + 9:col + 10], None, ALU.mult).then_inc(pp_made, 1)

            def prompt_step(i):
                if i < H:
                    prompt_scores(i)
                    prompt_normalise(i)
                if 1 <= i <= H and TR_P["prompt", i - 1] % 2 == 1:
                    copy_transposed(TR_P["prompt", i - 1], PT[:, (i - 1) % 2, :], trb[1][:, 0:3 * P])
                if i >= 2:
                    h = i - 2
                    bank = take()
                    rows = slice((h % 2) * DH, (h % 2 + 1) * DH)
                    free(dve.tensor_copy(MIX[rows, CA + h // 2, 0:NP], bank[rows, 0:NP]))

            k_copies()
            link(dve.tensor_copy(SM[:, 2, 0:1], SM[:, 1, 0:1]))
            dve.sem_inc(d_step, 1)
            def conv_a_product():
                dve.wait_ge(tr_act, TR_HIST // 2 + 1)
                dve.tensor_tensor(CUP[:, :, 2:], BIG[:, CA:2 * CA, 0:NP], BIG[:, 2 * CA:3 * CA, 0:NP], ALU.mult)
                dve.tensor_copy(CUS[:, :, :, 0:2], hista[:, :, :, :])
                link(dve.tensor_tensor(CUS[:, :, :, 2:], BIG[:, CA:2 * CA, NP:NT].rearrange("p c (b t) -> p c b t", t=T),
                                       BIG[:, 2 * CA:3 * CA, NP:NT].rearrange("p c (b t) -> p c b t", t=T), ALU.mult))

            def conv_a_tap(j):
                for c in range(CA):
                    w = par[:, 0, PCA + j * CA + c:PCA + j * CA + c + 1]
                    for dst, src in ((MIX[:, c, 0:NP], CUP[:, c, j:j + NP]),
                                     (MIX[:, c, NP:NT].rearrange("p (b t) -> p b t", t=T), CUS[:, c, :, j:j + T])):
                        if j == 0:
                            last = dve.tensor_scalar(dst, src, w, None, ALU.mult)
                        else:
                            last = dve.scalar_tensor_tensor(dst, src, w, dst, ALU.mult, ALU.add)
                link(last)

            def conv_a_gate():
                dve.tensor_tensor(MIX[:, 0:CA, :], MIX[:, 0:CA, :], BIG[:, 0:CA, :], ALU.mult)
                dve.tensor_copy(co_a[:, :, 0:2], CUP[:, :, NP:NP + 2])
                dve.tensor_copy(co_a[:, :, 2:].rearrange("p c (b j) -> p c b j", j=2), CUS[:, :, :, T:T + 2]).then_inc(mix_made, 1)

            def sample_output(b):
                bank = take()
                free(dve.tensor_copy(MIX[:, CA:, NP + b * T:NP + (b + 1) * T],
                                     bank[:, 0:H // 2 * T].rearrange("p (h t) -> p h t", t=T)))

            choose()
            row_max()
            query_max()
            exp_bias()
            sum_exponentials(0)
            diagonal(0)
            diagonal(1)
            copy_sample(1)
            sum_exponentials(1)
            weigh_own()
            own_probabilities()
            prompt_step(0)
            for b in range(NB):
                if 1 <= b < NB - 1:
                    diagonal(b + 1)
                    copy_sample(b + 1)
                if b:
                    prompt_step(b)
                    sample_output(b - 1)
                if b == 1:
                    conv_a_product()
                if 2 <= b <= 4:
                    conv_a_tap(b - 2)
                if b == 5:
                    conv_a_gate()
            prompt_step(NB)
            sample_output(NB - 1)
            prompt_step(NB + 1)
            dve.wait_ge(acc_free, n_acc[0])
            dve.sem_inc(mix_made, 1)
            dve.wait_ge(mix_made, 2)
            for k in range(KD):
                rest(HX1, k, None, MIX[:, k, :])
            split(N_OUT0)
            split(N_OUT0 + 1)
            copy_transposed(TR_COA + 1, coT_a[0:2 + 2 * NB, 2 * P:4 * P], trb[1][0:2 + 2 * NB, 0:2 * P])

            def post_norm(i, kparts, col, hx, pre_col, input_norm=False):
                for k in range(KD):
                    if k % 2 == 0:
                        for _ in range(kparts - 1):
                            next_split(i)
                            i += 1
                    if input_norm:
                        free(dve.tensor_tensor(Y[:, k, :], take()[:, 0:NT], RR[:, :], ALU.mult))
                    else:
                        free(dve.tensor_copy(Y[:, k, :], take()[:, 0:NT]))
                    if k % 2 == 1 and k < KD - 1:
                        next_split(i)
                        i += 1
                reciprocal_root()
                dve.wait_ge(acc_free, n_acc[0])
                marked = []
                for k in range(KD + 3):
                    if k < KD:
                        marked.append(mark(dve.scalar_tensor_tensor(Y[:, k, :], Y[:, k, :], par[:, 0, col + k:col + k + 1],
                                                                    RR[:, :], ALU.mult, ALU.mult)))
                    if 1 <= k <= KD:
                        dve.wait_ge(vch, marked[k - 1])
                        dve.tensor_tensor(X[:, k - 1, :], X[:, k - 1, :], Y[:, k - 1, :], ALU.add).then_inc(x_made, 1)
                    if k >= 3 and hx is not None:
                        rest(hx, k - 3, pre_col + k - 3)
                    if k == 3:
                        next_split(i)

            def ffn(layer, i):
                reciprocal_root()
                gs, us, ht, hid = GS[layer], US[layer], HT[layer], HID[layer]
                base = layer * FM
                for pair in range(FM // 2):
                    if pair:
                        dve.wait_ge(hid_made, base + 2 * pair)
                    for r in range(2):
                        free(dve.tensor_tensor(gs[:, r, :], take()[:, 0:NT], RR[:, :], ALU.mult))
                    next_split(i + 2 * pair)
                    for r in range(2):
                        free(dve.tensor_tensor(us[:, r, :], take()[:, 0:NT], RR[:, :], ALU.mult))
                    for r in range(2):
                        dve.wait_ge(acc_free, n_acc[0] - 1 + r)
                        dve.wait_ge(hid_silu, base + 2 * pair + r + 1)
                        dve.tensor_tensor(ht[:, r, :], gs[:, r, :], us[:, r, :], ALU.mult).then_inc(ht_made, 1)
                    next_split(i + 2 * pair + 1)
                    for r in range(2):
                        m = 2 * pair + r
                        dve.wait_ge(hid_hi, base + m + 1)
                        dve.tensor_tensor(hid[:, m, 1, :], ht[:, r, :], hid[:, m, 0, :], ALU.subtract).then_inc(hid_made, 1)

            post_norm(N_OUT0, 1, PN["mix_post0"], HX1, PN["ffn_pre0"])
            ffn(0, N_GU0)
            post_norm(N_DOWN0, 3, PN["ffn_post0"], HX1, PN["mix_pre1"])

            reciprocal_root()
            dve.tensor_copy(exts[:, :, :, 0:3], hists[:, :, :].rearrange("p c (b j) -> p c b j", j=3))
            for c in range(CC):
                e = c % 2
                bank = take()
                new = exts[:, c, :, 3:]
                dve.tensor_tensor(ext[:, e, 3:], bank[:, 0:NP], RR[:, 0:NP], ALU.mult)
                free(dve.tensor_tensor(new, bank[:, NP:NT].rearrange("p (b t) -> p b t", t=T),
                                       RR[:, NP:NT].rearrange("p (b t) -> p b t", t=T), ALU.mult))
                dve.wait_ge(acc_free, n_acc[0])
                dve.tensor_copy(co_s[:, c, 0:3], ext[:, e, NP:NP + 3])
                dst = XBC[:, c, 0:NP]
                for j in range(4):
                    w = par[:, 1, j * CC + c:j * CC + c + 1]
                    if j == 0:
                        last = dve.tensor_scalar(dst, ext[:, e, j:j + NP], w, None, ALU.mult)
                    else:
                        last = dve.scalar_tensor_tensor(dst, ext[:, e, j:j + NP], w, dst, ALU.mult, ALU.add)
                    if j < 3:
                        link(last)
                    else:
                        last.then_inc(cv_made, 1)
                if c % 2 == 1:
                    next_split(N_IN1 + c // 2)
            bank = take()
            w = [hw[:, i, :] for i in range(6)]
            ins = dve.tensor_tensor(w[3], bank[0:SH, 0:NT], RR[0:SH, :], ALU.mult)
            free(ins)
            dve.wait_ge(acc_free, n_acc[0])

            def conv_samples():
                new = XBC[:, :, NP:NT].rearrange("p c (b t) -> p c b t", t=T)

                def of_chunk(table, first):
                    return table[:, first:first + CC].unsqueeze(2).unsqueeze(3).to_broadcast([P, CC, NB, T])

                dve.tensor_copy(co_s[:, :, 3:].rearrange("p c (b j) -> p c b j", j=3), exts[:, :, :, T:T + 3]).then_inc(co_made, 1)
                link(dve.tensor_tensor(new, exts[:, :, :, 0:T], of_chunk(par[:, 1, :], 0), ALU.mult))
                for j in range(1, 4):
                    link(dve.tensor_tensor(EXTMP, exts[:, :, :, j:j + T], of_chunk(par[:, 1, :], j * CC), ALU.mult))
                    link(dve.tensor_tensor(new, new, EXTMP, ALU.add))
                dve.tensor_tensor(new, new, of_chunk(par[:, 0, :], PCB), ALU.add).then_inc(cv_made, 1)

            def dt_exponent():
                dve.wait_ge(ld_head, 64)
                link(dve.tensor_scalar(w[3], w[3], hp3[:, 0:1], None, ALU.add))
                link(dve.tensor_scalar(w[4], w[3], -1.0, None, ALU.mult))
                dve.tensor_tensor(w[4], w[4], w[3], ALU.max).then_inc(dt_step, 1)

            def dt_argument():
                dve.wait_ge(dt_act, 2)
                dve.tensor_scalar(w[4], w[5], 1.0, None, ALU.add).then_inc(dt_step, 1)
                dve.wait_ge(dt_step, 2)
                link(dve.tensor_scalar(w[1], w[4], -1.0, None, ALU.add))
                link(dve.tensor_scalar(w[2], w[1], 0.0, None, ALU.is_equal))
                link(dve.tensor_tensor(w[1], w[1], w[2], ALU.add))

            def dt_sums():
                dve.wait_ge(dt_act, 3)
                dve.tensor_tensor(w[0], w[0], w[2], ALU.add)
                link(dve.reciprocal(w[1], w[1]))
                link(dve.tensor_tensor(w[0], w[0], w[5], ALU.mult))
                link(dve.tensor_tensor(w[0], w[0], w[1], ALU.mult))
                link(dve.scalar_tensor_tensor(w[2], w[3], 0.0, w[0], ALU.max, ALU.add))
                link(dve.tensor_scalar(w[3], w[2], hp3[:, 1:2], -1.0, ALU.mult, ALU.mult))
                for t in range(2):
                    cols = slice(t * P, (t + 1) * P)
                    dve.tensor_tensor_scan(w[0][:, cols], ones[0:SH, :], w[3][:, cols], 0.0, ALU.mult, ALU.add)
                link(dve.tensor_copy(w[0][:, NP:NT], w[3][:, NP:NT]))
                seq = w[0][:, NP:NT].rearrange("p (b t) -> p b t", t=T)
                for t in range(1, T):
                    link(dve.tensor_tensor(seq[:, :, t], seq[:, :, t], seq[:, :, t - 1], ALU.add))
                for t in range(2):
                    cols = slice(t * P, (t + 1) * P)
                    dve.tensor_scalar(w[4][:, cols], w[0][:, cols], -1.0, w[0][:, (t + 1) * P - 1:(t + 1) * P], ALU.mult, ALU.add)
                dve.tensor_tensor(w[4][:, NP:NT].rearrange("p (b t) -> p b t", t=T), seq[:, :, T - 1:T].to_broadcast([SH, NB, T]),
                                  seq, ALU.subtract).then_inc(dt_step, 1)
                dve.tensor_copy(hs[0:SH, :], w[2])
                dve.tensor_copy(hs[2 * SH:3 * SH, :], w[0])
                dve.memset(hs[3 * SH:4 * SH, P:NT], 0.0)
                dve.tensor_copy(decin[:, NB:NB + 1], hp3[:, 2:3])

            def dt_weights():
                dve.wait_ge(dt_act, 5)
                link(dve.tensor_tensor(w[5], w[5], w[2], ALU.mult))
                dve.tensor_copy(decin[:, 0:NB], w[1][:, NP:NT].rearrange("p (b t) -> p b t", t=T)[:, :, T - 1])
                dve.tensor_copy(hs[SH:2 * SH, :], w[5])
                dve.tensor_scalar(hs[3 * SH:4 * SH, 0:P], w[5][:, 0:P], w[1][:, NP - 1:NP], None, ALU.mult).then_inc(hs_made, 1)

            for m in range(CX):
                bank = take()
                free(dve.tensor_tensor(ZS[:, m, :], bank[:, 0:NT], RR[:, :], ALU.mult))
                if m % 2 == 1:
                    next_split(N_IN1 + (CC + m) // 2)
                if m == 1:
                    dt_exponent()
                if m == 3:
                    dt_argument()
                if m == 5:
                    dt_sums()
                if m == 7:
                    dt_weights()
                if m == 9:
                    conv_samples()

            DT, W1, AC, W0 = (i * SH for i in range(4))
            bank = take()
            dve.tensor_copy(tc[:, 0:2, :], bank[:, 0:2 * P].rearrange("p (t c) -> p t c", c=P))
            free(dve.tensor_copy(tc[0:NS, 2, :], bank[0:NS, 2 * P:3 * P]))
            for t in range(3):
                rows = P if t < 2 else NS
                free(dve.tensor_copy(BT[0:rows, t, :], take()[0:rows, :]))
            dve.wait_ge(acc_free, n_acc[0])
            dve.sem_inc(bt_made, 1)
            dve.wait_ge(consts, marks["seg"])
            for g in range(G):
                bank = take()
                dve.tensor_tensor(CBM[:, g, 0:NP].rearrange("p (t c) -> p t c", c=P), bank[:, 0:NP].rearrange("p (t c) -> p t c", c=P),
                                  trilT[:, :].unsqueeze(1).to_broadcast([P, 2, P]), ALU.mult)
                free(dve.tensor_tensor(CBM[0:NS, g, NP:NT], bank[0:NS, NP:NT], bd01[:, :], ALU.mult))
            free(dve.tensor_copy(dec[:, :, :], take()[:, 0:CX * (NB + 1)].rearrange("p (k c) -> p k c", c=NB + 1)))

            def by_head(rows, t, first, g):
                return tc[0:rows, t, first + g * HG:first + (g + 1) * HG].unsqueeze(2).to_broadcast([rows, HG, DH])

            def heads(ap):
                return ap.rearrange("p (h d) -> p h d", d=DH)

            for g in range(G):
                bank = take()
                cols = slice(g * HG * DH, (g + 1) * HG * DH)
                dve.tensor_tensor(heads(XDS[0:NS, cols]), heads(bank[0:NS, :]), by_head(NS, 2, DT, g), ALU.mult)
                free(dve.tensor_tensor(heads(XWS[Q1, cols]), heads(bank[0:NS, :]), by_head(NS, 2, W1, g), ALU.mult))
            dve.wait_ge(acc_free, n_acc[0])
            dve.sem_inc(bt_made, 1)

            def copy_state(b, q):
                if b >= 2:
                    dve.wait_ge(o_full, NB + b - 1)
                copy_transposed(TR_ST + b * G + q, S0T[b % 2][:, q, :], trb[1][:, :])

            copy_state(0, 1)
            copy_state(0, 3)
            for b in range(NB):
                st = ring[:, (FIRST_STATE + b) % R, :].rearrange("p (k n) -> p k n", n=NST)
                for q in range(G):
                    if q == 3:
                        free(dve.tensor_copy(YOS[:, :, b, :].rearrange("p (g c) t -> p c g t", c=PG),
                                             take()[:, 0:CX * T].rearrange("p (c g t) -> p c g t", g=G, t=T)))
                    bank = take()
                    for hh in range(PG):
                        k = q * PG + hh
                        last = dve.scalar_tensor_tensor(st[:, k, :], st[:, k, :], dec[:, k, b:b + 1],
                                                        bank[:, hh * NST:(hh + 1) * NST], ALU.mult, ALU.add)
                    free(last)
                    if b + 1 < NB and q % 2 == 1:
                        copy_state(b + 1, q)
                dve.wait_ge(acc_free, n_acc[0])
                dve.sem_inc(st_made, 1)
            for i in range(1, CC // 4, 2):
                copy_transposed(TR_CO + i, CO1T[CQ:CQ + 3 + 3 * NB, i * 4 * P:(i + 1) * 4 * P], trb[1][0:3 + 3 * NB, :])

            def weigh_x(g):
                gp = g % 2
                for t in range(2):
                    bank = take()
                    dve.tensor_tensor(heads(XDT[:, gp, t, :]), heads(bank[:, :]), by_head(P, t, DT, g), ALU.mult)
                    if t == 0:
                        dve.tensor_tensor(heads(XW0), heads(bank[:, :]), by_head(P, t, W0, g), ALU.mult)
                    free(dve.tensor_tensor(heads(XW1[:, gp, t, :]), heads(bank[:, :]), by_head(P, t, W1, g), ALU.mult))
                dve.wait_ge(acc_free, n_acc[0])
                dve.sem_inc(g_made, 1)

            def copy_states(g):
                free(dve.tensor_copy(SENT[g % 2], take()[:, :]))
                dve.wait_ge(acc_free, n_acc[0])
                dve.sem_inc(sent_made, 1)
                if g >= 1:
                    dve.wait_ge(stp_out, 16 * g)
                free(dve.tensor_copy(STP[:, :, :], take()[:, :].rearrange("p (k n) -> p k n", n=NST)))
                dve.wait_ge(acc_free, n_acc[0])
                dve.sem_inc(stp_made, 1)

            weigh_x(0)
            copy_states(0)
            for g in range(G):
                for hh in range(HG):
                    h = g * HG + hh
                    bank = take()
                    for t in range(3):
                        rows = P if t < 2 else NS
                        cols = slice(t * P, t * P + rows)
                        last = dve.tensor_scalar(SEG[0:rows, hh, cols], bank[0:rows, cols], tc[0:rows, t, AC + h:AC + h + 1],
                                                 0.0, ALU.subtract, ALU.min)
                    free(last)
                dve.wait_ge(acc_free, n_acc[0])
                dve.sem_inc(seg_in, 1)
                if g + 1 < G:
                    weigh_x(g + 1)
                dve.wait_ge(seg_exp, g + 1)
                dve.tensor_tensor(SEG[:, :, :], SEG[:, :, :], CBM[:, g, :].unsqueeze(1).to_broadcast([P, HG, NT]),
                                  ALU.mult).then_inc(seg_made, 1)
                if g + 1 < G:
                    copy_states(g + 1)
                for c in range(PG):
                    k = g * PG + c
                    e = c % 2
                    within, entering, grown = take(), take(), take()
                    y, late = YTMP[:, e, :], XCH[:, e, :]
                    dve.scalar_tensor_tensor(y, XBC[:, k, :], dec[:, k, NB:NB + 1], within[:, 0:NT], ALU.mult, ALU.add).then_inc(acc_free, 1)
                    link(dve.tensor_copy(EBT[:, e, :], grown[:, 0:NT - P]))
                    dve.tensor_tensor(late[:, P:], YOS[:, k, :, :].rearrange("p b t -> p (b t)"), EBT[:, e, P:], ALU.mult)
                    dve.tensor_tensor(late[:, 0:P], entering[:, 0:P], EBT[:, e, 0:P], ALU.mult).then_inc(acc_free, 1)
                    dve.wait_ge(acc_free, n_acc[0] - 1)
                    free(dve.tensor_tensor(y[:, P:], y[:, P:], late, ALU.add))
                    dve.wait_ge(acc_free, n_acc[0])
                    dve.wait_ge(zs_made, k // 4 + 1)
                    dve.tensor_tensor(XBC[:, k, :], y, ZS[:, k, :], ALU.mult).then_inc(gy_made, 1)

            for k in range(CX):
                rest(G1, k, None, XBC[:, k, :])
                if k == 0:
                    split(N_OUT1)
                    split(N_OUT1 + 1)
            reciprocal_root()
            post_norm(N_OUT1, CX // KD, PN["mix_post1"], G1, PN["ffn_pre1"], input_norm=True)
            ffn(1, N_GU1)
            post_norm(N_DOWN1, 3, PN["ffn_post1"], None, None)
            for t in range(3):
                rows = P if t < 2 else NS
                copy_transposed(TR_Y + 2 * t + 1, YT[0:rows, t, 4 * P:8 * P], trb[1][0:rows, :])


_INS = ['x_prompt', 'x_sample', 'cache_k', 'cache_v', 'page_table', 'state_conv_a', 'state_conv_ssm', 'state_ssm',
        'l0_norm_mix_pre', 'l0_w_in', 'l0_conv_w', 'l0_w_out', 'l0_norm_mix_post',
        'l0_norm_ffn_pre', 'l0_ffn_gate', 'l0_ffn_up', 'l0_ffn_down', 'l0_norm_ffn_post',
        'l1_norm_mix_pre', 'l1_w_in', 'l1_conv_w', 'l1_conv_b', 'l1_dt_bias', 'l1_a_log', 'l1_d_skip',
        'l1_norm_gate', 'l1_w_out', 'l1_norm_mix_post',
        'l1_norm_ffn_pre', 'l1_ffn_gate', 'l1_ffn_up', 'l1_ffn_down', 'l1_norm_ffn_post']
_OUTS = [(1, 256, 1024), (8, 4, 1024), (1, 2, 8, 128, 64), (1, 2, 8, 128, 64), (8, 8, 4, 64), (8, 8, 4, 64),
         (1, 2, 512), (8, 2, 512), (1, 3, 3072), (8, 3, 3072), (1, 32, 64, 128), (8, 32, 64, 128)]


def kernel(**inputs):
    import numpy as _np
    import concourse.bacc as _bacc
    from concourse import mybir as _mybir
    from concourse.bass_utils import run_bass_kernel_spmd as _run

    nc = _bacc.Bacc("TRN2", target_bir_lowering=False, num_devices=1)
    arrays, args = {}, []
    for name in _INS:
        a = _np.ascontiguousarray(inputs[name])
        arrays[f"in_{name}_dram"] = a
        args.append(nc.dram_tensor(f"in_{name}_dram", a.shape, _mybir.dt.from_np(a.dtype), kind="ExternalInput").ap())
    for i, shape in enumerate(_OUTS):
        args.append(nc.dram_tensor(f"out_{i}_dram", shape, _mybir.dt.float32, kind="ExternalOutput").ap())
    hybrid_decoder_kernel(nc, *args)
    r = _run(nc, [arrays], core_ids=[0])
    return tuple(r.results[0][f"out_{i}_dram"] for i in range(len(_OUTS)))
```
